# Optimizing a Trainium2 kernel written in Bass

```python
import math
import jax, jax.numpy as jnp
from jax import lax
import numpy as np

D_MODEL = 2048
BATCH = 1
SEQ = 256
DEPTH = 2

GRID_W = 64
A_HEAD_DIM = 128
A_WIDTH = D_MODEL // 2
A_HEADS = A_WIDTH // A_HEAD_DIM
HGRN_CHUNK = 64
B_WIDTH = D_MODEL // 2
B_GROUP_DIM = 128
B_GROUPS = B_WIDTH // B_GROUP_DIM
B_CHUNK = 128
IN0_COLS = 5 * A_WIDTH + 2 * B_WIDTH
MIX0_WIDTH = A_WIDTH + B_WIDTH
C_HEAD_DIM = 128
C_Q_HEADS = D_MODEL // C_HEAD_DIM
C_KV_HEADS = C_Q_HEADS // 4
C_GROUP = C_Q_HEADS // C_KV_HEADS
C_Q_BLOCK = 128
ROPE_THETA = 10000.0
IN1_COLS = (C_Q_HEADS + 2 * C_KV_HEADS) * C_HEAD_DIM
MIX1_WIDTH = C_Q_HEADS * C_HEAD_DIM
D_FF = 5632
CONV_W = 3
N_EVEN = (DEPTH + 1) // 2
N_ODD = DEPTH // 2
ALPHA = (2.0 * DEPTH) ** 0.25
BETA = (8.0 * DEPTH) ** -0.25
LN_EPS = 1e-5
RMS_EPS = 1e-6


def layer_norm(x, g, b):
    xf = x.astype(jnp.float32)
    mu = jnp.mean(xf, axis=-1, keepdims=True)
    var = jnp.mean(jnp.square(xf - mu), axis=-1, keepdims=True)
    return ((xf - mu) * lax.rsqrt(var + LN_EPS) * g.astype(jnp.float32) + b.astype(jnp.float32)).astype(x.dtype)

def rms_norm(x, g):
    xf = x.astype(jnp.float32)
    y = xf * lax.rsqrt(jnp.mean(xf * xf, axis=-1, keepdims=True) + RMS_EPS)
    return (y * g.astype(jnp.float32)).astype(x.dtype)

def hgrn2_scan(q, k, v, log_f):
    Bn, H, T, DK = q.shape
    DV = v.shape[-1]
    C = HGRN_CHUNK
    N = T // C
    q, k, log_f = [a.astype(jnp.float32).reshape(Bn, H, N, C, DK) for a in (q, k, log_f)]
    v = v.astype(jnp.float32).reshape(Bn, H, N, C, DV)
    b = jnp.cumsum(log_f, axis=3)
    b_last = b[:, :, :, C - 1:C, :]
    b_mid = b[:, :, :, C // 2 - 1:C // 2, :]
    scores = jnp.einsum('bhntd,bhnsd->bhnts', q * jnp.exp(b - b_mid), k * jnp.exp(b_mid - b))
    mask = jnp.tril(jnp.ones((C, C), dtype=bool))
    scores = jnp.where(mask, scores, 0.0)
    o_intra = jnp.einsum('bhnts,bhnsv->bhntv', scores, v)
    kv = jnp.einsum('bhnsd,bhnsv->bhndv', k * jnp.exp(b_last - b), v)
    decay = jnp.exp(b_last[:, :, :, 0, :])

    def step(S, inp):
        kv_n, dec_n = inp
        return dec_n[..., None] * S + kv_n, S

    S0 = jnp.zeros((Bn, H, DK, DV), jnp.float32)
    _, S_prev = lax.scan(step, S0, (jnp.moveaxis(kv, 2, 0), jnp.moveaxis(decay, 2, 0)))
    S_prev = jnp.moveaxis(S_prev, 0, 2)
    o_inter = jnp.einsum('bhntd,bhndv->bhntv', q * jnp.exp(b), S_prev)
    return (o_intra + o_inter).reshape(Bn, H, T, DV)

def hgrn2_bidirectional(q, i_in, f_fw_pre, f_bw_pre, lb):
    Bn, T, _ = q.shape

    def heads(a):
        return a.reshape(Bn, T, A_HEADS, A_HEAD_DIM).transpose(0, 2, 1, 3)

    def gate(pre):
        return lb + (1.0 - lb) * jax.nn.sigmoid(pre.astype(jnp.float32))

    f_fw = gate(f_fw_pre)
    f_bw = gate(f_bw_pre)
    qh, ih = heads(q), heads(i_in)
    o_fw = hgrn2_scan(qh, heads(1.0 - f_fw), ih, heads(jnp.log(f_fw)))

    def flip(a):
        return jnp.flip(a, axis=2)

    o_bw = flip(hgrn2_scan(flip(qh), flip(heads(1.0 - f_bw)), flip(ih), flip(heads(jnp.log(f_bw)))))
    return (o_fw + o_bw).transpose(0, 2, 1, 3)

def even_mixer(x, w_in, lb, a_norm_g, b_ln_g, b_ln_b, b_ws, b_bias, w_out):
    Bn, T, _ = x.shape
    h = x @ w_in
    cuts = [A_WIDTH, 2 * A_WIDTH, 3 * A_WIDTH, 4 * A_WIDTH, 5 * A_WIDTH, 5 * A_WIDTH + B_WIDTH]
    q, f_fw, f_bw, i_in, g, u, v = jnp.split(h, cuts, axis=-1)
    o = hgrn2_bidirectional(q, i_in, f_fw, f_bw, lb).astype(x.dtype)
    o = rms_norm(o, a_norm_g.reshape(A_HEADS, A_HEAD_DIM)).reshape(Bn, T, A_WIDTH)
    o_a = o * jax.nn.silu(g)
    v = layer_norm(v, b_ln_g, b_ln_b)
    N = T // B_CHUNK
    v = v.reshape(Bn, N, B_CHUNK, B_GROUPS, B_GROUP_DIM)
    s = jnp.einsum('gts,bnsgc->bntgc', b_ws, v) + b_bias.T[None, None, :, :, None]
    o_b = (u.reshape(Bn, N, B_CHUNK, B_GROUPS, B_GROUP_DIM) * s).reshape(Bn, T, B_WIDTH)
    return jnp.concatenate([o_a, o_b], axis=-1) @ w_out

def axial_rope_angles(T):
    rows = T // GRID_W
    r = jnp.repeat(jnp.arange(rows, dtype=jnp.float32), GRID_W)
    c = jnp.tile(jnp.arange(GRID_W, dtype=jnp.float32), rows)
    half = C_HEAD_DIM // 2
    inv_freq = jnp.exp(-math.log(ROPE_THETA) * jnp.arange(0, half, 2, dtype=jnp.float32) / half)
    return r[:, None] * inv_freq, c[:, None] * inv_freq

def rope_rotate(x, ang):
    n2 = x.shape[-1] // 2
    cos = jnp.cos(ang)[:, None, :].astype(x.dtype)
    sin = jnp.sin(ang)[:, None, :].astype(x.dtype)
    x1, x2 = x[..., :n2], x[..., n2:]
    return jnp.concatenate([x1 * cos - x2 * sin, x2 * cos + x1 * sin], axis=-1)

def apply_axial_rope(x, ang_r, ang_c):
    half = C_HEAD_DIM // 2
    return jnp.concatenate([rope_rotate(x[..., :half], ang_r), rope_rotate(x[..., half:], ang_c)], axis=-1)

def odd_mixer(x, w_in, q_g, k_g, w_out):
    Bn, T, _ = x.shape
    h = x @ w_in
    qd, kd = C_Q_HEADS * C_HEAD_DIM, C_KV_HEADS * C_HEAD_DIM
    q, k, v = jnp.split(h, [qd, qd + kd], axis=-1)
    q = q.reshape(Bn, T, C_Q_HEADS, C_HEAD_DIM)
    k = k.reshape(Bn, T, C_KV_HEADS, C_HEAD_DIM)
    v = v.reshape(Bn, T, C_KV_HEADS, C_HEAD_DIM)
    ang_r, ang_c = axial_rope_angles(T)
    q = apply_axial_rope(rms_norm(q, q_g), ang_r, ang_c)
    k = apply_axial_rope(rms_norm(k, k_g), ang_r, ang_c)
    kk = k.transpose(0, 2, 1, 3)
    vv = v.transpose(0, 2, 1, 3)
    NB = T // C_Q_BLOCK
    qb = q.reshape(Bn, T, C_KV_HEADS, C_GROUP, C_HEAD_DIM).transpose(0, 2, 3, 1, 4)
    qb = jnp.moveaxis(qb.reshape(Bn, C_KV_HEADS, C_GROUP, NB, C_Q_BLOCK, C_HEAD_DIM), 3, 0)
    scale = C_HEAD_DIM ** -0.5

    def attend(q_blk):
        s = jnp.einsum('bkgqd,bksd->bkgqs', q_blk, kk).astype(jnp.float32) * scale
        p = jax.nn.softmax(s, axis=-1)
        return jnp.einsum('bkgqs,bksd->bkgqd', p.astype(vv.dtype), vv)

    out = lax.map(attend, qb)
    out = out.transpose(1, 0, 4, 2, 3, 5).reshape(Bn, T, MIX1_WIDTH)
    return out @ w_out

def conv_ffn(x, w_up, conv_w, conv_b, w_down):
    T = x.shape[1]
    h = x @ w_up
    pad = CONV_W // 2
    hp = jnp.pad(h, ((0, 0), (pad, pad), (0, 0)))
    h = sum(hp[:, j:j + T, :] * conv_w[j] for j in range(CONV_W)) + conv_b
    gate, val = jnp.split(h, 2, axis=-1)
    return (jax.nn.silu(gate) * val) @ w_down

def first_inputs(seed: int = 0) -> dict:
    key = jax.random.key(seed)
    ks = jax.random.split(key, 24)
    f32 = jnp.float32

    def nrm(k, shape, scale):
        return jax.random.normal(k, shape, f32) * scale

    return {
        'x': nrm(ks[0], (BATCH, SEQ, D_MODEL), 1.0),
        'w_in_ab': nrm(ks[1], (N_EVEN, D_MODEL, IN0_COLS), D_MODEL ** -0.5),
        'hgrn_lb_table': nrm(ks[2], (DEPTH + 1, A_WIDTH), 0.1),
        'hgrn_norm_g': 1.0 + nrm(ks[3], (N_EVEN, A_WIDTH), 0.02),
        'gmlp_ln_g': 1.0 + nrm(ks[4], (N_EVEN, B_WIDTH), 0.02),
        'gmlp_ln_b': nrm(ks[5], (N_EVEN, B_WIDTH), 0.02),
        'gmlp_ws': nrm(ks[6], (N_EVEN, B_GROUPS, B_CHUNK, B_CHUNK), B_CHUNK ** -0.5),
        'gmlp_bias': 1.0 + nrm(ks[7], (N_EVEN, B_GROUPS, B_CHUNK), 0.02),
        'w_out_ab': nrm(ks[8], (N_EVEN, MIX0_WIDTH, D_MODEL), BETA * MIX0_WIDTH ** -0.5),
        'w_in_attn': nrm(ks[9], (N_ODD, D_MODEL, IN1_COLS), D_MODEL ** -0.5),
        'q_norm_g': 1.0 + nrm(ks[10], (N_ODD, C_HEAD_DIM), 0.02),
        'k_norm_g': 1.0 + nrm(ks[11], (N_ODD, C_HEAD_DIM), 0.02),
        'w_out_attn': nrm(ks[12], (N_ODD, MIX1_WIDTH, D_MODEL), BETA * MIX1_WIDTH ** -0.5),
        'ffn_up': nrm(ks[13], (DEPTH, D_MODEL, 2 * D_FF), D_MODEL ** -0.5),
        'ffn_conv_w': nrm(ks[14], (DEPTH, CONV_W, 2 * D_FF), CONV_W ** -0.5),
        'ffn_conv_b': nrm(ks[15], (DEPTH, 2 * D_FF), 0.02),
        'ffn_down': nrm(ks[16], (DEPTH, D_FF, D_MODEL), BETA * D_FF ** -0.5),
        'ln1_g': 1.0 + nrm(ks[17], (DEPTH, D_MODEL), 0.02),
        'ln1_b': nrm(ks[18], (DEPTH, D_MODEL), 0.02),
        'ln2_g': 1.0 + nrm(ks[19], (DEPTH, D_MODEL), 0.02),
        'ln2_b': nrm(ks[20], (DEPTH, D_MODEL), 0.02),
    }

def first_block(x, w_in_ab, hgrn_lb_table, hgrn_norm_g, gmlp_ln_g, gmlp_ln_b, gmlp_ws, gmlp_bias,
              w_out_ab, w_in_attn, q_norm_g, k_norm_g, w_out_attn, ffn_up, ffn_conv_w, ffn_conv_b,
              ffn_down, ln1_g, ln1_b, ln2_g, ln2_b):
    lb_all = jnp.cumsum(jax.nn.softmax(hgrn_lb_table.astype(jnp.float32), axis=0), axis=0)
    for layer in range(DEPTH):
        j = layer // 2
        if layer % 2 == 0:
            mix = even_mixer(x, w_in_ab[j], lb_all[layer], hgrn_norm_g[j], gmlp_ln_g[j], gmlp_ln_b[j],
                             gmlp_ws[j], gmlp_bias[j], w_out_ab[j])
        else:
            mix = odd_mixer(x, w_in_attn[j], q_norm_g[j], k_norm_g[j], w_out_attn[j])
        x = layer_norm(ALPHA * x + mix, ln1_g[layer], ln1_b[layer])
        x = layer_norm(ALPHA * x + conv_ffn(x, ffn_up[layer], ffn_conv_w[layer], ffn_conv_b[layer], ffn_down[layer]),
                       ln2_g[layer], ln2_b[layer])
    return x


DEPTH_2 = 1

D_RNN = 2048
RNN_BLOCKS = 16
RNN_BLOCK_W = D_RNN // RNN_BLOCKS
CONV_W_2 = 4
LRU_C = 8.0
HEAD_DIM = 128
HEADS_PER_GROUP = 8
DILATED_GROUPS = ((128, 1), (512, 4), (2048, 16))
N_GROUPS = len(DILATED_GROUPS)
N_ATTN_HEADS = N_GROUPS * HEADS_PER_GROUP
D_QKV = N_ATTN_HEADS * HEAD_DIM
D_ATTN_OUT = HEADS_PER_GROUP * HEAD_DIM
ATTN_BLOCK = 128
ROPE_THETA_2 = 500000.0
ROT_DIM = HEAD_DIM // 4
NORM_EPS = 1e-6
SPLIT_SIZES = (D_RNN, D_RNN, D_QKV, D_QKV, D_QKV, D_ATTN_OUT, D_MODEL, D_MODEL)
D_IN_TOTAL = 2 * D_RNN + 3 * D_QKV + D_ATTN_OUT + 2 * D_MODEL


def rms_norm_2(x, g):
    xf = x.astype(jnp.float32)
    y = xf * lax.rsqrt(jnp.mean(xf * xf, axis=-1, keepdims=True) + NORM_EPS)
    return (y * g.astype(jnp.float32)).astype(x.dtype)

def split_columns(p):
    offs, acc = [], 0
    for s in SPLIT_SIZES[:-1]:
        acc += s
        offs.append(acc)
    return jnp.split(p, offs, axis=-1)

def partial_rope(t, pos):
    half = ROT_DIM // 2
    inv = jnp.exp(-math.log(ROPE_THETA_2) * jnp.arange(half, dtype=jnp.float32) * (2.0 / ROT_DIM))
    ang = pos.astype(jnp.float32)[:, None] * inv[None, :]
    cos = jnp.cos(ang)[None, :, None, :]
    sin = jnp.sin(ang)[None, :, None, :]
    tr = t[..., :ROT_DIM].astype(jnp.float32)
    t1, t2 = tr[..., :half], tr[..., half:]
    rot = jnp.concatenate([t1 * cos - t2 * sin, t2 * cos + t1 * sin], axis=-1)
    return jnp.concatenate([rot.astype(t.dtype), t[..., ROT_DIM:]], axis=-1)

def rg_lru(u, conv_w, conv_b, w_rg, b_rg, w_ig, b_ig, lru_lambda):
    B, S, C = u.shape
    xc = lax.conv_general_dilated(
        u, conv_w[:, None, :].astype(u.dtype), window_strides=(1,), padding=[(CONV_W_2 - 1, 0)],
        dimension_numbers=("NWC", "WIO", "NWC"), feature_group_count=C) + conv_b
    xb = xc.reshape(B, S, RNN_BLOCKS, RNN_BLOCK_W)
    r = jax.nn.sigmoid(jnp.einsum('bsnc,ncd->bsnd', xb, w_rg).reshape(B, S, C) + b_rg)
    i = jax.nn.sigmoid(jnp.einsum('bsnc,ncd->bsnd', xb, w_ig).reshape(B, S, C) + b_ig)
    log_a = -LRU_C * r.astype(jnp.float32) * jax.nn.softplus(-lru_lambda.astype(jnp.float32))
    a = jnp.exp(log_a)
    b = jnp.sqrt(-jnp.expm1(2.0 * log_a)) * (i * xc).astype(jnp.float32)

    def combine(left, right):
        a1, b1 = left
        a2, b2 = right
        return a1 * a2, a2 * b1 + b2

    _, h = lax.associative_scan(combine, (a, b), axis=1)
    return h.astype(u.dtype)

def dilated_group_attention(q, k, v, window, dilation):
    B, S, H, D = q.shape
    L = S // dilation
    steps = window // dilation
    n_blk = -(-L // ATTN_BLOCK)
    Lp = n_blk * ATTN_BLOCK

    def to_blocks(t):
        t = t.reshape(B, L, dilation, H, D).transpose(0, 2, 1, 3, 4)
        t = jnp.pad(t, ((0, 0), (0, 0), (0, Lp - L), (0, 0), (0, 0)))
        return t.reshape(B, dilation, n_blk, ATTN_BLOCK, H, D)

    def with_prev(t):
        prev = jnp.pad(t, ((0, 0), (0, 0), (1, 0), (0, 0), (0, 0), (0, 0)))[:, :, :-1]
        return jnp.concatenate([prev, t], axis=3)

    qb = to_blocks(q).astype(jnp.float32)
    kk = with_prev(to_blocks(k)).astype(jnp.float32)
    vv = with_prev(to_blocks(v)).astype(jnp.float32)
    s = jnp.einsum('brnqhd,brnkhd->brnhqk', qb, kk) * (D ** -0.5)
    qi = jnp.arange(ATTN_BLOCK)[:, None]
    kj = jnp.arange(2 * ATTN_BLOCK)[None, :]
    dist = qi + ATTN_BLOCK - kj
    key_pos = jnp.arange(n_blk)[:, None, None] * ATTN_BLOCK + kj[None] - ATTN_BLOCK
    valid = (dist >= 0)[None] & (dist <= steps)[None] & (key_pos >= 0)
    s = jnp.where(valid[None, None, :, None], s, -1e30)
    m = jnp.max(s, axis=-1)
    p = jnp.exp(s - m[..., None])
    l = jnp.sum(p, axis=-1)
    o = jnp.einsum('brnhqk,brnkhd->brnqhd', p, vv) / jnp.swapaxes(l, -1, -2)[..., None]
    log_den = jnp.swapaxes(m + jnp.log(l), -1, -2)

    def from_blocks(t):
        rest = t.shape[4:]
        t = t.reshape((B, dilation, Lp) + rest)[:, :, :L]
        t = jnp.moveaxis(t, 1, 2)
        return t.reshape((B, S) + rest)

    return from_blocks(o), from_blocks(log_den)

def second_inputs(seed: int = 0) -> dict:
    key = jax.random.key(seed)
    ks = jax.random.split(key, 16)
    f32 = jnp.float32
    nrm = lambda k, shape, scale: jax.random.normal(k, shape, f32) * scale
    u = jax.random.uniform(ks[8], (DEPTH_2, D_RNN), f32, 0.9, 0.999)
    s = u ** (1.0 / LRU_C)
    lru_lambda = jnp.log(s) - jnp.log1p(-s)
    return {
        "x": jax.random.normal(ks[0], (BATCH, SEQ, D_MODEL), f32),
        "ln_pre_g": 1.0 + nrm(ks[1], (DEPTH_2, D_MODEL), 0.02),
        "w_in": nrm(ks[2], (DEPTH_2, D_MODEL, D_IN_TOTAL), D_MODEL ** -0.5),
        "conv_w": nrm(ks[3], (DEPTH_2, CONV_W_2, D_RNN), CONV_W_2 ** -0.5),
        "conv_b": nrm(ks[4], (DEPTH_2, D_RNN), 0.02),
        "w_rg": nrm(ks[5], (DEPTH_2, RNN_BLOCKS, RNN_BLOCK_W, RNN_BLOCK_W), RNN_BLOCK_W ** -0.5),
        "b_rg": nrm(ks[6], (DEPTH_2, D_RNN), 0.02),
        "w_ig": nrm(ks[7], (DEPTH_2, RNN_BLOCKS, RNN_BLOCK_W, RNN_BLOCK_W), RNN_BLOCK_W ** -0.5),
        "b_ig": nrm(ks[9], (DEPTH_2, D_RNN), 0.02),
        "lru_lambda": lru_lambda,
        "w_rnn_out": nrm(ks[10], (DEPTH_2, D_RNN, D_MODEL), D_RNN ** -0.5),
        "w_attn_out": nrm(ks[11], (DEPTH_2, D_ATTN_OUT, D_MODEL), D_ATTN_OUT ** -0.5),
        "w_o": nrm(ks[12], (DEPTH_2, D_MODEL, D_MODEL), D_MODEL ** -0.5),
        "ln_post_g": 1.0 + nrm(ks[13], (DEPTH_2, D_MODEL), 0.02),
    }

def second_block(x, ln_pre_g, w_in, conv_w, conv_b, w_rg, b_rg, w_ig, b_ig, lru_lambda,
              w_rnn_out, w_attn_out, w_o, ln_post_g):
    B, S, _ = x.shape
    pos = jnp.arange(S)
    for layer in range(DEPTH_2):
        h = rms_norm_2(x, ln_pre_g[layer])
        proj = jnp.einsum('bsd,de->bse', h, w_in[layer])
        rnn_x, rnn_gate, q, k, v, attn_gate, g_rnn, g_attn = split_columns(proj)

        hr = rg_lru(rnn_x, conv_w[layer], conv_b[layer], w_rg[layer], b_rg[layer],
                    w_ig[layer], b_ig[layer], lru_lambda[layer])
        y_rnn = jnp.einsum('bsc,cd->bsd', hr * jax.nn.silu(rnn_gate), w_rnn_out[layer])

        q = partial_rope(q.reshape(B, S, N_ATTN_HEADS, HEAD_DIM), pos)
        k = partial_rope(k.reshape(B, S, N_ATTN_HEADS, HEAD_DIM), pos)
        v = v.reshape(B, S, N_ATTN_HEADS, HEAD_DIM)
        q = q.reshape(B, S, N_GROUPS, HEADS_PER_GROUP, HEAD_DIM)
        k = k.reshape(B, S, N_GROUPS, HEADS_PER_GROUP, HEAD_DIM)
        v = v.reshape(B, S, N_GROUPS, HEADS_PER_GROUP, HEAD_DIM)
        outs, dens = [], []
        for g, (window, dilation) in enumerate(DILATED_GROUPS):
            o_g, d_g = dilated_group_attention(q[:, :, g], k[:, :, g], v[:, :, g], window, dilation)
            outs.append(o_g)
            dens.append(d_g)
        alpha = jax.nn.softmax(jnp.stack(dens, axis=0), axis=0)
        o = jnp.sum(alpha[..., None] * jnp.stack(outs, axis=0), axis=0)
        o = o.reshape(B, S, D_ATTN_OUT).astype(x.dtype)
        y_attn = jnp.einsum('bsc,cd->bsd', o * jax.nn.silu(attn_gate), w_attn_out[layer])

        merged = jax.nn.sigmoid(g_rnn) * y_rnn + jax.nn.sigmoid(g_attn) * y_attn
        y = jnp.einsum('bsd,de->bse', merged, w_o[layer])
        x = x + rms_norm_2(y, ln_post_g[layer])
    return x


def setup_inputs(seed=0):
    out = dict(first_inputs(seed))
    for name, value in second_inputs(seed + 1).items():
        if name != "x":
            out[name + "_2"] = value
    return out


def reference(
    x, w_in_ab, hgrn_lb_table, hgrn_norm_g, gmlp_ln_g, gmlp_ln_b, gmlp_ws, gmlp_bias, w_out_ab,
    w_in_attn, q_norm_g, k_norm_g, w_out_attn, ffn_up, ffn_conv_w, ffn_conv_b, ffn_down, ln1_g,
    ln1_b, ln2_g, ln2_b, ln_pre_g_2, w_in_2, conv_w_2, conv_b_2, w_rg_2, b_rg_2, w_ig_2, b_ig_2,
    lru_lambda_2, w_rnn_out_2, w_attn_out_2, w_o_2, ln_post_g_2,
):
    x = first_block(
        x, w_in_ab, hgrn_lb_table, hgrn_norm_g, gmlp_ln_g, gmlp_ln_b, gmlp_ws, gmlp_bias,
        w_out_ab, w_in_attn, q_norm_g, k_norm_g, w_out_attn, ffn_up, ffn_conv_w, ffn_conv_b,
        ffn_down, ln1_g, ln1_b, ln2_g, ln2_b,
    )
    return second_block(
        x, ln_pre_g_2, w_in_2, conv_w_2, conv_b_2, w_rg_2, b_rg_2, w_ig_2, b_ig_2, lru_lambda_2,
        w_rnn_out_2, w_attn_out_2, w_o_2, ln_post_g_2,
    )


_drawn_inputs = setup_inputs


def setup_inputs(seed=0):
    import zlib

    import numpy as np

    out = dict(_drawn_inputs(seed))
    spreads = {}
    factors = {'hgrn_lb_table': 4.589,
     'hgrn_norm_g': 8.0,
     'gmlp_ln_g': 8.0,
     'gmlp_ln_b': 8.0,
     'gmlp_bias': 8.0,
     'q_norm_g': 8.0,
     'k_norm_g': 8.0,
     'ffn_conv_b': 3.836,
     'b_rg_2': 8.0,
     'b_ig_2': 8.0,
     'ln_post_g_2': 3.938}
    for name, (base, spread) in spreads.items():
        noise = np.random.default_rng([zlib.crc32(name.encode()), seed]).standard_normal(out[name].shape)
        drawn = base * np.exp(spread * noise) if base else spread * noise
        out[name] = __import__('jax').numpy.asarray(drawn.astype(out[name].dtype))
    for name, factor in factors.items():
        out[name] = (out[name] * factor).astype(out[name].dtype)
    return out
```

```python
import math
from contextlib import ExitStack

import numpy as np

import concourse.bass as bass
from concourse import mybir
from concourse.alu_op_type import AluOpType as ALU

F32 = mybir.dt.float32
F32R = mybir.dt.float32r
I32 = mybir.dt.int32
ACT = mybir.ActivationFunctionType
AX = mybir.AxisListType.X

P = 128
T = 256
DM = 2048
MT = DM // P
FF = 5632
FT = FF // P
FG = FT // 4
HT = 1024 // P
CK, CF = 4, 4
CHUNK = CK * CF * P
ALPHA = (2.0 * 2) ** 0.25
LN_EPS, RMS_EPS = 1e-5, 1e-6
SEG = 64
NSEG = T // SEG
LRU_C = 8.0
WINDOWS = ((128, 1), (512, 4), (2048, 16))

STAGES = [("mix0_in", 14, 4), ("mix0_out", 4, 4),
          ("up0", 2 * FG, 4), ("down0", 4, FT // CK),
          ("attn_in", 6, 4), ("attn_out", 4, 4),
          ("up1", 2 * FG, 4), ("down1", 4, FT // CK),
          ("rnn_in", 8, 4), ("half0", 10, 4), ("half1", 10, 4), ("gates", 8, 4),
          ("rnn_out", 4, 4), ("dil_out", 4, 2), ("last_out", 4, 4)]
TASK0, CHUNK0, NTASK, NCHUNK_OF = {}, {}, {}, {}
_t = _c = 0
for _name, _n, _k in STAGES:
    TASK0[_name], CHUNK0[_name], NTASK[_name], NCHUNK_OF[_name] = _t, _c, _n, _k
    _t += _n
    _c += _n * _k
NCHUNKS = _c

_READY = ["mix0_in", "mix0_out", "up0", "attn_in", "attn_out", "up1", "rnn_in", "rnn_out"]
READY0 = {n: 4 * i for i, n in enumerate(_READY)}
READY0["dil_out"] = 4 * len(_READY)
READY0["last_out"] = READY0["dil_out"] + 2

PARS = [("hgrn_lb_table", 3 * HT), ("hgrn_norm_g", HT), ("gmlp_ln_g", HT), ("gmlp_ln_b", HT),
        ("qk_norm_g", (16 + 4) // 2),
        ("ln1_g", 2 * MT), ("ln1_b", 2 * MT), ("ln2_g", 2 * MT), ("ln2_b", 2 * MT),
        ("ffn_conv_w", 2 * 3 * 2 * FT), ("ffn_conv_b", 2 * 2 * FT),
        ("ln_pre_g_2", MT), ("conv_w_2", 4 * MT), ("conv_b_2", MT), ("b_rg_2", MT), ("b_ig_2", MT),
        ("lru_lambda_2", MT), ("ln_post_g_2", MT)]
PAR0, _c = {}, 0
for _name, _n in PARS:
    PAR0[_name] = _c
    _c += _n
NPAR = _c

CONS = [("ident", P), ("seg_start", T), ("fw_mask", 4 * P), ("bw_mask", 4 * P),
        ("rope1_perm", P), ("rope1_cos", T), ("rope1_sin", T),
        ("rope2_perm", P), ("rope2_cos", T), ("rope2_sin", T),
        ("dil_mask0", 3 * P), ("dil_mask1", 3 * T)]
CON0, _c = {}, 0
for _name, _n in CONS:
    CON0[_name] = _c
    _c += _n
NCON = _c


def program(nc, d):
    ctx = ExitStack()
    with ctx:
        base = (nc.sbuf_base + 63) // 64 * 64
        at = [base]

        def place(name, shape, dt=F32, offset=None):
            size = 4 * int(np.prod(shape[1:]))
            if offset is None:
                offset = at[0]
                at[0] += (size + 31) // 32 * 32
            return nc.alloc_sbuf_tensor_at(name, shape, dt, offset=offset)

        raw = place("w_raw", [P, 2, CHUNK])
        whi = place("w_hi", [P, 2, CHUNK], F32R)
        wlo = place("w_lo", [P, 2, CHUNK], F32R)
        X0 = at[0]
        xhl = place("x_hi_lo", [P, MT, 2 * T], F32R)
        z = place("resid", [P, MT, T])
        U0 = at[0]
        hid = place("hidden_hi_lo", [P, FT, 2 * T], F32R)
        u = place("u_tiles", [P, 2 * FT, T], F32, U0)
        W0 = at[0]
        WSIZE = 4 * 4 * (T + 2) * 2 + 2 * 4 * 4 * T
        at[0] += WSIZE
        par = place("par", [P, NPAR])
        ident = place("ident", [P, P])
        ones = place("ones", [P, P])
        eps = place("eps", [P, 8])
        lbs = place("lower_bound", [P, 4 * HT])
        nrg = place("rnn_cols", [P, 4 * MT])
        sbuf_end = at[0]
        assert sbuf_end <= nc.sbuf_usable_end, (sbuf_end, nc.sbuf_usable_end)
        fence = ctx.enter_context(nc.sbuf_tensor("fence", [P, (sbuf_end - nc.sbuf_base + 3) // 4], F32))

        names = [0]

        def over(start, pieces):
            out, o = [], start
            for shape in pieces:
                names[0] += 1
                out.append(place(f"over{names[0]}", shape, F32, o))
                o += (4 * int(np.prod(shape[1:])) + 31) // 32 * 32
            return out, o

        acc = ctx.enter_context(nc.psum_tensor("acc", [P, 8, 2 * T], F32))

        (gpad, vpad, gconv, vconv), end = over(W0, [[P, 4, T + 2], [P, 4, T + 2], [P, 4, T], [P, 4, T]])
        assert end <= W0 + WSIZE
        (zsum, mu, var, rstd, etmp, esq), end = over(
            W0, [[P, 2 * T], [P, T], [P, T], [P, T], [P, 4, T], [P, 4, T]])
        assert end <= W0 + WSIZE

        def sem(name):
            return ctx.enter_context(nc.semaphore(name))

        raw_landed = [sem("raw_landed0"), sem("raw_landed1")]
        weights_hi = sem("weights_hi")
        weights_split = sem("weights_split")
        chunk_used = sem("chunk_used")
        acc_free = sem("acc_free")
        moving_ready = sem("moving_ready")
        x_landed = sem("x_landed")
        par_landed = sem("par_landed")
        con_landed = sem("con_landed")
        consts_ready = sem("consts_ready")
        lb_exp = sem("lb_exp")
        lb_max = sem("lb_max")
        x_hi = sem("x_hi")
        z_ready = sem("z_ready")
        sq_ready = sem("sq_ready")
        sq_used = sem("sq_used")
        partials = sem("partials")
        sums_ready = sem("sums_ready")
        var_ready = sem("var_ready")
        rstd_ready = sem("rstd_ready")
        norm_ready = sem("norm_ready")
        out_ready = sem("out_ready")
        out_stored = sem("out_stored")

        block = ctx.enter_context(nc.Block())

        on = [name for name, _, _ in STAGES]

        def col(name, i=0, n=1):
            return par[:, bass.ds(PAR0[name] + i, n)]

        def loop(eng, trips, unroll=False):
            if trips == 1 or unroll:
                yield from range(trips)
            else:
                with eng.Fori(0, trips) as i:
                    yield i

        def cast_chunk(act, n, slot):
            act.wait_ge(raw_landed[slot], 16 * (n // 2 + 1) if isinstance(n, int) else n * 8 + (16 - 8 * slot))
            if not isinstance(n, int) or n >= 2:
                act.wait_ge(chunk_used, n - 1)
            nc.scalar.activation(whi[:, slot, :], raw[:, slot, :], ACT.Copy).then_inc(weights_hi, 1)

        def split_chunk(dve, n, slot):
            dve.wait_ge(weights_hi, n + 1)
            nc.vector.tensor_tensor(wlo[:, slot, :], raw[:, slot, :], whi[:, slot, :].bitcast(F32),
                                    ALU.subtract).then_inc(weights_split, 1)

        def drive(eng, name, piece, after_task, unroll=False, mid_task=None):
            per, nch = 2, NCHUNK_OF[name]
            for i in loop(eng, NTASK[name] // per, unroll):
                for t in range(per):
                    for c in range(1, nch):
                        at_c = t * nch + c
                        n = CHUNK0[name] + i * (per * nch) + at_c
                        if not isinstance(n, int) or n + 1 < NCHUNKS:
                            piece(eng, n + 1, (at_c + 1) % 2)
                        if c == nch - 1:
                            if not isinstance(n, int) or n + 2 < NCHUNKS:
                                piece(eng, n + 2, at_c % 2)
                            if after_task:
                                after_task(i, t, TASK0[name] + i * per + t, n)
                        elif mid_task:
                            mid_task(i, t, c)

        def multiply(pe, name, moving, ready=None):
            per, nch = 2, NCHUNK_OF[name]
            for i in loop(pe, NTASK[name] // per):
                for t in range(per):
                    pe.wait_ge(acc_free, TASK0[name] + i * per + t + 1)
                    for c in range(nch):
                        at_c = t * nch + c
                        s = at_c % 2
                        if t == 0 and ready:
                            ready(pe, c)
                        pe.wait_ge(weights_split, CHUNK0[name] + i * (per * nch) + at_c + 1)
                        for f in range(CF):
                            bank = 4 * t + f
                            for kk in range(CK):
                                k = CK * c + kk
                                w0 = (f * CK + kk) * P
                                both = (acc[:, bank, :], whi[:, s, w0:w0 + P], moving(k, 0, 2 * T))
                                rest = (acc[:, bank, 0:T], wlo[:, s, w0:w0 + P], moving(k, 0, T))
                                if k == 0:
                                    nc.tensor.matmul(*both, start=True, stop=False)
                                    last = nc.tensor.matmul(*rest, start=False, stop=False)
                                else:
                                    nc.tensor.matmul(*rest, start=False, stop=False)
                                    last = nc.tensor.matmul(*both, start=False,
                                                            stop=(k == CK * nch - 1))
                        last.then_inc(chunk_used, 1)

        def x_moving(k, a, b):
            return xhl[:, k, a:b]

        def hid_moving(k, a, b):
            return hid[:, k, a:b]

        def ready_from(name):
            def ready(pe, c):
                pe.wait_ge(moving_ready, READY0[name] + c + 1)
            return ready

        def halves(bank):
            return acc[:, bank, :].rearrange("p (h n) -> p n h", h=2)

        def read_out(dst, bank):
            return nc.vector.tensor_reduce(dst, halves(bank), AX, ALU.add)

        def dve_store(first_tile):
            def after(i, t, task, n):
                nc.vector.wait_ge(chunk_used, n + 1)
                for f in range(CF):
                    o = read_out(u[:, bass.ds(first_tile + i * 8 + t * 4 + f, 1), :].squeeze(1), 4 * t + f)
                o.then_inc(acc_free, 1)
            return after

        def dve_residual(occ):
            def after(i, t, task, n):
                nc.vector.wait_ge(chunk_used, n + 1)
                for f in range(CF):
                    o = read_out(etmp[:, f, :], 4 * t + f)
                o.then_inc(acc_free, 1)
                nc.vector.drain()
                for f in range(CF):
                    zt = z[:, bass.ds(i * 8 + t * 4 + f, 1), :].squeeze(1)
                    o = nc.vector.scalar_tensor_tensor(zt, zt, ALPHA, etmp[:, f, :], ALU.mult, ALU.add)
                o.then_inc(z_ready, 1)
            return after

        def act_squares(occ, src):
            def after(i, t, task, n):
                m = 4 * occ + i * 2 + t
                if occ < 4:
                    nc.scalar.wait_ge(z_ready, m + 1)
                else:
                    nc.scalar.wait_ge(acc_free, task + 3)
                nc.scalar.wait_ge(sq_used, m + 1)
                nc.scalar.activation(esq[:], src[:, bass.ds(i * 8 + t * 4, 4), :], ACT.Square)\
                    .then_inc(sq_ready, 1)
            return after

        def pool_sums(occ, src):
            pool = nc.gpsimd
            if occ == 4:
                pool.wait_ge(sums_ready, 5)
            elif occ == 5:
                pool.wait_ge(acc_free, TASK0["last_out"] + 3)
            else:
                pool.wait_ge(z_ready, 4 * occ + 1)
            pool.memset(zsum[:], 0.0)
            pool.drain()
            for i in loop(pool, 2):
                for t in range(2):
                    pool.wait_ge(sq_ready, 4 * occ + i * 2 + t + 1)
                    for f in range(4):
                        if src is not None:
                            pool.tensor_tensor(zsum[:, 0:T], zsum[:, 0:T],
                                               src[:, bass.ds(i * 8 + t * 4 + f, 1), :].squeeze(1), ALU.add)
                        pool.tensor_tensor(zsum[:, T:2 * T], zsum[:, T:2 * T], esq[:, f, :], ALU.add)
                        pool.drain()
                    pool.engine_nop().then_inc(sq_used, 1)
            pool.engine_nop().then_inc(partials, 1)

        def pe_sums(pe, s):
            pe.wait_ge(partials, s + 1)
            nc.tensor.matmul(acc[:, 0, :], ones[:], zsum[:], start=True, stop=True).then_inc(sums_ready, 1)

        def dve_mean_var(s, width):
            dve = nc.vector
            dve.wait_ge(sums_ready, s + 1)
            dve.tensor_scalar(mu[:], acc[:, 0, 0:T], 1.0 / width, None, ALU.mult)
            dve.drain()
            dve.tensor_tensor(rstd[:], mu[:], mu[:], ALU.mult)
            dve.drain()
            dve.scalar_tensor_tensor(var[:], acc[:, 0, T:2 * T], 1.0 / width, rstd[:], ALU.mult, ALU.subtract)
            dve.drain()
            dve.tensor_scalar(var[:], var[:], 0.0, None, ALU.max).then_inc(var_ready, 1)

        def act_rstd(v, e, src=None, scale=1.0):
            act = nc.scalar
            if src is None:
                act.wait_ge(var_ready, v + 1)
                src = var[:]
            act.activation(var[:], src, ACT.Ln, bias=eps[:, e:e + 1], scale=scale)
            act.drain()
            act.activation(rstd[:], var[:], ACT.Exp, scale=-0.5).then_inc(rstd_ready, 1)

        def wide(t2, n):
            return t2.unsqueeze(1).to_broadcast([P, n, T])

        def lo_part(dve, q, src, count, dst=None):
            dst = xhl[:, 4 * q:4 * q + 4, :] if dst is None else dst
            dve.wait_ge(x_hi, count)
            nc.vector.tensor_tensor(dst[:, :, T:2 * T], src, dst[:, :, 0:T].bitcast(F32), ALU.subtract)\
                .then_inc(moving_ready, 1)

        def hi_part(act, q, src, dst=None):
            dst = xhl[:, 4 * q:4 * q + 4, :] if dst is None else dst
            nc.scalar.activation(dst[:, :, 0:T], src, ACT.Copy).then_inc(x_hi, 1)

        def dve_norm(r, nxt):
            dve = nc.vector
            dve.wait_ge(rstd_ready, r + 1)
            for q in range(4):
                zq = z[:, 4 * q:4 * q + 4, :]
                dve.tensor_tensor(zq, zq, wide(mu[:], 4), ALU.subtract)
                dve.drain()
                dve.tensor_tensor(zq, zq, wide(rstd[:], 4), ALU.mult).then_inc(norm_ready, 1)
                if nxt and q:
                    lo_part(dve, q - 1, z[:, 4 * q - 4:4 * q, :], READY0[nxt] + q)
            if nxt:
                lo_part(dve, 3, z[:, 12:16, :], READY0[nxt] + 4)

        def act_affine(q0, g, b, nxt, off):
            act = nc.scalar
            for q in range(4):
                zq = z[:, 4 * q:4 * q + 4, :]
                act.wait_ge(norm_ready, q0 + q + 1)
                for m in range(4 * q, 4 * q + 4):
                    act.activation(z[:, m, :], z[:, m, :], ACT.Identity,
                                   bias=col(b, off + m), scale=col(g, off + m))
                act.drain()
                if nxt:
                    hi_part(act, q, zq)
                else:
                    m = 16 + q
                    act.wait_ge(sq_used, m + 1)
                    act.activation(esq[:], zq, ACT.Square).then_inc(sq_ready, 1)

        gate_conv = sem("gate_conv")
        val_conv = sem("val_conv")
        gate_silu = sem("gate_silu")
        hid_ready = sem("hid_ready")

        def dve_conv(layer):
            dve = nc.vector

            def conv(pad, out, i, val):
                w0 = PAR0["ffn_conv_w"] + layer * 3 * 2 * FT + val * FT
                b0 = PAR0["ffn_conv_b"] + layer * 2 * FT + val * FT

                def c(first, f):
                    return par[:, bass.ds(first + i * 4 + f, 1)]
                for f in range(4):
                    dve.tensor_scalar(out[:, f, :], pad[:, f, 1:T + 1], c(w0 + 2 * FT, f), c(b0, f),
                                      ALU.mult, ALU.add)
                dve.drain()
                for j in (0, 2):
                    for f in range(4):
                        o = dve.scalar_tensor_tensor(out[:, f, :], pad[:, f, j:j + T], c(w0 + j * 2 * FT, f),
                                                     out[:, f, :], ALU.mult, ALU.add)
                    if j == 0:
                        dve.drain()
                return o

            def after(i, t, task, n):
                dve.wait_ge(chunk_used, n + 1)
                pad = vpad if t else gpad
                for f in range(CF):
                    o = read_out(pad[:, f, 1:T + 1], 4 * t + f)
                o.then_inc(acc_free, 1)
                dve.drain()
                done = layer * FG + i
                if t == 0:
                    dve.wait_ge(hid_ready, done + 1)
                    conv(gpad, gconv, i, 0).then_inc(gate_conv, 1)
                else:
                    conv(vpad, vconv, i, 1).then_inc(val_conv, 1)
            return after

        def act_silu(layer):
            def after(i, t, task, n):
                if t == 0:
                    nc.scalar.wait_ge(gate_conv, layer * FG + i + 1)
                    nc.scalar.activation(gconv[:], gconv[:], ACT.Silu).then_inc(gate_silu, 1)
            return after

        def pool_hidden(layer):
            pool = nc.gpsimd
            for i in loop(pool, FG):
                pool.wait_ge(gate_silu, layer * FG + i + 1)
                pool.wait_ge(val_conv, layer * FG + i + 1)
                pool.tensor_tensor(vconv[:], vconv[:], gconv[:], ALU.mult)
                pool.drain()
                pool.tensor_copy(hid[:, bass.ds(i * 4, 4), 0:T], vconv[:])
                pool.drain()
                pool.tensor_tensor(hid[:, bass.ds(i * 4, 4), T:2 * T], vconv[:],
                                   hid[:, bass.ds(i * 4, 4), 0:T].bitcast(F32), ALU.subtract)\
                    .then_inc(hid_ready, 1)

        def hid_from(layer):
            def ready(pe, c):
                pe.wait_ge(hid_ready, layer * FG + c + 2)
            return ready

        (cum, gate, logf, key, qmid, kmid, klast, qcum), end = over(X0, [[P, 4, T]] * 8)
        assert end <= X0 + 4 * MT * 2 * T
        (vin, vtok, ktok, prob, state, gsil, osq, orn, fwm, bwm, seg1, decay), end = over(
            U0 + 4 * 7 * HT * T,
            [[P, 2, T], [P, 2, 2, P], [P, 8, P], [P, 8, P], [P, 4, 3, P], [P, 2, T], [P, 2, T], [P, 2, T],
             [P, 4, P], [P, 4, P], [P, T], [P, 4, NSEG]])
        assert end <= W0
        (gm_sq, gm_tok), end = over(X0, [[P, HT, T], [P, 2, HT, P]])
        (_, gm_ws, gm_bias), end = over(W0, [[P, 2 * T + 3 * T], [P, HT, P], [P, HT * P]])
        assert end <= W0 + WSIZE

        hg = {n: sem("hg_" + n) for n in (
            "vin", "exp", "gate", "log", "cum", "factors", "klast", "kmid", "qs", "vtok_ps", "vtok", "ktok_ps",
            "ktok", "kv_ps", "state", "score_ps", "prob", "out_ps", "sq", "ms_ps", "rn", "gexp", "done")}
        gm = {n: sem("gm_" + n) for n in ("sq", "norm", "affine", "tok_ps", "tok", "out_ps", "done")}
        Q0, FW0, BW0, I0, G0, UU0, V0 = (HT * i for i in range(7))
        def utile(first, n, i):
            return u[:, bass.ds(i * n + first, n), :]

        def pcol(name, off=0):
            return par[:, PAR0[name] + off:PAR0[name] + off + 1]

        def segs(t3):
            return t3.rearrange("p a (s c) -> p (a s) c", c=SEG)

        kv_order = [[(a, sg) for a in range(4) for sg in ((0, 1, 2) if a < 2 else (3, 2, 1)) if sg % 2 == odd]
                    for odd in range(2)]

        def kv_place(a, sg):
            i = kv_order[sg % 2].index((a, sg))
            return acc[:, 3 + 2 * (sg % 2) + i // 4, (i % 4) * P:(i % 4 + 1) * P]

        def hgrn_act(act):
            act.wait_ge(lb_max, 1)
            act.activation(lbs[:, HT:4 * HT], lbs[:, HT:4 * HT], ACT.Exp).then_inc(lb_exp, 1)
            act.wait_ge(acc_free, TASK0["mix0_out"] + 2)
            for g in loop(act, 4):
                act.wait_ge(hg["done"], g + 1)
                act.activation(vin[:], utile(I0, 2, g), ACT.Copy).then_inc(hg["vin"], 1)
                act.activation(cum[:, 0:2, :], utile(FW0, 2, g), ACT.Exp, scale=-1.0)
                act.activation(cum[:, 2:4, :], utile(BW0, 2, g), ACT.Exp, scale=-1.0).then_inc(hg["exp"], 1)
                act.activation(gsil[:], utile(G0, 2, g), ACT.Exp, scale=-1.0).then_inc(hg["gexp"], 1)
                act.wait_ge(hg["gate"], g + 1)
                act.activation(logf[:], gate[:], ACT.Ln).then_inc(hg["log"], 1)
                act.wait_ge(hg["cum"], g + 1)
                act.activation(klast[:], logf[:], ACT.Exp)
                act.activation(kmid[:], gate[:], ACT.Exp, scale=-1.0)
                act.activation(qmid[:], gate[:], ACT.Exp)
                act.activation(decay[:, 0:2, :], cum[:, 0:2, SEG - 1:T:SEG], ACT.Exp)
                act.activation(decay[:, 2:4, :], cum[:, 2:4, 0:T:SEG], ACT.Exp)
                act.activation(qcum[:], cum[:], ACT.Exp).then_inc(hg["factors"], 1)
                act.wait_ge(hg["ktok_ps"], g + 1)
                for b in range(2):
                    o = act.activation(ktok[:, 4 * b:4 * b + 4, :].rearrange("p a n -> p (a n)"),
                                       acc[:, 1 + b, :], ACT.Copy)
                o.then_inc(hg["ktok"], 1)
                act.wait_ge(hg["out_ps"], g + 1)
                act.activation(osq[:].rearrange("p a n -> p (a n)"), acc[:, 7, :], ACT.Square)\
                   .then_inc(hg["sq"], 1)
                act.wait_ge(hg["ms_ps"], g + 1)
                orow = orn[:].rearrange("p a n -> p (a n)")
                act.activation(orow, acc[:, 0, :], ACT.Ln, bias=eps[:, 1:2], scale=1.0 / P)
                act.drain()
                act.activation(orow, orow, ACT.Exp, scale=-0.5).then_inc(hg["rn"], 1)
            act.activation(gm_sq[:], u[:, V0:V0 + HT, :], ACT.Square).then_inc(gm["sq"], 1)
            act_rstd(0, 0)
            act.wait_ge(gm["norm"], 1)
            for m in range(HT):
                o = act.activation(u[:, V0 + m, :], u[:, V0 + m, :], ACT.Identity,
                                   bias=pcol("gmlp_ln_b", m), scale=pcol("gmlp_ln_g", m))
            o.then_inc(gm["affine"], 1)
            act.wait_ge(gm["tok_ps"], 1)
            for b in range(4):
                o = act.activation(gm_tok[:].rearrange("p n g c -> p (n g c)")[:, 512 * b:512 * b + 512],
                                   acc[:, b, :], ACT.Copy)
            o.then_inc(gm["tok"], 1)
            for q in range(4):
                t0 = (Q0 + 4 * q) if q < 2 else UU0 + 4 * (q - 2)
                act.wait_ge(gm["done"], 1)
                hi_part(act, q, u[:, t0:t0 + 4, :])

        def hgrn_dve(dve):
            dve.memset(prob[:], 0.0)
            for g in loop(dve, 4):
                dve.wait_ge(hg["exp"], g + 1)
                dve.tensor_scalar(cum[:], cum[:], 1.0, None, ALU.add)
                dve.drain()
                dve.reciprocal(cum[:], cum[:])
                dve.drain()
                for a in range(4):
                    h = g * 2 + a % 2
                    o = dve.tensor_scalar(gate[:, a, :], cum[:, a, :], lbs[:, bass.ds(h + HT, 1)],
                                          lbs[:, bass.ds(h, 1)], ALU.mult, ALU.add)
                o.then_inc(hg["gate"], 1)
                dve.drain()
                dve.tensor_scalar(key[:], gate[:], -1.0, 1.0, ALU.mult, ALU.add)
                dve.wait_ge(hg["gexp"], g + 1)
                dve.tensor_scalar(gsil[:], gsil[:], 1.0, None, ALU.add)
                dve.drain()
                dve.reciprocal(gsil[:], gsil[:])
                dve.drain()
                dve.tensor_tensor(gsil[:], gsil[:], utile(G0, 2, g), ALU.mult)
                dve.wait_ge(hg["vtok_ps"], g + 1)
                dve.tensor_copy(vtok[:].rearrange("p b h n -> p (b h n)"), acc[:, 0, :]).then_inc(hg["vtok"], 1)
                dve.wait_ge(hg["log"], g + 1)
                for a in range(4):
                    way = slice(None) if a < 2 else slice(None, None, -1)
                    dve.tensor_tensor_scan(cum[:, a, way], seg1[:], logf[:, a, way], 0.0, ALU.mult, ALU.add)
                dve.drain()
                for dr, (mid, end) in enumerate(((SEG // 2 - 1, SEG - 1), (SEG // 2, 0))):
                    a = slice(2 * dr, 2 * dr + 2)
                    c = segs(cum[:, a, :])
                    shape = [P, 2 * NSEG, SEG]
                    dve.tensor_tensor(segs(gate[:, a, :]), c, c[:, :, mid:mid + 1].to_broadcast(shape), ALU.subtract)
                    o = dve.tensor_tensor(segs(logf[:, a, :]), c[:, :, end:end + 1].to_broadcast(shape), c,
                                          ALU.subtract)
                o.then_inc(hg["cum"], 1)
                dve.wait_ge(hg["factors"], g + 1)
                dve.tensor_tensor(klast[:], klast[:], key[:], ALU.mult).then_inc(hg["klast"], 1)
                dve.tensor_tensor(kmid[:], kmid[:], key[:], ALU.mult).then_inc(hg["kmid"], 1)
                dve.wait_ge(hg["kv_ps"], g + 1)
                for j in range(3):
                    if j == 2:
                        dve.wait_ge(hg["score_ps"], g + 1)
                    for a in range(4):
                        sg = j if a < 2 else NSEG - 1 - j
                        kv = kv_place(a, sg)
                        if j == 0:
                            o = dve.tensor_copy(state[:, a, j, :], kv)
                        else:
                            o = dve.scalar_tensor_tensor(state[:, a, j, :], state[:, a, j - 1, :],
                                                         decay[:, a, sg:sg + 1], kv, ALU.mult, ALU.add)
                    if j < 2:
                        dve.drain()
                o.then_inc(hg["state"], 1)
                for dr, mask in enumerate((fwm, bwm)):
                    o = dve.copy_predicated(prob[:, 4 * dr:4 * dr + 4, :], mask[:].bitcast(I32),
                                            acc[:, 1 + dr, :].rearrange("p (a n) -> p a n", a=4))
                o.then_inc(hg["prob"], 1)
                dve.wait_ge(hg["rn"], g + 1)
                for hh in range(2):
                    dve.scalar_tensor_tensor(osq[:, hh, :], acc[:, 7, hh * T:hh * T + T],
                                             col("hgrn_norm_g", g * 2 + hh), orn[:, hh, :], ALU.mult, ALU.mult)
                dve.drain()
                dve.tensor_tensor(utile(Q0, 2, g), osq[:], gsil[:], ALU.mult).then_inc(hg["done"], 1)
            dve.tensor_reduce(zsum[:, 0:T], u[:, V0:V0 + HT, :].rearrange("p m n -> p n m"), AX, ALU.add)
            dve.wait_ge(gm["sq"], 1)
            dve.tensor_reduce(zsum[:, T:2 * T], gm_sq[:].rearrange("p m n -> p n m"), AX, ALU.add)\
               .then_inc(partials, 1)
            dve_mean_var(0, HT * P)
            dve.wait_ge(rstd_ready, 1)
            v = u[:, V0:V0 + HT, :]
            dve.tensor_tensor(v, v, wide(mu[:], HT), ALU.subtract)
            dve.drain()
            dve.tensor_tensor(v, v, wide(rstd[:], HT), ALU.mult).then_inc(gm["norm"], 1)
            dve.wait_ge(gm["out_ps"], 1)
            for b in range(4):
                ub = u[:, UU0 + 2 * b:UU0 + 2 * b + 2, :]
                o = dve.tensor_tensor(ub, ub, acc[:, 4 + b, :].rearrange("p (g n) -> p g n", g=2), ALU.mult)
            o.then_inc(gm["done"], 1)
            for q in range(4):
                t0 = (Q0 + 4 * q) if q < 2 else UU0 + 4 * (q - 2)
                lo_part(dve, q, u[:, t0:t0 + 4, :], READY0["mix0_out"] + q + 1)

        def hgrn_pool(pool):
            for g in loop(pool, 4):
                pool.wait_ge(hg["factors"], g + 1)
                for dr in range(2):
                    a = slice(2 * dr, 2 * dr + 2)
                    pool.tensor_tensor(qmid[:, a, :], qmid[:, a, :], utile(Q0, 2, g), ALU.mult)
                    pool.tensor_tensor(qcum[:, a, :], qcum[:, a, :], utile(Q0, 2, g), ALU.mult)
                pool.drain()
                pool.engine_nop().then_inc(hg["qs"], 1)

        def hgrn_pe(pe):
            for g in loop(pe, 4):
                pe.wait_ge(hg["vin"], g + 1)
                for b in range(2):
                    for hh in range(2):
                        o = nc.tensor.transpose(acc[:, 0, (2 * b + hh) * P:(2 * b + hh + 1) * P],
                                                vin[:, hh, b * P:(b + 1) * P], ident[:])
                o.then_inc(hg["vtok_ps"], 1)
                pe.wait_ge(hg["klast"], g + 1)
                for a in range(4):
                    for b in range(2):
                        i = 2 * a + b
                        o = nc.tensor.transpose(acc[:, 1 + i // 4, (i % 4) * P:(i % 4 + 1) * P],
                                                klast[:, a, b * P:(b + 1) * P], ident[:])
                o.then_inc(hg["ktok_ps"], 1)
                pe.wait_ge(hg["ktok"], g + 1)
                pe.wait_ge(hg["vtok"], g + 1)
                for a in range(4):
                    for j in range(3):
                        sg = j if a < 2 else NSEG - 1 - j
                        rows = slice(SEG * (sg % 2), SEG * (sg % 2) + SEG)
                        o = nc.tensor.matmul(kv_place(a, sg), ktok[rows, 2 * a + sg // 2, :],
                                             vtok[rows, sg // 2, a % 2, :], start=True, stop=True)
                o.then_inc(hg["kv_ps"], 1)
                pe.wait_ge(hg["kmid"], g + 1)
                pe.wait_ge(hg["qs"], g + 1)
                for a in range(4):
                    for b in range(2):
                        i = 2 * a + b
                        o = nc.tensor.matmul(acc[:, 1 + i // 4, (i % 4) * P:(i % 4 + 1) * P],
                                             kmid[:, a, b * P:(b + 1) * P], qmid[:, a, b * P:(b + 1) * P],
                                             start=True, stop=True)
                o.then_inc(hg["score_ps"], 1)
                pe.wait_ge(hg["prob"], g + 1)
                pe.wait_ge(hg["state"], g + 1)
                for hh in range(2):
                    o0 = hh * T
                    for a in (hh, 2 + hh):
                        for b in range(2):
                            nc.tensor.matmul(acc[:, 7, o0 + b * P:o0 + (b + 1) * P], vtok[:, b, hh, :],
                                             prob[:, 2 * a + b, :], start=(a < 2 and b == 0), stop=False)
                        for j in range(3):
                            sg = j + 1 if a < 2 else NSEG - 2 - j
                            o = nc.tensor.matmul(acc[:, 7, o0 + sg * SEG:o0 + (sg + 1) * SEG], state[:, a, j, :],
                                                 qcum[:, a, sg * SEG:(sg + 1) * SEG], start=False,
                                                 stop=(a >= 2 and j == 2))
                o.then_inc(hg["out_ps"], 1)
                pe.wait_ge(hg["sq"], g + 1)
                nc.tensor.matmul(acc[:, 0, :], ones[:], osq[:].rearrange("p a n -> p (a n)"),
                                 start=True, stop=True).then_inc(hg["ms_ps"], 1)
            pe_sums(pe, 0)
            pe.wait_ge(gm["affine"], 1)
            for n in range(2):
                for m in range(HT):
                    i = n * HT + m
                    o = nc.tensor.transpose(acc[:, i // 4, (i % 4) * P:(i % 4 + 1) * P],
                                            u[:, V0 + m, n * P:(n + 1) * P], ident[:])
            o.then_inc(gm["tok_ps"], 1)
            pe.wait_ge(gm["tok"], 1)
            for m in range(HT):
                for n in range(2):
                    dst = acc[:, 4 + m // 2, (m % 2) * T + n * P:(m % 2) * T + (n + 1) * P]
                    nc.tensor.matmul(dst, ones[0:1, :], gm_bias[0:1, m * P:(m + 1) * P], start=True, stop=False)
                    o = nc.tensor.matmul(dst, gm_tok[:, n, m, :], gm_ws[:, m, :], start=False, stop=True)
            o.then_inc(gm["out_ps"], 1)

        (r_sq, r_rn, r_g, r_cos, perm1, cos1, sin1), end = over(
            U0 + 4 * 24 * T, [[P, 2, 2, T]] * 4 + [[P, P], [P, T], [P, T]])
        (q_st, v_in, v_tok, p_row, p_tok, mx, rs), end = over(
            end, [[P, 4, T], [P, T], [P, 2, P], [P, 8, T], [P, 4, 2 * T], [P, 8], [P, 8]])
        assert end <= W0
        at_ = {n: sem("at_" + n) for n in (
            "con", "sq", "ms_ps", "rn", "g", "rot_ps", "cos", "turned", "copied", "vtok_ps", "vtok", "score_ps", "max",
            "exp", "prob", "ptok_ps", "ptok", "out_ps")}
        SCALE = float(P) ** -0.5
        NPAIR = 10

        def flat(x):
            return x.rearrange("p a n -> p (a n)")

        def attn_act(act):
            act.wait_ge(acc_free, TASK0["attn_out"] + 2)
            for i in loop(act, NPAIR // 2):
                for b in range(2):
                    m = i * 2 + b
                    act.activation(r_sq[:, b], utile(2 * b, 4, i)[:, 0:2, :], ACT.Square).then_inc(at_["sq"], 1)
                    act.wait_ge(at_["ms_ps"], m + 1)
                    act.wait_ge(at_["g"], m + 1)
                    act.activation(flat(r_rn[:, b]), acc[:, b, :], ACT.Ln, bias=eps[:, 1:2], scale=1.0 / P)
                    act.drain()
                    act.activation(r_rn[:, b], r_rn[:, b], ACT.Exp, scale=-0.5).then_inc(at_["rn"], 1)
            act.wait_ge(at_["turned"], NPAIR)
            for g in loop(act, 4):
                act.wait_ge(moving_ready, g + READY0["attn_out"])
                act.activation(q_st[:], utile(0, 4, g), ACT.Copy)
                act.activation(v_in[:], utile(20, 1, g).squeeze(1), ACT.Copy).then_inc(at_["copied"], 1)
                act.wait_ge(at_["max"], g + 1)
                for h in range(4):
                    for b in range(2):
                        i = 2 * h + b
                        o = act.activation(p_row[:, i, :], acc[:, h, b * T:(b + 1) * T], ACT.Exp,
                                           bias=mx[:, i:i + 1], scale=SCALE, accum_out=rs[:, i:i + 1])
                o.then_inc(at_["exp"], 1)
                act.wait_ge(at_["ptok_ps"], g + 1)
                for h in range(4):
                    o = act.activation(p_tok[:, h, :], acc[:, 4 + h, :], ACT.Copy)
                o.then_inc(at_["ptok"], 1)
                act.wait_ge(at_["out_ps"], g + 1)
                act.activation(xhl[:, bass.ds(g * 4, 4), 0:T],
                               acc[:, 0:2, :].rearrange("p b (h n) -> p (b h) n", h=2), ACT.Copy).then_inc(x_hi, 1)

        def attn_dve(dve):
            dve.wait_ge(at_["con"], 48)
            for i in loop(dve, NPAIR // 2):
                for b in range(2):
                    m = i * 2 + b
                    pair = utile(2 * b, 4, i)[:, 0:2, :]
                    dve.wait_ge(at_["sq"], m + 1)
                    dve.tensor_scalar(r_g[:, b], pair, col("qk_norm_g", m), None, ALU.mult).then_inc(at_["g"], 1)
                    dve.wait_ge(at_["rot_ps"], m + 1)
                    dve.tensor_tensor(pair, acc[:, 2 + b, :].rearrange("p (a n) -> p a n", a=2),
                                      wide(sin1[:], 2), ALU.mult)
                    dve.drain()
                    dve.wait_ge(at_["cos"], m + 1)
                    dve.tensor_tensor(pair, pair, r_cos[:, b], ALU.add)
                    dve.drain()
                    dve.wait_ge(at_["rn"], m + 1)
                    dve.tensor_tensor(pair, pair, r_rn[:, b], ALU.mult).then_inc(at_["turned"], 1)
            for g in loop(dve, 4):
                dve.wait_ge(at_["vtok_ps"], g + 1)
                dve.tensor_copy(flat(v_tok[:]), acc[:, 4, 0:T]).then_inc(at_["vtok"], 1)
                dve.wait_ge(at_["score_ps"], g + 1)
                dve.tensor_reduce(mx[:], acc[:, 0:4, :].rearrange("p h (b n) -> p (h b) n", b=2), AX, ALU.max)
                dve.drain()
                dve.tensor_scalar(mx[:], mx[:], -SCALE, None, ALU.mult).then_inc(at_["max"], 1)
                dve.wait_ge(at_["exp"], g + 1)
                dve.reciprocal(rs[:], rs[:])
                dve.drain()
                dve.tensor_tensor(p_row[:], p_row[:], rs[:].unsqueeze(2).to_broadcast([P, 8, T]), ALU.mult)\
                   .then_inc(at_["prob"], 1)
                dve.wait_ge(x_hi, g + READY0["attn_out"] + 1)
                dst = xhl[:, bass.ds(g * 4, 4), :]
                dve.tensor_tensor(dst[:, :, T:2 * T], acc[:, 0:2, :].rearrange("p b (h n) -> p (b h) n", h=2),
                                  dst[:, :, 0:T].bitcast(F32), ALU.subtract).then_inc(moving_ready, 1)

        def attn_pool(pool):
            pool.wait_ge(at_["con"], 48)
            for i in loop(pool, NPAIR // 2):
                for b in range(2):
                    m = i * 2 + b
                    pool.wait_ge(at_["g"], m + 1)
                    pool.tensor_tensor(r_cos[:, b], r_g[:, b], wide(cos1[:], 2), ALU.mult).then_inc(at_["cos"], 1)

        def attn_pe(pe):
            pe.wait_ge(at_["con"], 48)
            for i in loop(pe, NPAIR // 2):
                for b in range(2):
                    m = i * 2 + b
                    pe.wait_ge(at_["sq"], m + 1)
                    nc.tensor.matmul(acc[:, b, :], ones[:], flat(r_sq[:, b]), start=True, stop=True)\
                        .then_inc(at_["ms_ps"], 1)
                    pe.wait_ge(at_["g"], m + 1)
                    nc.tensor.matmul(acc[:, 2 + b, :], perm1[:], flat(r_g[:, b]), start=True, stop=True)\
                        .then_inc(at_["rot_ps"], 1)
            for g in loop(pe, 4):
                pe.wait_ge(at_["copied"], g + 1)
                for b in range(2):
                    o = nc.tensor.transpose(acc[:, 4, b * P:(b + 1) * P], v_in[:, b * P:(b + 1) * P], ident[:])
                o.then_inc(at_["vtok_ps"], 1)
                for h in range(4):
                    for b in range(2):
                        o = nc.tensor.matmul(acc[:, h, b * T:(b + 1) * T], q_st[:, h, b * P:(b + 1) * P],
                                             utile(16, 1, g).squeeze(1), start=True, stop=True)
                o.then_inc(at_["score_ps"], 1)
                pe.wait_ge(at_["prob"], g + 1)
                pe.wait_ge(at_["vtok"], g + 1)
                for h in range(4):
                    for sb in range(2):
                        for b in range(2):
                            o = nc.tensor.transpose(acc[:, 4 + h, sb * T + b * P:sb * T + (b + 1) * P],
                                                    p_row[:, 2 * h + b, sb * P:(sb + 1) * P], ident[:])
                o.then_inc(at_["ptok_ps"], 1)
                pe.wait_ge(at_["ptok"], g + 1)
                for h in range(4):
                    for sb in range(2):
                        o = nc.tensor.matmul(acc[:, h // 2, (h % 2) * T:(h % 2 + 1) * T], v_tok[:, sb, :],
                                             p_tok[:, h, sb * T:(sb + 1) * T], start=(sb == 0), stop=(sb == 1))
                o.then_inc(at_["out_ps"], 1)
            pe.wait_ge(moving_ready, READY0["attn_out"] + 4)

        UX0, UG0, XC0, R0, IG0 = 0, MT, 2 * MT, 3 * MT, 4 * MT
        (w_gates,), end = over(W0, [[P, 2, MT, P]])
        assert end <= W0 + WSIZE
        ru = {n: sem("ru_" + n) for n in ("con", "abs", "e", "cols", "conv", "ps", "exp", "log", "tanh", "bsq",
                                          "sqrt", "silu", "done")}
        NBR, NBI, NSP, TMP = 0, MT, 2 * MT, 3 * MT

        def rnn_act(act):
            act.wait_ge(ru["abs"], 1)
            act.activation(nrg[:, TMP:TMP + MT], nrg[:, TMP:TMP + MT], ACT.Exp, scale=-1.0).then_inc(ru["e"], 1)
            act.wait_ge(ru["cols"], 1)
            for i in loop(act, 2):
                for b in range(8):
                    m = i * 8 + b
                    act.wait_ge(ru["ps"], m + 1)
                    act.activation(u[:, bass.ds(m + R0, 1), :].squeeze(1), acc[:, b, 0:T], ACT.Exp,
                                   bias=nrg[:, bass.ds(m + NBR, 1)], scale=-1.0)
                    act.activation(u[:, bass.ds(m + IG0, 1), :].squeeze(1), acc[:, b, T:2 * T], ACT.Exp,
                                   bias=nrg[:, bass.ds(m + NBI, 1)], scale=-1.0).then_inc(ru["exp"], 1)
            for q in loop(act, 4):
                act.wait_ge(ru["log"], q + 1)
                act.activation(utile(UX0, 4, q), utile(R0, 4, q), ACT.Exp)
                act.activation(utile(R0, 4, q), utile(R0, 4, q), ACT.Tanh).then_inc(ru["tanh"], 1)
            for q in loop(act, 4):
                act.wait_ge(ru["bsq"], q + 1)
                act.activation(utile(XC0, 4, q), utile(XC0, 4, q), ACT.Sqrt, scale=-1.0).then_inc(ru["sqrt"], 1)
            for q in loop(act, 4):
                act.activation(utile(UG0, 4, q), utile(UG0, 4, q), ACT.Silu).then_inc(ru["silu"], 1)

        def rnn_dve(dve):
            lam = par[:, PAR0["lru_lambda_2"]:PAR0["lru_lambda_2"] + MT]
            c = lambda at0: nrg[:, at0:at0 + MT]
            dve.wait_ge(par_landed, 16)
            dve.scalar_tensor_tensor(c(TMP), lam, -1.0, lam, ALU.mult, ALU.max).then_inc(ru["abs"], 1)
            b = PAR0["b_rg_2"]
            dve.tensor_scalar(nrg[:, NBR:NBR + 2 * MT], par[:, b:b + 2 * MT], -1.0, None, ALU.mult)
            dve.wait_ge(ru["e"], 1)
            dve.tensor_scalar(c(NSP), c(TMP), 2.0, None, ALU.add)
            dve.drain()
            dve.reciprocal(c(NSP), c(NSP))
            dve.drain()
            dve.tensor_tensor(c(TMP), c(TMP), c(NSP), ALU.mult)
            dve.drain()
            sq, ser = u[:, 5 * MT, 0:MT], u[:, 5 * MT, MT:2 * MT]
            dve.tensor_tensor(sq, c(TMP), c(TMP), ALU.mult)
            dve.memset(ser, 1.0 / 19)
            dve.drain()
            for k in range(8, -1, -1):
                dve.tensor_tensor(ser, ser, sq, ALU.mult)
                dve.drain()
                dve.tensor_scalar(ser, ser, 1.0 / (2 * k + 1), None, ALU.add)
                dve.drain()
            dve.scalar_tensor_tensor(c(TMP), ser, 2.0, c(TMP), ALU.mult, ALU.mult)
            dve.tensor_scalar(sq, lam, -1.0, 0.0, ALU.mult, ALU.max)
            dve.drain()
            dve.tensor_tensor(c(TMP), c(TMP), sq, ALU.add)
            dve.drain()
            dve.tensor_scalar(c(NSP), c(TMP), -LRU_C, None, ALU.mult).then_inc(ru["cols"], 1)
            cw = PAR0["conv_w_2"]
            for i in loop(dve, MT // 4):
                for f in range(4):
                    xc = u[:, bass.ds(i * 4 + f + XC0, 1), :].squeeze(1)
                    ux = u[:, bass.ds(i * 4 + f + UX0, 1), :].squeeze(1)
                    o = dve.tensor_scalar(xc, ux, par[:, bass.ds(i * 4 + f + cw + 3 * MT, 1)],
                                          col("conv_b_2", i * 4 + f), ALU.mult, ALU.add)
                dve.drain()
                for s in (1, 2, 3):
                    for f in range(4):
                        xc = u[:, bass.ds(i * 4 + f + XC0, 1), s:T].squeeze(1)
                        ux = u[:, bass.ds(i * 4 + f + UX0, 1), 0:T - s].squeeze(1)
                        o = dve.scalar_tensor_tensor(xc, ux, par[:, bass.ds(i * 4 + f + cw + (3 - s) * MT, 1)],
                                                     xc, ALU.mult, ALU.add)
                    if s < 3:
                        dve.drain()
                o.then_inc(ru["conv"], 1)
            for q in loop(dve, 4):
                dve.wait_ge(ru["exp"], q * 4 + 4)
                r, g = utile(R0, 4, q), utile(IG0, 4, q)
                for x in (r, g):
                    dve.tensor_scalar(x, x, 1.0, None, ALU.add)
                dve.drain()
                for x in (r, g):
                    dve.reciprocal(x, x)
                dve.drain()
                for f in range(4):
                    x = u[:, bass.ds(q * 4 + f + R0, 1), :].squeeze(1)
                    o = dve.tensor_scalar(x, x, nrg[:, bass.ds(q * 4 + f + NSP, 1)], None, ALU.mult)
                o.then_inc(ru["log"], 1)
                dve.tensor_tensor(g, g, utile(XC0, 4, q), ALU.mult)
            for q in loop(dve, 4):
                dve.wait_ge(ru["tanh"], q + 1)
                a, xq = utile(UX0, 4, q), utile(XC0, 4, q)
                dve.tensor_tensor(xq, a, a, ALU.mult)
                dve.drain()
                dve.scalar_tensor_tensor(xq, xq, 1.0, utile(R0, 4, q), ALU.add, ALU.mult).then_inc(ru["bsq"], 1)
            for q in loop(dve, 4):
                dve.wait_ge(ru["sqrt"], q + 1)
                g = utile(IG0, 4, q)
                dve.tensor_tensor(g, g, utile(XC0, 4, q), ALU.mult)
                dve.drain()
                for f in range(4):
                    t = lambda at0: u[:, bass.ds(q * 4 + f + at0, 1), :].squeeze(1)
                    dve.tensor_tensor_scan(t(R0), t(UX0), t(IG0), 0.0, ALU.mult, ALU.add)
                dve.drain()
                dve.wait_ge(ru["silu"], q + 1)
                dve.tensor_tensor(utile(UX0, 4, q), utile(R0, 4, q), utile(UG0, 4, q), ALU.mult)\
                   .then_inc(ru["done"], 1)

        def rnn_pe(pe):
            pe.wait_ge(ru["con"], 16)
            for m in range(MT):
                pe.wait_ge(ru["conv"], m // 4 + 1)
                if m >= 8:
                    pe.wait_ge(ru["exp"], m - 7)
                for j in range(2):
                    o = nc.tensor.matmul(acc[:, m % 8, j * T:(j + 1) * T], w_gates[:, j, m, :], u[:, XC0 + m, :],
                                         start=True, stop=True)
                o.then_inc(ru["ps"], 1)
            pe.wait_ge(ru["exp"], MT)

        QD, KD, VD, AG = 2 * MT, 2 * MT + 12, 2 * MT + 24, 2 * MT + 36
        OD = MT
        (perm2, cos2, sin2, mask0, mask1, t_cos, t_rot), end = over(
            W0, [[P, P], [P, T], [P, T], [P, 3 * P], [P, 3 * T], [P, 2, 2 * T], [P, 2, 2 * T]])
        assert end <= W0 + WSIZE
        (dq, dv), end = over(U0 + 4 * 24 * T, [[P, 3, T], [P, 3, T]])
        assert end <= U0 + 4 * 32 * T
        (dvt, dp0, dp1, dt0, dt1, dmx, drs), end = over(
            U0 + 4 * 72 * T, [[P, 6, P], [P, 3 * P], [P, 3 * T], [P, 3, P], [P, 6, P], [P, 2], [P, 2]])
        assert end <= W0
        dl = {n: sem("dl_" + n) for n in ("con", "rot_ps", "cos", "turned", "copied", "vtok_ps", "vtok", "score_ps",
                                          "max", "exp", "prob", "ptok_ps", "ptok", "out_ps", "out", "silu", "gated",
                                          "o_done")}

        def dil_act(hf):
            def run(act):
                act.wait_ge(dl["turned"], 12 * hf + 12)
                for h in loop(act, 4):
                    n = h + 4 * hf
                    act.wait_ge(dl["out"], n + 1)
                    act.activation(dq[:], u[:, bass.ds(h + QD, 12), :][:, 0:12:4, :], ACT.Copy)
                    act.activation(dv[:], u[:, bass.ds(h + VD, 12), :][:, 0:12:4, :], ACT.Copy)\
                       .then_inc(dl["copied"], 1)
                    act.wait_ge(dl["vtok_ps"], n + 1)
                    act.activation(dvt[:].rearrange("p a n -> p (a n)")[:, 0:4 * P], acc[:, 3, :], ACT.Copy)
                    act.activation(dvt[:].rearrange("p a n -> p (a n)")[:, 4 * P:6 * P], acc[:, 4, 0:2 * P], ACT.Copy)\
                       .then_inc(dl["vtok"], 1)
                    act.wait_ge(dl["max"], n + 1)
                    act.activation(dp0[:], dp0[:], ACT.Exp, bias=dmx[:, 0:1], accum_out=drs[:, 0:1])
                    act.activation(dp1[:], dp1[:], ACT.Exp, bias=dmx[:, 1:2], accum_out=drs[:, 1:2])\
                       .then_inc(dl["exp"], 1)
                    act.wait_ge(dl["ptok_ps"], n + 1)
                    act.activation(flat(dt0[:]), acc[:, 5, 0:3 * P], ACT.Copy)
                    act.activation(flat(dt1[:])[:, 0:4 * P], acc[:, 6, :], ACT.Copy)
                    act.activation(flat(dt1[:])[:, 4 * P:6 * P], acc[:, 7, 0:2 * P], ACT.Copy).then_inc(dl["ptok"], 1)
                act.activation(u[:, AG:AG + 4, :], u[:, AG:AG + 4, :], ACT.Silu).then_inc(dl["silu"], 1)
            return run

        def dil_dve(hf):
            def run(dve):
                dve.wait_ge(dl["con"], 80)
                for i in loop(dve, 6):
                    for b in range(2):
                        m = i * 2 + b + 12 * hf
                        pair = utile(QD + 2 * b, 4, i)[:, 0:2, :]
                        dve.wait_ge(dl["rot_ps"], m + 1)
                        dve.tensor_tensor(t_rot[:, b, :].rearrange("p (a n) -> p a n", a=2),
                                          acc[:, b, :].rearrange("p (a n) -> p a n", a=2), wide(sin2[:], 2), ALU.mult)
                        dve.drain()
                        dve.wait_ge(dl["cos"], m + 1)
                        dve.tensor_tensor(pair, t_rot[:, b, :].rearrange("p (a n) -> p a n", a=2),
                                          t_cos[:, b, :].rearrange("p (a n) -> p a n", a=2), ALU.add)\
                           .then_inc(dl["turned"], 1)
                for h in loop(dve, 4):
                    n = h + 4 * hf
                    dve.wait_ge(dl["score_ps"], n + 1)
                    dve.scalar_tensor_tensor(dp0[:], acc[:, 0, 0:3 * P], SCALE, mask0[:], ALU.mult, ALU.add)
                    dve.scalar_tensor_tensor(dp1[:, 0:2 * T], acc[:, 1, :], SCALE, mask1[:, 0:2 * T],
                                             ALU.mult, ALU.add)
                    dve.scalar_tensor_tensor(dp1[:, 2 * T:3 * T], acc[:, 2, 0:T], SCALE, mask1[:, 2 * T:3 * T],
                                             ALU.mult, ALU.add)
                    dve.drain()
                    dve.tensor_reduce(dmx[:, 0:1], dp0[:], AX, ALU.max)
                    dve.tensor_reduce(dmx[:, 1:2], dp1[:], AX, ALU.max)
                    dve.drain()
                    dve.tensor_scalar(dmx[:], dmx[:], -1.0, None, ALU.mult).then_inc(dl["max"], 1)
                    dve.wait_ge(dl["exp"], n + 1)
                    dve.reciprocal(drs[:], drs[:])
                    dve.drain()
                    dve.tensor_scalar(dp0[:], dp0[:], drs[:, 0:1], None, ALU.mult)
                    dve.tensor_scalar(dp1[:], dp1[:], drs[:, 1:2], None, ALU.mult).then_inc(dl["prob"], 1)
                    dve.wait_ge(dl["out_ps"], n + 1)
                    dve.tensor_copy(u[:, bass.ds(h + OD + 4 * hf, 1), :].squeeze(1), acc[:, 3, 0:T])\
                       .then_inc(dl["out"], 1)
                dve.wait_ge(dl["silu"], hf + 1)
                dve.drain()
                o = u[:, OD + 4 * hf:OD + 4 * hf + 4, :]
                dve.tensor_tensor(o, o, u[:, AG:AG + 4, :], ALU.mult).then_inc(dl["gated"], 1)
            return run

        def dil_pool(hf):
            def run(pool):
                pool.wait_ge(dl["con"], 80)
                pool.wait_ge(acc_free, TASK0["half%d" % hf] + NTASK["half%d" % hf] + 2)
                for i in loop(pool, 6):
                    for b in range(2):
                        m = i * 2 + b + 12 * hf
                        pool.wait_ge(dl["rot_ps"], m + 1)
                        pool.tensor_tensor(t_cos[:, b, :].rearrange("p (a n) -> p a n", a=2),
                                           utile(QD + 2 * b, 4, i)[:, 0:2, :], wide(cos2[:], 2), ALU.mult)\
                            .then_inc(dl["cos"], 1)
            return run

        def dil_pe(hf):
            def run(pe):
                pe.wait_ge(dl["con"], 80)
                pe.wait_ge(acc_free, TASK0["half%d" % hf] + NTASK["half%d" % hf] + 2)
                for m in range(12):
                    if m >= 2:
                        pe.wait_ge(dl["turned"], m - 1 + 12 * hf)
                    nc.tensor.matmul(acc[:, m % 2, :], perm2[:], flat(u[:, QD + 2 * m:QD + 2 * m + 2, :]),
                                     start=True, stop=True).then_inc(dl["rot_ps"], 1)
                for h in loop(pe, 4):
                    n = h + 4 * hf
                    pe.wait_ge(dl["copied"], n + 1)
                    for g in range(3):
                        for b in range(2):
                            i = 2 * g + b
                            o = nc.tensor.transpose(acc[:, 3 + i // 4, (i % 4) * P:(i % 4 + 1) * P],
                                                    dv[:, g, b * P:(b + 1) * P], ident[:])
                    o.then_inc(dl["vtok_ps"], 1)
                    for g in range(3):
                        k = u[:, bass.ds(h + KD + 4 * g, 1), :].squeeze(1)
                        nc.tensor.matmul(acc[:, 0, g * P:(g + 1) * P], dq[:, g, 0:P], k[:, 0:P],
                                         start=True, stop=True)
                        o = nc.tensor.matmul(acc[:, 1 + g // 2, (g % 2) * T:(g % 2 + 1) * T], dq[:, g, P:2 * P], k,
                                             start=True, stop=True)
                    o.then_inc(dl["score_ps"], 1)
                    pe.wait_ge(dl["prob"], n + 1)
                    for g in range(3):
                        nc.tensor.transpose(acc[:, 5, g * P:(g + 1) * P], dp0[:, g * P:(g + 1) * P], ident[:])
                    for i in range(6):
                        o = nc.tensor.transpose(acc[:, 6 + i // 4, (i % 4) * P:(i % 4 + 1) * P],
                                                dp1[:, i * P:(i + 1) * P], ident[:])
                    o.then_inc(dl["ptok_ps"], 1)
                    pe.wait_ge(dl["ptok"], n + 1)
                    pe.wait_ge(dl["vtok"], n + 1)
                    for g in range(3):
                        nc.tensor.matmul(acc[:, 3, 0:P], dvt[:, 2 * g, :], dt0[:, g, :], start=(g == 0), stop=(g == 2))
                    for i in range(6):
                        o = nc.tensor.matmul(acc[:, 3, P:2 * P], dvt[:, i, :], dt1[:, i, :],
                                             start=(i == 0), stop=(i == 5))
                    o.then_inc(dl["out_ps"], 1)
                pe.wait_ge(dl["out"], 4 * hf + 5)
            return run

        pre_norm = sem("pre_norm")
        pre_scaled = sem("pre_scaled")
        gates_sig = sem("gates_sig")
        merged = sem("merged")
        fin = sem("fin")

        def pre_act(act):
            act.wait_ge(sums_ready, 6)
            act_rstd(5, 1, acc[:, 0, T:2 * T], 1.0 / DM)
            for q in range(4):
                act.wait_ge(pre_norm, q + 1)
                for m in range(4 * q, 4 * q + 4):
                    act.activation(u[:, m, :], u[:, m, :], ACT.Copy, scale=pcol("ln_pre_g_2", m))
                act.drain()
                hi_part(act, q, u[:, 4 * q:4 * q + 4, :])
            act.dma_start(w_gates[:], d["w_gates"]).then_inc(ru["con"], 16)

        def pre_dve(dve):
            dve.wait_ge(rstd_ready, 6)
            for q in range(4):
                dve.tensor_tensor(u[:, 4 * q:4 * q + 4, :], z[:, 4 * q:4 * q + 4, :], wide(rstd[:], 4), ALU.mult)\
                   .then_inc(pre_norm, 1)
                if q:
                    lo_part(dve, q - 1, u[:, 4 * q - 4:4 * q, :], READY0["rnn_in"] + q)
            lo_part(dve, 3, u[:, 12:16, :], READY0["rnn_in"] + 4)

        def gates_act(act):
            act.wait_ge(acc_free, TASK0["rnn_out"] + 2)
            for q in range(4):
                hi_part(act, q, u[:, UX0 + 4 * q:UX0 + 4 * q + 4, :])
            for q in range(2):
                hi_part(act, q, u[:, OD + 4 * q:OD + 4 * q + 4, :], hid[:, FT - HT + 4 * q:FT - HT + 4 * q + 4, :])
            for q in range(8):
                act.activation(u[:, 32 + 4 * q:36 + 4 * q, :], u[:, 32 + 4 * q:36 + 4 * q, :], ACT.Sigmoid)\
                   .then_inc(gates_sig, 1)

        def gates_dve(dve):
            for q in range(4):
                lo_part(dve, q, u[:, UX0 + 4 * q:UX0 + 4 * q + 4, :], READY0["rnn_out"] + q + 1)
            for q in range(2):
                lo_part(dve, q, u[:, OD + 4 * q:OD + 4 * q + 4, :], READY0["dil_out"] + q + 1,
                        hid[:, FT - HT + 4 * q:FT - HT + 4 * q + 4, :])

        def dve_gated(which):
            def after(i, t, task, n):
                dve = nc.vector
                dve.drain()
                dve.wait_ge(chunk_used, n + 1)
                if which == 0:
                    dve.wait_ge(gates_sig, i * 2 + t + 1)
                else:
                    dve.wait_ge(gates_sig, i * 2 + t + 5)
                for f in range(CF):
                    o = read_out(etmp[:, f, :], 4 * t + f)
                o.then_inc(acc_free, 1)
                dve.drain()
                first = utile(32, 8, i)[:, 4 * t:4 * t + 4, :]
                own = utile(48, 8, i)[:, 4 * t:4 * t + 4, :] if which else first
                o = dve.tensor_tensor(own, own, etmp[:], ALU.mult)
                if which:
                    dve.drain()
                    o = dve.tensor_tensor(first, first, own, ALU.add)
                    o.then_inc(merged, 1)
            return after

        def merge_act(act):
            for q in range(4):
                act.wait_ge(merged, q + 1)
                hi_part(act, q, u[:, 32 + 4 * q:36 + 4 * q, :])

        def merge_dve(dve):
            for q in range(4):
                lo_part(dve, q, u[:, 32 + 4 * q:36 + 4 * q, :], READY0["last_out"] + q + 1)

        def dve_last(i, t, task, n):
            nc.vector.wait_ge(chunk_used, n + 1)
            for f in range(CF):
                o = read_out(u[:, bass.ds(i * 8 + t * 4 + f, 1), :].squeeze(1), 4 * t + f)
                if f == CF - 1:
                    o.then_inc(acc_free, 1)

        def final_act(act):
            act.wait_ge(sums_ready, 7)
            act_rstd(6, 1, acc[:, 0, T:2 * T], 1.0 / DM)

        def final_dve(dve):
            dve.wait_ge(rstd_ready, 7)
            for q in range(4):
                uq = u[:, 4 * q:4 * q + 4, :]
                dve.tensor_tensor(uq, uq, wide(rstd[:], 4), ALU.mult)
                dve.drain()
                for m in range(4 * q, 4 * q + 4):
                    o = dve.scalar_tensor_tensor(z[:, m, :], u[:, m, :], pcol("ln_post_g_2", m), z[:, m, :],
                                                 ALU.mult, ALU.add)
                o.then_inc(out_ready, 1)

        FIRST_TILE = {"mix0_in": 0, "attn_in": 0, "rnn_in": 0, "half0": QD, "half1": QD, "gates": 2 * MT}
        LNS = {"mix0_out": (0, "ln1", 0, "up0"), "down0": (1, "ln2", 0, "attn_in"),
               "attn_out": (2, "ln1", 1, "up1"), "down1": (3, "ln2", 1, None)}

        @block.sync
        def _(sp):
            wd = d["weights"]
            for n in range(2):
                sp.dma_start(raw[:, n, :], wd[n]).then_inc(raw_landed[n], 16)
            with sp.Fori(1, NCHUNKS // 2) as i:
                for s in range(2):
                    sp.wait_ge(weights_split, i * 2 + s - 1)
                    sp.dma_start(raw[:, s, :], wd[bass.ds(i * 2 + s, 1)].squeeze(0)).then_inc(raw_landed[s], 16)
            for q in range(4):
                sp.wait_ge(out_ready, q + 1)
                sp.dma_start(d["out"][:, 4 * q:4 * q + 4, :], z[:, 4 * q:4 * q + 4, :]).then_inc(out_stored, 16)
            sp.wait_ge(out_stored, 64)

        @block.gpsimd
        def _(pool):
            for name in on:
                if name in LNS:
                    pool_sums(LNS[name][0], z)
                elif name.startswith("up"):
                    pool_hidden(int(name[2]))
                elif name == "mix0_in":
                    hgrn_pool(pool)
                elif name == "attn_in":
                    attn_pool(pool)
                elif name.startswith("half"):
                    dil_pool(int(name[4]))(pool)
                elif name == "last_out":
                    pool_sums(5, None)
                if name == "down1":
                    pool_sums(4, None)

        @block.scalar
        def _(act):
            act.dma_start(z[:], d["x"]).then_inc(x_landed, 16)
            act.dma_start(par[:], d["par"]).then_inc(par_landed, 16)

            def con(dst, name, n, s):
                dst = dst if len(dst.shape) == 2 else flat(dst)
                act.dma_start(dst, d["con"][:, CON0[name]:CON0[name] + n]).then_inc(s, 16)
            for dst, name, n in ((ident[:], "ident", P), (seg1[:], "seg_start", T), (fwm[:], "fw_mask", 4 * P),
                                 (bwm[:], "bw_mask", 4 * P)):
                con(dst, name, n, con_landed)
            act.dma_start(gm_ws[:], d["gmlp_ws"]).then_inc(con_landed, 16)
            act.dma_start(gm_bias[0:1, :], d["gmlp_bias"]).then_inc(con_landed, 16)
            act.wait_ge(x_landed, 16)
            for q in range(4):
                hi_part(act, q, z[:, 4 * q:4 * q + 4, :])
            cast_chunk(act, 0, 0)
            cast_chunk(act, 1, 1)
            act.wait_ge(par_landed, 16)
            for name in on:
                end = name == STAGES[-1][0]
                if name in LNS:
                    occ, ln, layer, nxt = LNS[name]
                    drive(act, name, cast_chunk, act_squares(occ, z), unroll=end)
                    act_rstd(1 + occ, 0)
                    act_affine(4 * occ, ln + "_g", ln + "_b", nxt, layer * MT)
                    if name == "down0":
                        for dst, cn, n in ((perm1[:], "rope1_perm", P), (cos1[:], "rope1_cos", T),
                                           (sin1[:], "rope1_sin", T)):
                            con(dst, cn, n, at_["con"])
                    if name == "down1":
                        pre_act(act)
                elif name.startswith("up"):
                    drive(act, name, cast_chunk, act_silu(int(name[2])), unroll=end)
                elif name == "last_out":
                    drive(act, name, cast_chunk, act_squares(5, u), unroll=end)
                    final_act(act)
                else:
                    drive(act, name, cast_chunk, None, unroll=end)
                if name == "mix0_in":
                    hgrn_act(act)
                elif name == "attn_in":
                    attn_act(act)
                elif name == "rnn_in":
                    rnn_act(act)
                    act.wait_ge(ru["ps"], MT)
                    for dst, cn, n in ((perm2[:], "rope2_perm", P), (cos2[:], "rope2_cos", T),
                                       (sin2[:], "rope2_sin", T), (mask0[:], "dil_mask0", 3 * P),
                                       (mask1[:], "dil_mask1", 3 * T)):
                        con(dst, cn, n, dl["con"])
                elif name.startswith("half"):
                    dil_act(int(name[4]))(act)
                elif name == "gates":
                    gates_act(act)
                elif name == "dil_out":
                    merge_act(act)

        @block.vector
        def _(dve):
            dve.memset(ones[:], 1.0)
            dve.memset(eps[:, 0:1], LN_EPS)
            dve.memset(eps[:, 1:2], RMS_EPS).then_inc(acc_free, 2)
            for c, s in enumerate((hg["done"], hid_ready, sq_used, dl["out"])):
                dve.memset(eps[:, 2 + c:3 + c], 0.0).then_inc(s, 1)
            for q in range(4):
                lo_part(dve, q, z[:, 4 * q:4 * q + 4, :], q + 1)
            split_chunk(dve, 0, 0)
            split_chunk(dve, 1, 1)
            dve.wait_ge(par_landed, 16)
            tab = lambda r: par[:, PAR0["hgrn_lb_table"] + r * HT:PAR0["hgrn_lb_table"] + (r + 1) * HT]
            row = lambda r: lbs[:, r * HT:(r + 1) * HT]
            dve.tensor_tensor(row(0), tab(0), tab(1), ALU.max)
            dve.drain()
            dve.tensor_tensor(row(0), row(0), tab(2), ALU.max)
            dve.drain()
            for r in range(3):
                o = dve.tensor_tensor(row(r + 1), tab(r), row(0), ALU.subtract)
            o.then_inc(lb_max, 1)
            for name in on:
                end = name == STAGES[-1][0]
                if name in LNS:
                    occ, ln, layer, nxt = LNS[name]
                    drive(dve, name, split_chunk, dve_residual(occ), unroll=end)
                    dve_mean_var(1 + occ, DM)
                    dve_norm(1 + occ, nxt)
                    if name == "down1":
                        pre_dve(dve)
                elif name.startswith("up"):
                    for pad in (gpad, vpad):
                        dve.memset(pad[:, :, 0:1], 0.0)
                        dve.memset(pad[:, :, T + 1:T + 2], 0.0)
                    dve.drain()
                    drive(dve, name, split_chunk, dve_conv(int(name[2])), unroll=end)
                elif name == "rnn_out":
                    drive(dve, name, split_chunk, dve_gated(0), unroll=end)
                elif name == "dil_out":
                    drive(dve, name, split_chunk, dve_gated(1), unroll=end)
                    merge_dve(dve)
                elif name == "last_out":
                    drive(dve, name, split_chunk, dve_last, unroll=end)
                    final_dve(dve)
                else:
                    drive(dve, name, split_chunk, dve_store(FIRST_TILE[name]), unroll=end)
                if name == "mix0_in":
                    dve.wait_ge(lb_exp, 1)
                    dve.tensor_tensor(row(0), row(1), row(2), ALU.add)
                    dve.drain()
                    dve.tensor_tensor(row(0), row(0), row(3), ALU.add)
                    dve.drain()
                    dve.reciprocal(row(0), row(0))
                    dve.drain()
                    dve.tensor_tensor(row(0), row(0), row(1), ALU.mult)
                    dve.drain()
                    dve.tensor_scalar(row(1), row(0), -1.0, 1.0, ALU.mult, ALU.add)
                    dve.wait_ge(con_landed, 96)
                    dve.drain()
                    hgrn_dve(dve)
                elif name == "attn_in":
                    attn_dve(dve)
                elif name == "rnn_in":
                    rnn_dve(dve)
                elif name.startswith("half"):
                    dil_dve(int(name[4]))(dve)
                elif name == "gates":
                    gates_dve(dve)

        @block.tensor
        def _(pe):
            for name in on:
                if name in ("down0", "down1"):
                    multiply(pe, name, hid_moving, hid_from(int(name[4])))
                elif name == "dil_out":
                    multiply(pe, name, lambda k, a, b: hid[:, FT - HT + k, a:b], ready_from(name))
                elif name in ("half0", "half1", "gates"):
                    multiply(pe, name, x_moving)
                else:
                    multiply(pe, name, x_moving, ready_from(name))
                if name in LNS:
                    pe_sums(pe, 1 + LNS[name][0])
                    if name == "down1":
                        pe_sums(pe, 5)
                elif name == "mix0_in":
                    pe.wait_ge(con_landed, 96)
                    hgrn_pe(pe)
                elif name == "attn_in":
                    attn_pe(pe)
                elif name == "rnn_in":
                    rnn_pe(pe)
                elif name.startswith("half"):
                    dil_pe(int(name[4]))(pe)
                elif name == "last_out":
                    pe_sums(pe, 6)


def constants():
    out = np.zeros((P, NCON), np.float32)
    p, t = np.arange(P), np.arange(T)

    def put(name, a):
        a = np.asarray(a, np.float32).reshape(P, -1)
        out[:, CON0[name]:CON0[name] + a.shape[1]] = a

    put("ident", np.eye(P))
    put("seg_start", np.tile((t % SEG != 0), (P, 1)))
    same = p[:, None] // SEG == p[None, :] // SEG
    put("fw_mask", np.tile(same & (p[:, None] <= p[None, :]), (1, 4)))
    put("bw_mask", np.tile(same & (p[:, None] >= p[None, :]), (1, 4)))

    def rope(tag, partner, sign, ang, turned):
        perm = np.zeros((P, P))
        perm[partner[turned], p[turned]] = sign[turned]
        put(tag + "_perm", perm)
        put(tag + "_cos", np.where(turned[:, None], np.cos(ang), 1.0))
        put(tag + "_sin", np.where(turned[:, None], np.sin(ang), 0.0))

    half, n2 = P // 2, P // 4
    inv = np.exp(np.float32(-math.log(10000.0)) * np.arange(0, half, 2, dtype=np.float32) / half).astype(np.float32)
    pos = np.where((p < half)[:, None], (t // 64)[None, :], (t % 64)[None, :]).astype(np.float32)
    first = p % half < n2
    rope("rope1", np.where(first, p + n2, p - n2), np.where(first, -1.0, 1.0),
         pos * inv[p % n2][:, None], np.ones(P, bool))
    rot = P // 4
    inv = np.exp(np.float32(-math.log(500000.0)) * np.arange(rot // 2, dtype=np.float32) * np.float32(2.0 / rot))
    inv = inv.astype(np.float32)
    first = p < rot // 2
    rope("rope2", np.where(first, p + rot // 2, p - rot // 2), np.where(first, -1.0, 1.0),
         t[None, :].astype(np.float32) * inv[p % (rot // 2)][:, None], p < rot)

    def mask(queries, keys):
        gap = queries[:, None] - keys[None, :]
        return [np.where((gap >= 0) & (gap <= w) & (gap % dil == 0), 0.0, -1e30) for w, dil in WINDOWS]
    put("dil_mask0", np.concatenate(mask(p, p), 1))
    put("dil_mask1", np.concatenate(mask(p + P, t), 1))
    return out


def tasks(w, cols=None):
    k, n = w.shape
    a = w.reshape(k // (CK * P), CK, P, n // (CF * P), CF, P).transpose(3, 0, 2, 4, 1, 5)
    return a if cols is None else a[cols]


def kernel(**inputs):
    import concourse.bacc as bacc
    from concourse.bass_utils import run_bass_kernel_spmd

    a = {k: np.asarray(v) for k, v in inputs.items()}
    pairs = [i for g in range(FG) for i in (g, FG + g)]
    win2 = tasks(a["w_in_2"][0])

    def half(h):
        return [first + 2 * g + h for first in (8, 14, 20) for g in range(3)] + [26 + h]
    parts = [tasks(a["w_in_ab"][0]), tasks(a["w_out_ab"][0]), tasks(a["ffn_up"][0], pairs), tasks(a["ffn_down"][0]),
             tasks(a["w_in_attn"][0]), tasks(a["w_out_attn"][0]), tasks(a["ffn_up"][1], pairs),
             tasks(a["ffn_down"][1]), win2[0:8], win2[half(0)], win2[half(1)], win2[28:36],
             tasks(a["w_rnn_out_2"][0]), tasks(a["w_attn_out_2"][0]), tasks(a["w_o_2"][0])]
    weights = np.concatenate([x.reshape(-1, P, CHUNK) for x in parts])
    assert weights.shape[0] == NCHUNKS

    def by_feature(x):
        return np.ascontiguousarray(x.reshape(T, MT, P).transpose(2, 1, 0))
    a["qk_norm_g"] = np.concatenate([a["q_norm_g"]] * 8 + [a["k_norm_g"]] * 2)
    par = np.concatenate([a[name].reshape(-1, P) for name, _ in PARS])
    assert par.shape[0] == NPAR
    arrays = {
        "x": by_feature(a["x"][0]),
        "weights": weights,
        "par": np.ascontiguousarray(par.T),
        "con": constants(),
        "gmlp_ws": np.ascontiguousarray(a["gmlp_ws"][0].transpose(2, 0, 1)),
        "gmlp_bias": np.ascontiguousarray(a["gmlp_bias"].reshape(1, HT * P)),
        "w_gates": np.ascontiguousarray(np.stack([a["w_rg_2"][0], a["w_ig_2"][0]]).transpose(2, 0, 1, 3)),
    }
    nc = bacc.Bacc("TRN2", target_bir_lowering=False, num_devices=1)
    d = {k: nc.dram_tensor(k + "_dram", v.shape, F32, kind="ExternalInput").ap() for k, v in arrays.items()}
    d["out"] = nc.dram_tensor("out_dram", (P, MT, T), F32, kind="ExternalOutput").ap()
    program(nc, d)
    r = run_bass_kernel_spmd(nc, [{k + "_dram": v for k, v in arrays.items()}], core_ids=[0])
    out = r.results[0]["out_dram"]
    return np.ascontiguousarray(out.transpose(2, 1, 0)).reshape(1, T, DM)
```

```python
import math
from contextlib import ExitStack

import numpy as np

import concourse.bass as bass
from concourse import mybir
from concourse.alu_op_type import AluOpType as ALU

F32 = mybir.dt.float32
F32R = mybir.dt.float32r
I32 = mybir.dt.int32
ACT = mybir.ActivationFunctionType
AX = mybir.AxisListType.X

P = 128
T = 256
DM = 2048
MT = DM // P
FF = 5632
FT = FF // P
FG = FT // 4
HT = 1024 // P
CK, CF = 4, 4
CHUNK = CK * CF * P
ALPHA = (2.0 * 2) ** 0.25
LN_EPS, RMS_EPS = 1e-5, 1e-6
SEG = 64
NSEG = T // SEG
LRU_C = 8.0
WINDOWS = ((128, 1), (512, 4), (2048, 16))

STAGES = [("mix0_in", 14, 4), ("mix0_out", 4, 4),
          ("up0", 2 * FG, 4), ("down0", 4, FT // CK),
          ("attn_in", 6, 4), ("attn_out", 4, 4),
          ("up1", 2 * FG, 4), ("down1", 4, FT // CK),
          ("rnn_in", 8, 4), ("half0", 10, 4), ("half1", 10, 4), ("gates", 8, 4),
          ("rnn_out", 4, 4), ("dil_out", 4, 2), ("last_out", 4, 4)]
TASK0, CHUNK0, NTASK, NCHUNK_OF = {}, {}, {}, {}
_t = _c = 0
for _name, _n, _k in STAGES:
    TASK0[_name], CHUNK0[_name], NTASK[_name], NCHUNK_OF[_name] = _t, _c, _n, _k
    _t += _n
    _c += _n * _k
NCHUNKS = _c

_READY = ["mix0_in", "mix0_out", "up0", "attn_in", "attn_out", "up1", "rnn_in", "rnn_out"]
READY0 = {n: 4 * i for i, n in enumerate(_READY)}
READY0["dil_out"] = 4 * len(_READY)
READY0["last_out"] = READY0["dil_out"] + 2

PARS = [("hgrn_lb_table", 3 * HT), ("hgrn_norm_g", HT), ("gmlp_ln_g", HT), ("gmlp_ln_b", HT),
        ("qk_norm_g", (16 + 4) // 2),
        ("ln1_g", 2 * MT), ("ln1_b", 2 * MT), ("ln2_g", 2 * MT), ("ln2_b", 2 * MT),
        ("ffn_conv_w", 2 * 3 * 2 * FT), ("ffn_conv_b", 2 * 2 * FT),
        ("ln_pre_g_2", MT), ("conv_w_2", 4 * MT), ("conv_b_2", MT), ("b_rg_2", MT), ("b_ig_2", MT),
        ("lru_lambda_2", MT), ("ln_post_g_2", MT)]
PAR0, _c = {}, 0
for _name, _n in PARS:
    PAR0[_name] = _c
    _c += _n
NPAR = _c

CONS = [("ident", P), ("seg_start", T), ("fw_mask", 4 * P), ("bw_mask", 4 * P),
        ("rope1_perm", P), ("rope1_cos", T), ("rope1_sin", T),
        ("rope2_perm", P), ("rope2_cos", T), ("rope2_sin", T),
        ("dil_mask0", 3 * P), ("dil_mask1", 3 * T)]
CON0, _c = {}, 0
for _name, _n in CONS:
    CON0[_name] = _c
    _c += _n
NCON = _c


def program(nc, d):
    ctx = ExitStack()
    with ctx:
        base = (nc.sbuf_base + 63) // 64 * 64
        at = [base]

        def place(name, shape, dt=F32, offset=None):
            size = 4 * int(np.prod(shape[1:]))
            if offset is None:
                offset = at[0]
                at[0] += (size + 31) // 32 * 32
            return nc.alloc_sbuf_tensor_at(name, shape, dt, offset=offset)

        raw = place("w_raw", [P, 2, CHUNK])
        whi = place("w_hi", [P, 2, CHUNK], F32R)
        wlo = place("w_lo", [P, 2, CHUNK], F32R)
        X0 = at[0]
        xhl = place("x_hi_lo", [P, MT, 2 * T], F32R)
        z = place("resid", [P, MT, T])
        U0 = at[0]
        hid = place("hidden_hi_lo", [P, FT, 2 * T], F32R)
        u = place("u_tiles", [P, 2 * FT, T], F32, U0)
        W0 = at[0]
        WSIZE = 4 * 4 * (T + 2) * 2 + 2 * 4 * 4 * T
        at[0] += WSIZE
        par = place("par", [P, NPAR])
        ident = place("ident", [P, P])
        ones = place("ones", [P, P])
        eps = place("eps", [P, 8])
        lbs = place("lower_bound", [P, 4 * HT])
        nrg = place("rnn_cols", [P, 4 * MT])
        sbuf_end = at[0]
        assert sbuf_end <= nc.sbuf_usable_end, (sbuf_end, nc.sbuf_usable_end)
        fence = ctx.enter_context(nc.sbuf_tensor("fence", [P, (sbuf_end - nc.sbuf_base + 3) // 4], F32))

        names = [0]

        def over(start, pieces):
            out, o = [], start
            for shape in pieces:
                names[0] += 1
                out.append(place(f"over{names[0]}", shape, F32, o))
                o += (4 * int(np.prod(shape[1:])) + 31) // 32 * 32
            return out, o

        acc = ctx.enter_context(nc.psum_tensor("acc", [P, 8, 2 * T], F32))

        (gpad, vpad, gconv, vconv), end = over(W0, [[P, 4, T + 2], [P, 4, T + 2], [P, 4, T], [P, 4, T]])
        assert end <= W0 + WSIZE
        (zsum, mu, var, rstd, etmp, esq), end = over(
            W0, [[P, 2 * T], [P, T], [P, T], [P, T], [P, 4, T], [P, 4, T]])
        assert end <= W0 + WSIZE

        def sem(name):
            return ctx.enter_context(nc.semaphore(name))

        raw_landed = [sem("raw_landed0"), sem("raw_landed1")]
        weights_hi = sem("weights_hi")
        weights_split = sem("weights_split")
        chunk_used = sem("chunk_used")
        acc_free = sem("acc_free")
        moving_ready = sem("moving_ready")
        x_landed = sem("x_landed")
        par_landed = sem("par_landed")
        con_landed = sem("con_landed")
        consts_ready = sem("consts_ready")
        lb_exp = sem("lb_exp")
        lb_max = sem("lb_max")
        x_hi = sem("x_hi")
        z_ready = sem("z_ready")
        sq_ready = sem("sq_ready")
        sq_used = sem("sq_used")
        partials = sem("partials")
        sums_ready = sem("sums_ready")
        var_ready = sem("var_ready")
        rstd_ready = sem("rstd_ready")
        norm_ready = sem("norm_ready")
        out_ready = sem("out_ready")
        out_stored = sem("out_stored")

        block = ctx.enter_context(nc.Block())

        on = [name for name, _, _ in STAGES]

        def col(name, i=0, n=1):
            return par[:, bass.ds(PAR0[name] + i, n)]

        def loop(eng, trips, unroll=False):
            if trips == 1 or unroll:
                yield from range(trips)
            else:
                with eng.Fori(0, trips) as i:
                    yield i

        def cast_chunk(act, n, slot):
            act.wait_ge(raw_landed[slot], 16 * (n // 2 + 1) if isinstance(n, int) else n * 8 + (16 - 8 * slot))
            if not isinstance(n, int) or n >= 2:
                act.wait_ge(chunk_used, n - 1)
            nc.scalar.activation(whi[:, slot, :], raw[:, slot, :], ACT.Copy).then_inc(weights_hi, 1)

        def split_chunk(dve, n, slot):
            dve.wait_ge(weights_hi, n + 1)
            nc.vector.tensor_tensor(wlo[:, slot, :], raw[:, slot, :], whi[:, slot, :].bitcast(F32),
                                    ALU.subtract).then_inc(weights_split, 1)

        def drive(eng, name, piece, after_task, unroll=False, between=None, peel=()):
            per, nch = 2, NCHUNK_OF[name]

            for i in spans(eng, name, peel, unroll):
                for t in range(per):
                    for c in range(1, nch):
                        at_c = t * nch + c
                        n = CHUNK0[name] + i * (per * nch) + at_c
                        if not isinstance(n, int) or n + 1 < NCHUNKS:
                            piece(eng, n + 1, (at_c + 1) % 2)
                        if between:
                            between(i, t, c)
                        if c == nch - 1:
                            if not isinstance(n, int) or n + 2 < NCHUNKS:
                                piece(eng, n + 2, at_c % 2)
                            if after_task:
                                after_task(i, t, TASK0[name] + i * per + t, n)

        def spans(eng, name, cuts, unroll=False):
            cuts = [0, *cuts, NTASK[name] // 2]
            for lo, hi in zip(cuts, cuts[1:]):
                if unroll or hi - lo == 1:
                    yield from range(lo, hi)
                else:
                    with eng.Fori(lo, hi) as i:
                        yield i

        def multiply(pe, name, moving, ready=None, cuts=(), extra=None, banks_read=None):
            per, nch = 2, NCHUNK_OF[name]
            for i in spans(pe, name, cuts):
                for t in range(per):
                    pe.wait_ge(acc_free, TASK0[name] + i * per + t + 1)
                    if banks_read:
                        banks_read(i, t)
                    for c in range(nch):
                        at_c = t * nch + c
                        s = at_c % 2
                        if extra:
                            extra(i, t, c)
                        if t == 0 and ready:
                            ready(pe, c)
                        pe.wait_ge(weights_split, CHUNK0[name] + i * (per * nch) + at_c + 1)
                        for f in range(CF):
                            bank = 4 * t + f
                            for kk in range(CK):
                                k = CK * c + kk
                                w0 = (f * CK + kk) * P
                                both = (acc[:, bank, :], whi[:, s, w0:w0 + P], moving(k, 0, 2 * T))
                                rest = (acc[:, bank, 0:T], wlo[:, s, w0:w0 + P], moving(k, 0, T))
                                if k == 0:
                                    nc.tensor.matmul(*both, start=True, stop=False)
                                    last = nc.tensor.matmul(*rest, start=False, stop=False)
                                else:
                                    nc.tensor.matmul(*rest, start=False, stop=False)
                                    last = nc.tensor.matmul(*both, start=False,
                                                            stop=(k == CK * nch - 1))
                        last.then_inc(chunk_used, 1)

        def x_moving(k, a, b):
            return xhl[:, k, a:b]

        def hid_moving(k, a, b):
            return hid[:, k, a:b]

        def ready_from(name):
            def ready(pe, c):
                pe.wait_ge(moving_ready, READY0[name] + c + 1)
            return ready

        def halves(bank):
            return acc[:, bank, :].rearrange("p (h n) -> p n h", h=2)

        def read_out(dst, bank):
            return nc.vector.tensor_reduce(dst, halves(bank), AX, ALU.add)

        def dve_store(first_tile):
            def after(i, t, task, n):
                nc.vector.wait_ge(chunk_used, n + 1)
                for f in range(CF):
                    o = read_out(u[:, bass.ds(first_tile + i * 8 + t * 4 + f, 1), :].squeeze(1), 4 * t + f)
                o.then_inc(acc_free, 1)
            return after

        def dve_residual():
            def after(i, t, task, n):
                nc.vector.wait_ge(chunk_used, n + 1)
                for f in range(CF):
                    o = read_out(etmp[:, f, :], 4 * t + f)
                o.then_inc(acc_free, 1)
            return after

        def dve_add(m):
            zt = z[:, 4 * m:4 * m + 4, :]
            nc.vector.drain()
            nc.vector.scalar_tensor_tensor(zt, zt, ALPHA, etmp[:], ALU.mult, ALU.add).then_inc(z_ready, 1)

        def dve_between(i, t, c):
            if c == 1 and i + t:
                dve_add(2 * i + t - 1)

        def act_square(occ, m, src):
            n = 4 * occ + m
            if occ < 4:
                nc.scalar.wait_ge(z_ready, n + 1)
            else:
                nc.scalar.wait_ge(acc_free, TASK0["last_out"] + m + 3)
            nc.scalar.wait_ge(sq_used, n + 1)
            nc.scalar.activation(esq[:], src[:, 4 * m:4 * m + 4, :], ACT.Square).then_inc(sq_ready, 1)

        def act_between(occ, src):
            def between(i, t, c):
                if c == 2 and i + t:
                    act_square(occ, 2 * i + t - 1, src)
            return between

        def pool_sums(occ, src):
            pool = nc.gpsimd
            if occ == 4:
                pool.wait_ge(sums_ready, 5)
            elif occ == 5:
                pool.wait_ge(acc_free, TASK0["last_out"] + 3)
            else:
                pool.wait_ge(z_ready, 4 * occ + 1)
            pool.memset(zsum[:], 0.0)
            pool.drain()
            for i in loop(pool, 2):
                for t in range(2):
                    pool.wait_ge(sq_ready, 4 * occ + i * 2 + t + 1)
                    for f in range(4):
                        if src is not None:
                            pool.tensor_tensor(zsum[:, 0:T], zsum[:, 0:T],
                                               src[:, bass.ds(i * 8 + t * 4 + f, 1), :].squeeze(1), ALU.add)
                        pool.tensor_tensor(zsum[:, T:2 * T], zsum[:, T:2 * T], esq[:, f, :], ALU.add)
                        pool.drain()
                    pool.engine_nop().then_inc(sq_used, 1)
            pool.engine_nop().then_inc(partials, 1)

        def pe_sums(pe, s):
            pe.wait_ge(partials, s + 1)
            nc.tensor.matmul(acc[:, 0, :], ones[:], zsum[:], start=True, stop=True).then_inc(sums_ready, 1)

        def dve_mean_var(s, width):
            dve = nc.vector
            dve.wait_ge(sums_ready, s + 1)
            dve.tensor_scalar(mu[:], acc[:, 0, 0:T], 1.0 / width, None, ALU.mult)
            dve.drain()
            dve.tensor_tensor(rstd[:], mu[:], mu[:], ALU.mult)
            dve.drain()
            dve.scalar_tensor_tensor(var[:], acc[:, 0, T:2 * T], 1.0 / width, rstd[:], ALU.mult, ALU.subtract)
            dve.drain()
            dve.tensor_scalar(var[:], var[:], 0.0, None, ALU.max).then_inc(var_ready, 1)

        def act_rstd(v, e, src=None, scale=1.0):
            act = nc.scalar
            if src is None:
                act.wait_ge(var_ready, v + 1)
                src = var[:]
            act.activation(var[:], src, ACT.Ln, bias=eps[:, e:e + 1], scale=scale)
            act.drain()
            act.activation(rstd[:], var[:], ACT.Exp, scale=-0.5).then_inc(rstd_ready, 1)

        def wide(t2, n):
            return t2.unsqueeze(1).to_broadcast([P, n, T])

        def lo_part(dve, q, src, count, dst=None):
            dst = xhl[:, 4 * q:4 * q + 4, :] if dst is None else dst
            dve.wait_ge(x_hi, count)
            nc.vector.tensor_tensor(dst[:, :, T:2 * T], src, dst[:, :, 0:T].bitcast(F32), ALU.subtract)\
                .then_inc(moving_ready, 1)

        def hi_part(act, q, src, dst=None):
            dst = xhl[:, 4 * q:4 * q + 4, :] if dst is None else dst
            nc.scalar.activation(dst[:, :, 0:T], src, ACT.Copy).then_inc(x_hi, 1)

        def dve_norm(r, nxt):
            dve = nc.vector
            dve.wait_ge(rstd_ready, r + 1)
            for q in range(4):
                zq = z[:, 4 * q:4 * q + 4, :]
                dve.tensor_tensor(zq, zq, wide(mu[:], 4), ALU.subtract)
                dve.drain()
                dve.tensor_tensor(zq, zq, wide(rstd[:], 4), ALU.mult).then_inc(norm_ready, 1)
                if nxt and q:
                    lo_part(dve, q - 1, z[:, 4 * q - 4:4 * q, :], READY0[nxt] + q)
            if nxt:
                lo_part(dve, 3, z[:, 12:16, :], READY0[nxt] + 4)

        def act_affine(q0, g, b, nxt, off):
            act = nc.scalar
            for q in range(4):
                zq = z[:, 4 * q:4 * q + 4, :]
                act.wait_ge(norm_ready, q0 + q + 1)
                for m in range(4 * q, 4 * q + 4):
                    act.activation(z[:, m, :], z[:, m, :], ACT.Identity,
                                   bias=col(b, off + m), scale=col(g, off + m))
                act.drain()
                if nxt:
                    hi_part(act, q, zq)
                else:
                    m = 16 + q
                    act.wait_ge(sq_used, m + 1)
                    act.activation(esq[:], zq, ACT.Square).then_inc(sq_ready, 1)

        gate_conv = sem("gate_conv")
        val_conv = sem("val_conv")
        gate_silu = sem("gate_silu")
        hid_ready = sem("hid_ready")

        def conv(layer, pad, out, i, val, tiles):
            dve = nc.vector
            w0 = PAR0["ffn_conv_w"] + layer * 3 * 2 * FT + val * FT
            b0 = PAR0["ffn_conv_b"] + layer * 2 * FT + val * FT

            def c(first, f):
                return par[:, bass.ds(first + i * 4 + f, 1)]
            for f in tiles:
                dve.tensor_scalar(out[:, f, :], pad[:, f, 1:T + 1], c(w0 + 2 * FT, f), c(b0, f),
                                  ALU.mult, ALU.add)
            for j in (0, 2):
                dve.drain()
                for f in tiles:
                    o = dve.scalar_tensor_tensor(out[:, f, :], pad[:, f, j:j + T], c(w0 + j * 2 * FT, f),
                                                 out[:, f, :], ALU.mult, ALU.add)
            return o

        def dve_pad(i, t, task, n):
            nc.vector.wait_ge(chunk_used, n + 1)
            for f in range(CF):
                o = read_out((vpad if t else gpad)[:, f, 1:T + 1], 4 * t + f)
            o.then_inc(acc_free, 1)

        def dve_conv(layer):
            def between(i, t, c):
                if c > 2:
                    return
                tiles = range(2 * c - 2, 2 * c)
                if t == 1:
                    if c == 1:
                        nc.vector.drain()
                        nc.vector.wait_ge(hid_ready, layer * FG + i + 1)
                    o = conv(layer, gpad, gconv, i, 0, tiles)
                    if c == 2:
                        o.then_inc(gate_conv, 1)
                elif not isinstance(i, int) or i > 0:
                    value(i - 1, c, tiles)

            def value(i, c, tiles):
                if c == 1:
                    nc.vector.drain()
                o = conv(layer, vpad, vconv, i, 1, tiles)
                if c == 2:
                    o.then_inc(val_conv, 1)
            return between, value

        def act_silu(layer):
            def after(i, t, task, n):
                if t == 1:
                    nc.scalar.wait_ge(gate_conv, layer * FG + i + 1)
                    nc.scalar.activation(gconv[:], gconv[:], ACT.Silu).then_inc(gate_silu, 1)
            return after

        def pool_hidden(layer):
            pool = nc.gpsimd
            for i in loop(pool, FG):
                pool.wait_ge(gate_silu, layer * FG + i + 1)
                pool.wait_ge(val_conv, layer * FG + i + 1)
                pool.tensor_tensor(vconv[:], vconv[:], gconv[:], ALU.mult)
                pool.drain()
                pool.tensor_copy(hid[:, bass.ds(i * 4, 4), 0:T], vconv[:])
                pool.drain()
                pool.tensor_tensor(hid[:, bass.ds(i * 4, 4), T:2 * T], vconv[:],
                                   hid[:, bass.ds(i * 4, 4), 0:T].bitcast(F32), ALU.subtract)\
                    .then_inc(hid_ready, 1)

        def hid_from(layer):
            def ready(pe, c):
                pe.wait_ge(hid_ready, layer * FG + c + 2)
            return ready

        F0, V0, I0, UU0, Q0, G0, K0, L0 = 0, 2 * HT, 3 * HT, 4 * HT, 5 * HT, 6 * HT, 7 * HT, 9 * HT
        VT0, IT0, QT0, GT0 = V0 // 4, I0 // 4, Q0 // 4, G0 // 4
        (qmid, prob, state, decay, bwm), end = over(
            X0, [[P, 2, 4, T], [P, 2, 8, P], [P, 2, 4 * 3, P], [P, 2 * HT, NSEG], [P, 4, P]])
        assert end <= X0 + 4 * MT * 2 * T
        osq = u[:, V0:V0 + HT, :]
        (_, seg1, fwm), end = over(W0, [[P, 2 * T + 3 * T + 8 * T], [P, T], [P, 4, P]])
        assert end <= W0 + WSIZE
        (_, gm_bias, gm_ws), _ = over(W0, [[P, 2 * T + 3 * T], [P, HT * P], [P, HT, P]])

        hg = {n: sem("hg_" + n) for n in (
            "sig", "gate", "key", "log", "diff", "exp", "klast", "kmid", "ktok_ps", "ktok", "vtok_ps", "vtok",
            "silu", "masks", "qdiff", "qexp", "qmid", "cumexp", "qcum", "kv_ps", "state", "score_ps", "prob",
            "out_ps", "out", "sq", "ms_ps", "rn", "done")}
        gm = {n: sem("gm_" + n) for n in ("sq", "summed", "norm", "affine", "tok_ps", "tok", "con", "out_ps", "done")}

        def pcol(name, off=0):
            return par[:, PAR0[name] + off:PAR0[name] + off + 1]

        def flat(x):
            return x.rearrange("p a n -> p (a n)")

        def utile(first, n, i):
            return u[:, bass.ds(i * n + first, n), :]

        def tiles(first, n=4):
            return u[:, first:first + n, :]

        def segs(t3):
            return t3.rearrange("p a (s c) -> p (a s) c", c=SEG)

        def seg_point(t3, point):
            n = t3.shape[1] * NSEG
            return segs(t3)[:, :, point:point + 1].to_broadcast([P, n, SEG])

        POINTS = ((SEG // 2 - 1, SEG - 1), (SEG // 2, 0))

        def hgrn_in_act(i, t, c):
            act, task, b0 = nc.scalar, 2 * i + t, 4 * (1 - t)
            j = task - 1
            if c == 1 and task == 0:
                act.wait_ge(lb_max, 1)
                act.activation(lbs[:, HT:4 * HT], lbs[:, HT:4 * HT], ACT.Exp).then_inc(lb_exp, 1)
            if c == 1 and 0 <= j < 4:
                act.wait_ge(acc_free, j + 3)
                act.activation(tiles(F0 + 4 * j), tiles(F0 + 4 * j), ACT.Sigmoid).then_inc(hg["sig"], 1)
            if c == 1 and VT0 <= j < VT0 + 2:
                act.wait_ge(acc_free, j + 3)
                if j > VT0:
                    act.wait_ge(gm["summed"], 1)
                act.activation(esq[:], tiles(4 * j), ACT.Square).then_inc(gm["sq"], 1)
            if c == 2 and 0 <= task - 3 < 4:
                k = task - 3
                act.wait_ge(hg["ktok_ps"], k + 1)
                for b in range(2):
                    o = act.activation(flat(tiles(L0 + 4 * k + 2 * b, 2)), acc[:, b0 + b, :], ACT.Copy)
                o.then_inc(hg["ktok"], 1)
            if c == 3 and 0 <= j < 4:
                act.wait_ge(hg["key"], j + 1)
                act.activation(tiles(F0 + 4 * j), tiles(F0 + 4 * j), ACT.Ln).then_inc(hg["log"], 1)
            if c == 3 and 0 <= task - 2 < 4:
                k = task - 2
                act.wait_ge(hg["diff"], k + 1)
                act.activation(tiles(L0 + 4 * k), tiles(L0 + 4 * k), ACT.Exp)
                act.activation(etmp[:], etmp[:], ACT.Exp).then_inc(hg["exp"], 1)
            if c == 3 and IT0 <= j < IT0 + 2:
                act.wait_ge(hg["vtok_ps"], j - IT0 + 1)
                for b in range(2):
                    o = act.activation(flat(tiles(4 * j + 2 * b, 2)), acc[:, b0 + 2 + b, :], ACT.Copy)
                o.then_inc(hg["vtok"], 1)
            if c == 3 and task == 7:
                act_rstd(0, 0)
            if c == 1 and task == 8:
                act.wait_ge(partials, 1)
                act.wait_ge(hg["kmid"], 4)
                act.dma_start(gm_ws[:], d["gmlp_ws"]).then_inc(gm["con"], 16)
                act.dma_start(gm_bias[0:1, :], d["gmlp_bias"]).then_inc(gm["con"], 16)
            if c == 3 and task == 8:
                act.wait_ge(gm["norm"], 1)
                for m in range(HT):
                    o = act.activation(u[:, V0 + m, :], u[:, V0 + m, :], ACT.Identity,
                                       bias=pcol("gmlp_ln_b", m), scale=pcol("gmlp_ln_g", m))
                o.then_inc(gm["affine"], 1)
            if c == 3 and task == 9:
                act.wait_ge(gm["tok_ps"], 1)
                for b in range(4):
                    o = act.activation(flat(tiles(V0 + 2 * b, 2)), acc[:, b0 + b, :], ACT.Copy)
                o.then_inc(gm["tok"], 1)
            if c == 1 and GT0 <= j < GT0 + 2:
                act.wait_ge(acc_free, j + 3)
                act.activation(tiles(4 * j), tiles(4 * j), ACT.Silu).then_inc(hg["silu"], 1)

        def hgrn_in_dve(i, t, c):
            dve, task, b0 = nc.vector, 2 * i + t, 4 * (1 - t)
            j, k = task - 1, task - 2
            if c == 1 and task == 1:
                row = lambda r: lbs[:, r * HT:(r + 1) * HT]
                dve.wait_ge(lb_exp, 1)
                dve.tensor_tensor(row(0), row(1), row(2), ALU.add)
                dve.drain()
                dve.tensor_tensor(row(0), row(0), row(3), ALU.add)
                dve.drain()
                dve.reciprocal(row(0), row(0))
                dve.drain()
                dve.tensor_tensor(row(0), row(0), row(1), ALU.mult)
                dve.drain()
                dve.tensor_scalar(row(1), row(0), -1.0, 1.0, ALU.mult, ALU.add)
                dve.drain()
            if c == 1 and 0 <= k < 4:
                way = slice(None) if k < 2 else slice(None, None, -1)
                dve.wait_ge(hg["log"], k + 1)
                for m in range(4 * k, 4 * k + 4):
                    dve.tensor_tensor_scan(u[:, F0 + m, way], seg1[:], u[:, F0 + m, way], 0.0, ALU.mult, ALU.add)
                dve.drain()
                f = tiles(F0 + 4 * k)
                dve.tensor_tensor(segs(tiles(L0 + 4 * k)), seg_point(f, POINTS[k // 2][1]), segs(f), ALU.subtract)
            if c == 2 and 0 <= j < 4:
                dve.wait_ge(hg["sig"], j + 1)
                for m in range(4 * j, 4 * j + 4):
                    h = m % HT
                    o = dve.tensor_scalar(u[:, F0 + m, :], u[:, F0 + m, :], lbs[:, HT + h:HT + h + 1],
                                          lbs[:, h:h + 1], ALU.mult, ALU.add)
                o.then_inc(hg["gate"], 1)
            if c == 2 and 0 <= k < 4:
                if k:
                    dve.wait_ge(hg["kmid"], k)
                f = tiles(F0 + 4 * k)
                dve.tensor_tensor(segs(etmp[:]), seg_point(f, POINTS[k // 2][0]), segs(f), ALU.subtract)\
                   .then_inc(hg["diff"], 1)
            if c == 3 and task == 7:
                dve_mean_var(0, HT * P)
            if c == 1 and task == 8:
                dve.drain()
                dve.tensor_tensor(tiles(V0, HT), tiles(V0, HT), wide(mu[:], HT), ALU.subtract)
            if c == 2 and task == 8:
                dve.drain()
                dve.wait_ge(rstd_ready, 1)
                dve.tensor_tensor(tiles(V0, HT), tiles(V0, HT), wide(rstd[:], HT), ALU.mult).then_inc(gm["norm"], 1)
            if c == 3 and task == 11:
                dve.wait_ge(gm["out_ps"], 1)
                for b in range(4):
                    o = dve.tensor_tensor(flat(tiles(UU0 + 2 * b, 2)), flat(tiles(UU0 + 2 * b, 2)),
                                          acc[:, b0 + b, :], ALU.mult)
                o.then_inc(gm["done"], 1)

        def hgrn_in_pool(pool):
            pool.memset(zsum[:], 0.0)
            for task in range(1, VT0 + 3):
                j, k = task - 1, task - 2
                if j < 4:
                    pool.wait_ge(hg["gate"], j + 1)
                    pool.tensor_scalar(tiles(K0 + 4 * j), tiles(F0 + 4 * j), -1.0, 1.0, ALU.mult, ALU.add)\
                        .then_inc(hg["key"], 1)
                if 0 <= k < 4:
                    pool.drain()
                    pool.wait_ge(hg["exp"], k + 1)
                    pool.tensor_tensor(tiles(L0 + 4 * k), tiles(L0 + 4 * k), tiles(K0 + 4 * k), ALU.mult)\
                        .then_inc(hg["klast"], 1)
                    pool.drain()
                    pool.tensor_tensor(tiles(K0 + 4 * k), tiles(K0 + 4 * k), etmp[:], ALU.mult)\
                        .then_inc(hg["kmid"], 1)
                if VT0 <= j < VT0 + 2:
                    pool.drain()
                    pool.wait_ge(gm["sq"], j - VT0 + 1)
                    for f in range(4):
                        pool.tensor_tensor(zsum[:, 0:T], zsum[:, 0:T], u[:, 4 * j + f, :], ALU.add)
                        pool.tensor_tensor(zsum[:, T:2 * T], zsum[:, T:2 * T], esq[:, f, :], ALU.add)
                        pool.drain()
                    pool.engine_nop().then_inc(gm["summed"], 1)
            pool.engine_nop().then_inc(partials, 1)

        def hgrn_in_pe(i, t, c):
            pe, task, b0 = nc.tensor, 2 * i + t, 4 * (1 - t)
            if c != 2:
                return
            j, k = task - 1, task - 3
            if 0 <= k < 4 or task == 7 or task == 9 or task == 11 or IT0 <= j < IT0 + 2:
                pe.wait_ge(acc_free, task + 2)
            if 0 <= k < 4:
                if k == 0:
                    pe.wait_ge(con_landed, 48)
                pe.wait_ge(hg["klast"], k + 1)
                for f in range(4):
                    for b in range(2):
                        x = 2 * f + b
                        o = pe.transpose(acc[:, b0 + x // 4, (x % 4) * P:(x % 4 + 1) * P],
                                         u[:, L0 + 4 * k + f, b * P:(b + 1) * P], ident[:])
                o.then_inc(hg["ktok_ps"], 1)
            if task == 7:
                pe_sums(pe, 0)
            if IT0 <= j < IT0 + 2:
                for f in range(4):
                    for b in range(2):
                        x = 2 * f + b
                        o = pe.transpose(acc[:, b0 + 2 + x // 4, (x % 4) * P:(x % 4 + 1) * P],
                                         u[:, 4 * j + f, b * P:(b + 1) * P], ident[:])
                o.then_inc(hg["vtok_ps"], 1)
            if task == 9:
                pe.wait_ge(gm["affine"], 1)
                for x in range(2 * HT):
                    o = pe.transpose(acc[:, b0 + x // 4, (x % 4) * P:(x % 4 + 1) * P],
                                     u[:, V0 + x // 2, (x % 2) * P:(x % 2 + 1) * P], ident[:])
                o.then_inc(gm["tok_ps"], 1)
            if task == 11:
                pe.wait_ge(gm["con"], 32)
                for m in range(HT):
                    for n in range(2):
                        dst = acc[:, b0 + m // 2, (m % 2) * T + n * P:(m % 2) * T + (n + 1) * P]
                        pe.matmul(dst, ones[0:1, :], gm_bias[0:1, m * P:(m + 1) * P], start=True, stop=False)
                        o = pe.matmul(dst, u[:, V0 + m, n * P:(n + 1) * P], gm_ws[:, m, :], start=False, stop=True)
                o.then_inc(gm["out_ps"], 1)

        def hgrn_in_read(i, t):
            pe, task = nc.tensor, 2 * i + t
            if 0 <= task - 4 < 4:
                pe.wait_ge(hg["ktok"], task - 3)
            if IT0 <= task - 2 < IT0 + 2:
                pe.wait_ge(hg["vtok"], task - 1 - IT0)
            if task == 8:
                pe.wait_ge(var_ready, 1)
            if task == 10:
                pe.wait_ge(gm["tok"], 1)
            if task == 12:
                pe.wait_ge(gm["done"], 1)

        NG = HT // 2
        kv_order = [[(a, sg) for a in range(4) for sg in ((0, 1, 2) if a < 2 else (3, 2, 1)) if sg % 2 == odd]
                    for odd in range(2)]

        def kv_place(a, sg):
            i = kv_order[sg % 2].index((a, sg))
            return acc[:, 3 + 2 * (sg % 2) + i // 4, (i % 4) * P:(i % 4 + 1) * P]

        def ftile(g, a):
            return HT * (a // 2) + 2 * g + a % 2

        def hgrn_act(act):
            act.wait_ge(acc_free, TASK0["mix0_out"] + 2)
            act.dma_start(flat(bwm[:]), d["con"][:, CON0["bw_mask"]:CON0["bw_mask"] + 4 * P]).then_inc(hg["masks"], 16)
            hgrn_in_act(7, 0, 1)
            for g in range(NG):
                act.wait_ge(hg["qdiff"], g + 1)
                act.activation(qmid[:, g % 2], qmid[:, g % 2], ACT.Exp).then_inc(hg["qexp"], 1)
                for dr, last in enumerate((SEG - 1, 0)):
                    f = tiles(ftile(g, 2 * dr), 2)
                    act.activation(decay[:, ftile(g, 2 * dr):ftile(g, 2 * dr) + 2, :], f[:, :, last:T:SEG], ACT.Exp)
                act.drain()
                for dr in range(2):
                    f = tiles(ftile(g, 2 * dr), 2)
                    o = act.activation(f, f, ACT.Exp)
                o.then_inc(hg["cumexp"], 1)
            for b in range(4):
                act.wait_ge(hg["out"], b + 1)
                act.activation(osq[:, 2 * b:2 * b + 2, :], tiles(Q0 + 2 * b, 2), ACT.Square).then_inc(hg["sq"], 1)
            act.wait_ge(hg["ms_ps"], 1)
            rn = osq.rearrange("p (b a) n -> p b (a n)", b=4)
            act.activation(rn, acc[:, 1:5, :], ACT.Ln, bias=eps[:, 1:2], scale=1.0 / P)
            act.drain()
            for b in range(2):
                act.activation(osq[:, 4 * b:4 * b + 4, :], osq[:, 4 * b:4 * b + 4, :], ACT.Exp, scale=-0.5)\
                   .then_inc(hg["rn"], 1)
            for q in range(4):
                if q < 2:
                    act.wait_ge(hg["done"], q + 1)
                hi_part(act, q, tiles((Q0 if q < 2 else UU0 - 8) + 4 * q))

        def hgrn_dve(dve):
            dve.memset(prob[:], 0.0)
            dve.wait_ge(hg["masks"], 16)

            def qdiff(g):
                for dr in range(2):
                    f = tiles(ftile(g, 2 * dr), 2)
                    o = dve.tensor_tensor(segs(qmid[:, g % 2, 2 * dr:2 * dr + 2, :]), segs(f),
                                          seg_point(f, POINTS[dr][0]), ALU.subtract)
                o.then_inc(hg["qdiff"], 1)
            qdiff(0)
            for g in range(NG):
                s, q = g % 2, tiles(Q0 + 2 * g, 2)
                if g + 1 < NG:
                    qdiff(g + 1)
                dve.wait_ge(hg["qexp"], g + 1)
                for dr in range(2):
                    o = dve.tensor_tensor(qmid[:, s, 2 * dr:2 * dr + 2, :], qmid[:, s, 2 * dr:2 * dr + 2, :], q, ALU.mult)
                o.then_inc(hg["qmid"], 1)
                dve.wait_ge(hg["cumexp"], g + 1)
                dve.wait_ge(hg["kv_ps"], g + 1)
                for j in range(3):
                    for a in range(4):
                        sg = j if a < 2 else NSEG - 1 - j
                        kv, st = kv_place(a, sg), lambda j: state[:, s, 3 * a + j, :]
                        if j == 0:
                            o = dve.tensor_copy(st(j), kv)
                        else:
                            o = dve.scalar_tensor_tensor(st(j), st(j - 1), decay[:, ftile(g, a), sg:sg + 1], kv,
                                                         ALU.mult, ALU.add)
                    if j < 2:
                        dve.drain()
                o.then_inc(hg["state"], 1)
                dve.wait_ge(hg["score_ps"], g + 1)
                for dr, mask in enumerate((fwm, bwm)):
                    o = dve.copy_predicated(prob[:, s, 4 * dr:4 * dr + 4, :], mask[:].bitcast(I32),
                                            acc[:, 1 + dr, :].rearrange("p (a n) -> p a n", a=4))
                o.then_inc(hg["prob"], 1)
                if g:
                    hgrn_take(dve, g - 1)
            hgrn_take(dve, NG - 1)
            for b in range(2):
                dve.wait_ge(hg["rn"], b + 1)
                for h in range(4 * b, 4 * b + 4):
                    dve.scalar_tensor_tensor(u[:, Q0 + h, :], u[:, Q0 + h, :], pcol("hgrn_norm_g", h), osq[:, h, :],
                                             ALU.mult, ALU.mult)
                dve.drain()
                dve.wait_ge(hg["silu"], 2)
                dve.tensor_tensor(tiles(Q0 + 4 * b), tiles(Q0 + 4 * b), tiles(G0 + 4 * b), ALU.mult)\
                   .then_inc(hg["done"], 1)
            for q in range(4):
                lo_part(dve, q, tiles((Q0 if q < 2 else UU0 - 8) + 4 * q), READY0["mix0_out"] + q + 1)

        def hgrn_take(dve, g):
            dve.wait_ge(hg["qcum"], g + 1)
            dve.wait_ge(hg["out_ps"], g + 1)
            dve.tensor_copy(flat(tiles(Q0 + 2 * g, 2)), acc[:, 7 * (g % 2), :]).then_inc(hg["out"], 1)

        def hgrn_pool(pool):
            hgrn_in_pool(pool)
            for g in range(NG):
                pool.wait_ge(hg["cumexp"], g + 1)
                for dr in range(2):
                    f = tiles(ftile(g, 2 * dr), 2)
                    o = pool.tensor_tensor(f, f, tiles(Q0 + 2 * g, 2), ALU.mult)
                o.then_inc(hg["qcum"], 1)

        def hgrn_pe(pe):
            def kv(g):
                for a in range(4):
                    for j in range(3):
                        sg = j if a < 2 else NSEG - 1 - j
                        rows, b = slice(SEG * (sg % 2), SEG * (sg % 2) + SEG), sg // 2
                        o = nc.tensor.matmul(kv_place(a, sg), u[rows, L0 + ftile(g, a), b * P:(b + 1) * P],
                                             u[rows, I0 + 2 * g + a % 2, b * P:(b + 1) * P], start=True, stop=True)
                o.then_inc(hg["kv_ps"], 1)

            def scores(g):
                pe.wait_ge(hg["qmid"], g + 1)
                for a in range(4):
                    for b in range(2):
                        i = 2 * a + b
                        o = nc.tensor.matmul(acc[:, 1 + i // 4, (i % 4) * P:(i % 4 + 1) * P],
                                             u[:, K0 + ftile(g, a), b * P:(b + 1) * P],
                                             qmid[:, g % 2, a, b * P:(b + 1) * P], start=True, stop=True)
                o.then_inc(hg["score_ps"], 1)
            pe.wait_ge(acc_free, TASK0["mix0_out"] + 2)
            kv(0)
            scores(0)
            for g in range(NG):
                pe.wait_ge(hg["state"], g + 1)
                if g + 1 < NG:
                    kv(g + 1)
                pe.wait_ge(hg["prob"], g + 1)
                if g + 1 < NG:
                    scores(g + 1)
                pe.wait_ge(hg["qcum"], g + 1)
                if g >= 2:
                    pe.wait_ge(hg["out"], g - 1)
                for hh in range(2):
                    o0, bank = hh * T, 7 * (g % 2)
                    for a in (hh, 2 + hh):
                        for b in range(2):
                            nc.tensor.matmul(acc[:, bank, o0 + b * P:o0 + (b + 1) * P],
                                             u[:, I0 + 2 * g + hh, b * P:(b + 1) * P],
                                             prob[:, g % 2, 2 * a + b, :], start=(a < 2 and b == 0), stop=False)
                        for j in range(3):
                            sg = j + 1 if a < 2 else NSEG - 2 - j
                            o = nc.tensor.matmul(acc[:, bank, o0 + sg * SEG:o0 + (sg + 1) * SEG],
                                                 state[:, g % 2, 3 * a + j, :],
                                                 u[:, ftile(g, a), sg * SEG:(sg + 1) * SEG], start=False,
                                                 stop=(a >= 2 and j == 2))
                o.then_inc(hg["out_ps"], 1)
            for b in range(4):
                pe.wait_ge(hg["sq"], b + 1)
                o = nc.tensor.matmul(acc[:, 1 + b, :], ones[:], flat(osq[:, 2 * b:2 * b + 2, :]), start=True, stop=True)
            o.then_inc(hg["ms_ps"], 1)
            pe.wait_ge(hg["rn"], 2)

        (r_sq, r_rn, r_g, r_cos, perm1, cos1, sin1), end = over(
            U0 + 4 * 24 * T, [[P, 4, T]] * 4 + [[P, P], [P, T], [P, T]])
        (v_tok, p_row, p_tok, mx, rs), end = over(
            end, [[P, 8, P], [P, 2, 4, T], [P, 2, 2 * T], [P, 2, 4], [P, 2, 4]])
        assert end <= W0
        at_ = {n: sem("at_" + n) for n in (
            "con", "sq", "ms_ps", "rn", "g", "rot_ps", "cos", "rot", "turned", "vtok_ps", "vtok", "score_ps", "max",
            "exp", "prob", "ptok_ps", "ptok", "out_ps", "hi", "lo")}
        NUNIT = 8
        SCALE = float(P) ** -0.5
        NTURN = 5

        def heads(first, j):
            return u[:, bass.ds(j * 4 + first, 4), :]

        def since(i, t, lo, hi):
            j = 2 * i + t - 1 if isinstance(i, int) else i * 2 + (t - 1)
            return j if not isinstance(i, int) or lo <= j < hi else None

        def heads(first, j):
            return u[:, bass.ds(j * 4 + first, 4), :]

        def since(i, t, lo, hi):
            j = 2 * i + t - 1 if isinstance(i, int) else i * 2 + (t - 1)
            return j if not isinstance(i, int) or lo <= j < hi else None

        def flat(x):
            return x.rearrange("p a n -> p (a n)")

        def norm_turn_act(i, t, c):
            act, j = nc.scalar, since(i, t, 0, NTURN)
            if j is None:
                return
            if c == 1:
                act.wait_ge(acc_free, TASK0["attn_in"] + j + 3)
                act.activation(r_sq[:], heads(0, j), ACT.Square).then_inc(at_["sq"], 1)
            elif c == 2:
                act.wait_ge(at_["ms_ps"], j + 1)
                act.wait_ge(at_["g"], j + 1)
                act.activation(r_rn[:].rearrange("p (b a) n -> p b (a n)", b=2),
                               acc[:, 4 * (1 - t):4 * (1 - t) + 2, :], ACT.Ln, bias=eps[:, 1:2], scale=1.0 / P)
                act.drain()
                act.activation(r_rn[:], r_rn[:], ACT.Exp, scale=-0.5).then_inc(at_["rn"], 1)

        def norm_turn_dve(i, t, c):
            dve, j = nc.vector, since(i, t, 0, NTURN)
            if j is None:
                return
            four = heads(0, j)
            if c == 1:
                dve.drain()
                dve.tensor_scalar(r_g[:], four, col("qk_norm_g", j * 2), None, ALU.mult).then_inc(at_["g"], 1)
            elif c == 2:
                dve.drain()
                dve.wait_ge(at_["rot_ps"], j + 1)
                dve.tensor_tensor(four, acc[:, 4 * (1 - t) + 2:4 * (1 - t) + 4, :].rearrange("p b (a n) -> p (b a) n", a=2),
                                  wide(sin1[:], 4), ALU.mult).then_inc(at_["rot"], 1)
            elif c == 3:
                dve.drain()
                dve.wait_ge(at_["cos"], j + 1)
                dve.tensor_tensor(four, four, r_cos[:], ALU.add)
                dve.drain()
                dve.wait_ge(at_["rn"], j + 1)
                dve.tensor_tensor(four, four, r_rn[:], ALU.mult).then_inc(at_["turned"], 1)

        def norm_turn_pe(i, t, c):
            pe, j = nc.tensor, since(i, t, 0, NTURN)
            if j is None or c != 2:
                return
            b0 = 4 * (1 - t)
            pe.wait_ge(acc_free, TASK0["attn_in"] + j + 3)
            pe.wait_ge(at_["sq"], j + 1)
            for h in range(2):
                o = pe.matmul(acc[:, b0 + h, :], ones[:], flat(r_sq[:, 2 * h:2 * h + 2, :]), start=True, stop=True)
            o.then_inc(at_["ms_ps"], 1)
            pe.wait_ge(at_["g"], j + 1)
            for h in range(2):
                o = pe.matmul(acc[:, b0 + 2 + h, :], perm1[:], flat(r_g[:, 2 * h:2 * h + 2, :]), start=True, stop=True)
            o.then_inc(at_["rot_ps"], 1)

        def norm_turn_read(i, t):
            j = since(i, t, 1, NTURN + 1)
            if j is not None:
                nc.tensor.wait_ge(at_["rn"], j)
                nc.tensor.wait_ge(at_["rot"], j)

        def attn_act(act):
            act.wait_ge(acc_free, TASK0["attn_out"] + 2)
            act.wait_ge(at_["vtok_ps"], 1)
            for b in range(2):
                o = act.activation(flat(v_tok[:, 4 * b:4 * b + 4, :]), acc[:, 6 + b, :], ACT.Copy)
            o.then_inc(at_["vtok"], 1)
            for n in range(NUNIT + 1):
                if n < NUNIT:
                    s = n % 2
                    act.wait_ge(at_["max"], n + 1)
                    if n >= 2:
                        act.wait_ge(at_["ptok_ps"], n - 1)
                    for i in range(4):
                        o = act.activation(p_row[:, s, i, :], acc[:, 2 * s + i // 2, (i % 2) * T:(i % 2 + 1) * T],
                                           ACT.Exp, bias=mx[:, s, i:i + 1], scale=SCALE, accum_out=rs[:, s, i:i + 1])
                    o.then_inc(at_["exp"], 1)
                if n:
                    m = n - 1
                    act.wait_ge(at_["ptok_ps"], m + 1)
                    for h in range(2):
                        o = act.activation(p_tok[:, h, :], acc[:, 4 + h, :], ACT.Copy)
                    o.then_inc(at_["ptok"], 1)
                    act.wait_ge(at_["out_ps"], m + 1)
                    act.activation(xhl[:, 2 * m:2 * m + 2, 0:T],
                                   acc[:, 6 + m % 2, :].rearrange("p (h n) -> p h n", h=2), ACT.Copy)\
                       .then_inc(x_hi if m % 2 else at_["hi"], 1)

        def attn_dve(dve):
            for n in range(NUNIT + 2):
                if n < NUNIT:
                    s = n % 2
                    if n >= 2:
                        dve.drain()
                        dve.wait_ge(at_["exp"], n - 1)
                    dve.wait_ge(at_["score_ps"], n + 1)
                    dve.tensor_reduce(mx[:, s, :], acc[:, 2 * s:2 * s + 2, :].rearrange("p h (b n) -> p (h b) n", b=2),
                                      AX, ALU.max)
                    dve.drain()
                    dve.tensor_scalar(mx[:, s, :], mx[:, s, :], -SCALE, None, ALU.mult).then_inc(at_["max"], 1)
                if 1 <= n <= NUNIT:
                    m = n - 1
                    s = m % 2
                    dve.wait_ge(at_["exp"], m + 1)
                    dve.reciprocal(rs[:, s, :], rs[:, s, :])
                    dve.drain()
                    dve.tensor_tensor(p_row[:, s], p_row[:, s], rs[:, s, :].unsqueeze(2).to_broadcast([P, 4, T]),
                                      ALU.mult).then_inc(at_["prob"], 1)
                if n >= 2:
                    m = n - 2
                    if m % 2:
                        dve.wait_ge(x_hi, READY0["attn_out"] + m // 2 + 1)
                    else:
                        dve.wait_ge(at_["hi"], m // 2 + 1)
                    dst = xhl[:, 2 * m:2 * m + 2, :]
                    o = dve.tensor_tensor(dst[:, :, T:2 * T], acc[:, 6 + m % 2, :].rearrange("p (h n) -> p h n", h=2),
                                          dst[:, :, 0:T].bitcast(F32), ALU.subtract)
                    o.then_inc(moving_ready if m % 2 else at_["lo"], 1)

        def attn_pool(pool):
            pool.wait_ge(at_["con"], 48)
            for j in loop(pool, NTURN):
                pool.wait_ge(at_["g"], j + 1)
                pool.tensor_tensor(r_cos[:], r_g[:], wide(cos1[:], 4), ALU.mult).then_inc(at_["cos"], 1)

        def attn_pe(pe):
            pe.wait_ge(acc_free, TASK0["attn_out"] + 2)
            pe.wait_ge(at_["turned"], NTURN)
            for g in range(4):
                for b in range(2):
                    o = nc.tensor.transpose(acc[:, 6 + g // 2, (2 * (g % 2) + b) * P:(2 * (g % 2) + b + 1) * P],
                                            u[:, 20 + g, b * P:(b + 1) * P], ident[:])
            o.then_inc(at_["vtok_ps"], 1)

            def scores(n):
                for i in range(4):
                    q = 2 * n + i // 2
                    o = nc.tensor.matmul(acc[:, 2 * (n % 2) + i // 2, (i % 2) * T:(i % 2 + 1) * T],
                                         u[:, q, (i % 2) * P:(i % 2 + 1) * P], u[:, 16 + q // 4, :],
                                         start=True, stop=True)
                o.then_inc(at_["score_ps"], 1)
            scores(0)
            scores(1)
            for n in range(NUNIT):
                pe.wait_ge(at_["prob"], n + 1)
                for i in range(8):
                    h, sb, b = i // 4, i // 2 % 2, i % 2
                    o = nc.tensor.transpose(acc[:, 4 + h, sb * T + b * P:sb * T + (b + 1) * P],
                                            p_row[:, n % 2, 2 * h + b, sb * P:(sb + 1) * P], ident[:])
                o.then_inc(at_["ptok_ps"], 1)
                if n + 2 < NUNIT:
                    scores(n + 2)
                pe.wait_ge(at_["ptok"], n + 1)
                if n == 0:
                    pe.wait_ge(at_["vtok"], 1)
                if n >= 2:
                    if n % 2:
                        pe.wait_ge(moving_ready, READY0["attn_out"] + n // 2)
                    else:
                        pe.wait_ge(at_["lo"], n // 2)
                for i in range(4):
                    h, sb = i // 2, i % 2
                    o = nc.tensor.matmul(acc[:, 6 + n % 2, h * T:(h + 1) * T], v_tok[:, 2 * (n // 2) + sb, :],
                                         p_tok[:, h, sb * T:(sb + 1) * T], start=(sb == 0), stop=(sb == 1))
                o.then_inc(at_["out_ps"], 1)
            pe.wait_ge(moving_ready, READY0["attn_out"] + 4)

        UX0, UG0, XC0, R0, IG0 = 0, MT, 2 * MT, 3 * MT, 4 * MT
        (w_gates,), end = over(W0, [[P, 2, MT, P]])
        assert end <= W0 + WSIZE
        ru = {n: sem("ru_" + n) for n in ("con", "abs", "e", "cols", "conv", "ps", "sig", "tanh", "bsq",
                                          "sqrt", "silu", "done")}
        NSP, TMP = 0, MT

        def rnn_act(i, t, c):
            act, task = nc.scalar, 2 * i + t
            if c == 1 and task == 0:
                act.wait_ge(ru["abs"], 1)
                act.activation(nrg[:, TMP:TMP + MT], nrg[:, TMP:TMP + MT], ACT.Exp, scale=-1.0).then_inc(ru["e"], 1)
            q = task - 1
            if c == 3 and 0 <= q < 4:
                act.wait_ge(ru["ps"], q + 1)
                for f in range(4):
                    m, bank = 4 * q + f, 4 * (1 - t) + f
                    act.activation(u[:, R0 + m, :], acc[:, bank, 0:T], ACT.Sigmoid, bias=pcol("b_rg_2", m))
                    o = act.activation(u[:, IG0 + m, :], acc[:, bank, T:2 * T], ACT.Sigmoid, bias=pcol("b_ig_2", m))
                o.then_inc(ru["sig"], 1)
            q = task - 2
            if c == 1 and 0 <= q < 4:
                act.wait_ge(ru["cols"], 1)
                act.drain()
                for f in range(4):
                    m = 4 * q + f
                    act.activation(u[:, UX0 + m, :], u[:, R0 + m, :], ACT.Exp, scale=nrg[:, NSP + m:NSP + m + 1])
                for f in range(4):
                    m = 4 * q + f
                    o = act.activation(u[:, R0 + m, :], u[:, R0 + m, :], ACT.Tanh, scale=nrg[:, NSP + m:NSP + m + 1])
                o.then_inc(ru["tanh"], 1)
            q = task - 3
            if c == 1 and 0 <= q < 4:
                act.wait_ge(ru["bsq"], q + 1)
                xq = u[:, XC0 + 4 * q:XC0 + 4 * q + 4, :]
                act.activation(xq, xq, ACT.Sqrt, scale=-1.0).then_inc(ru["sqrt"], 1)
            q = task - 5
            if c == 2 and 0 <= q < 4:
                act.wait_ge(acc_free, TASK0["rnn_in"] + 4 + q + 3)
                gq = u[:, UG0 + 4 * q:UG0 + 4 * q + 4, :]
                act.activation(gq, gq, ACT.Silu).then_inc(ru["silu"], 1)

        def rnn_cols(dve):
            c = lambda at0: nrg[:, at0:at0 + MT]
            lam = par[:, PAR0["lru_lambda_2"]:PAR0["lru_lambda_2"] + MT]
            dve.wait_ge(ru["e"], 1)
            dve.tensor_scalar(c(NSP), c(TMP), 2.0, None, ALU.add)
            dve.drain()
            dve.reciprocal(c(NSP), c(NSP))
            dve.drain()
            dve.tensor_tensor(c(TMP), c(TMP), c(NSP), ALU.mult)
            dve.drain()
            sq, ser = c(2 * MT), c(3 * MT)
            dve.tensor_tensor(sq, c(TMP), c(TMP), ALU.mult)
            dve.memset(ser, 1.0 / 19)
            dve.drain()
            for k in range(8, -1, -1):
                dve.tensor_tensor(ser, ser, sq, ALU.mult)
                dve.drain()
                dve.tensor_scalar(ser, ser, 1.0 / (2 * k + 1), None, ALU.add)
                dve.drain()
            dve.scalar_tensor_tensor(c(TMP), ser, 2.0, c(TMP), ALU.mult, ALU.mult)
            dve.tensor_scalar(sq, lam, -1.0, 0.0, ALU.mult, ALU.max)
            dve.drain()
            dve.tensor_tensor(c(TMP), c(TMP), sq, ALU.add)
            dve.drain()
            dve.tensor_scalar(c(NSP), c(TMP), -LRU_C, None, ALU.mult).then_inc(ru["cols"], 1)

        def rnn_dve(i, t, c):
            dve, task = nc.vector, 2 * i + t
            four = lambda at0, q: u[:, at0 + 4 * q:at0 + 4 * q + 4, :]
            if c == 1 and task == 0:
                lam = par[:, PAR0["lru_lambda_2"]:PAR0["lru_lambda_2"] + MT]
                dve.scalar_tensor_tensor(nrg[:, TMP:TMP + MT], lam, -1.0, lam, ALU.mult, ALU.max)\
                   .then_inc(ru["abs"], 1)
            if c == 3 and task == 0:
                rnn_cols(dve)
            q = task - 1
            if c == 1 and 0 <= q < 4:
                cw = PAR0["conv_w_2"]
                dve.drain()
                for m in range(4 * q, 4 * q + 4):
                    o = dve.tensor_scalar(u[:, XC0 + m, :], u[:, UX0 + m, :], par[:, cw + 3 * MT + m:cw + 3 * MT + m + 1],
                                          pcol("conv_b_2", m), ALU.mult, ALU.add)
                for s in (1, 2, 3):
                    dve.drain()
                    for m in range(4 * q, 4 * q + 4):
                        w = cw + (3 - s) * MT + m
                        o = dve.scalar_tensor_tensor(u[:, XC0 + m, s:T], u[:, UX0 + m, 0:T - s], par[:, w:w + 1],
                                                     u[:, XC0 + m, s:T], ALU.mult, ALU.add)
                o.then_inc(ru["conv"], 1)
            q = task - 2
            if c == 2 and 0 <= q < 4:
                dve.wait_ge(ru["tanh"], q + 1)
                a, xq, g = four(UX0, q), four(XC0, q), four(IG0, q)
                dve.tensor_tensor(g, g, xq, ALU.mult)
                dve.drain()
                dve.tensor_tensor(xq, a, a, ALU.mult)
                dve.drain()
                dve.scalar_tensor_tensor(xq, xq, 1.0, four(R0, q), ALU.add, ALU.mult).then_inc(ru["bsq"], 1)
            q = task - 3
            if c == 2 and 0 <= q < 4:
                dve.wait_ge(ru["sqrt"], q + 1)
                dve.tensor_tensor(four(IG0, q), four(IG0, q), four(XC0, q), ALU.mult)
                dve.drain()
                for m in range(4 * q, 4 * q + 4):
                    dve.tensor_tensor_scan(u[:, R0 + m, :], u[:, UX0 + m, :], u[:, IG0 + m, :], 0.0, ALU.mult, ALU.add)
            q = task - 5
            if c == 3 and 0 <= q < 4:
                dve.drain()
                dve.wait_ge(ru["silu"], q + 1)
                dve.tensor_tensor(four(UX0, q), four(R0, q), four(UG0, q), ALU.mult).then_inc(ru["done"], 1)

        def rnn_pe(i, t, c):
            pe, q = nc.tensor, 2 * i + t - 1
            if c == 3 and 0 <= q < 4:
                if q == 0:
                    pe.wait_ge(ru["con"], 16)
                pe.wait_ge(acc_free, TASK0["rnn_in"] + q + 3)
                pe.wait_ge(ru["conv"], q + 1)
                for f in range(4):
                    m = 4 * q + f
                    for j in range(2):
                        o = pe.matmul(acc[:, 4 * (1 - t) + f, j * T:(j + 1) * T], w_gates[:, j, m, :],
                                      u[:, XC0 + m, :], start=True, stop=True)
                o.then_inc(ru["ps"], 1)

        def rnn_read(i, t):
            if 0 <= 2 * i + t - 2 < 4:
                nc.tensor.wait_ge(ru["sig"], 2 * i + t - 1)

        QD, KD, VD, AG = 2 * MT, 2 * MT + 12, 2 * MT + 24, 2 * MT + 36
        OD = MT
        (perm2, cos2, sin2, mask0, mask1, t_cos, t_rot), end = over(
            W0, [[P, P], [P, T], [P, T], [P, 3 * P], [P, 3 * T], [P, 4, T], [P, 4, T]])
        assert end <= W0 + WSIZE
        (dvt1, dp01, dp11), end = over(U0 + 4 * 24 * T, [[P, 6, P], [P, 3 * P], [P, 3 * T]])
        assert end <= U0 + 4 * 32 * T
        (dvt0, dp00, dp10, dt0, dt1, dmx, drs), end = over(
            U0 + 4 * 72 * T, [[P, 6, P], [P, 3 * P], [P, 3 * T], [P, 3, P], [P, 6, P], [P, 2, 2], [P, 2, 2]])
        assert end <= W0
        dvt, dp0, dp1 = (dvt0, dvt1), (dp00, dp01), (dp10, dp11)
        dl = {n: sem("dl_" + n) for n in ("con", "rot_ps", "cos", "rot", "turned", "vtok_ps", "vtok", "score_ps",
                                          "scores_read", "max", "exp", "prob", "ptok_ps", "ptok", "out_ps", "out", "silu", "gated",
                                          "o_done")}

        def dil_act(hf):
            def run(act):
                act.wait_ge(acc_free, TASK0["half%d" % hf] + NTASK["half%d" % hf] + 2)
                for h in range(-1, 4):
                    n, s = h + 4 * hf, h % 2
                    if h >= 0:
                        act.wait_ge(dl["max"], n + 1)
                        act.activation(dp0[s][:], dp0[s][:], ACT.Exp, bias=dmx[:, s, 0:1], accum_out=drs[:, s, 0:1])
                        act.activation(dp1[s][:], dp1[s][:], ACT.Exp, bias=dmx[:, s, 1:2], accum_out=drs[:, s, 1:2])\
                           .then_inc(dl["exp"], 1)
                    if h + 1 < 4:
                        m, r = n + 1, 1 - s
                        act.wait_ge(dl["vtok_ps"], m + 1)
                        act.activation(flat(dvt[r][:])[:, 0:4 * P], acc[:, 3, :], ACT.Copy)
                        act.activation(flat(dvt[r][:])[:, 4 * P:6 * P], acc[:, 4, 0:2 * P], ACT.Copy)\
                           .then_inc(dl["vtok"], 1)
                    if h >= 0:
                        act.wait_ge(dl["ptok_ps"], n + 1)
                        act.activation(flat(dt0[:]), acc[:, 5, 0:3 * P], ACT.Copy)
                        act.activation(flat(dt1[:])[:, 0:4 * P], acc[:, 6, :], ACT.Copy)
                        act.activation(flat(dt1[:])[:, 4 * P:6 * P], acc[:, 7, 0:2 * P], ACT.Copy)\
                           .then_inc(dl["ptok"], 1)
                act.activation(u[:, AG:AG + 4, :], u[:, AG:AG + 4, :], ACT.Silu).then_inc(dl["silu"], 1)
            return run

        def dil_dve(hf):
            def run(dve):
                for h in range(-1, 4):
                    n, s = h + 4 * hf, h % 2
                    if h >= 0:
                        dve.wait_ge(dl["exp"], n + 1)
                        dve.reciprocal(drs[:, s, :], drs[:, s, :])
                        dve.drain()
                        dve.tensor_scalar(dp0[s][:], dp0[s][:], drs[:, s, 0:1], None, ALU.mult)
                        dve.tensor_scalar(dp1[s][:], dp1[s][:], drs[:, s, 1:2], None, ALU.mult)\
                           .then_inc(dl["prob"], 1)
                    if h + 1 < 4:
                        m, r = n + 1, 1 - s
                        dve.wait_ge(dl["score_ps"], m + 1)
                        if h >= 1:
                            dve.wait_ge(dl["ptok_ps"], m - 1)
                        dve.scalar_tensor_tensor(dp0[r][:], acc[:, 0, 0:3 * P], SCALE, mask0[:], ALU.mult, ALU.add)
                        dve.scalar_tensor_tensor(dp1[r][:, 0:2 * T], acc[:, 1, :], SCALE, mask1[:, 0:2 * T],
                                                 ALU.mult, ALU.add)
                        dve.scalar_tensor_tensor(dp1[r][:, 2 * T:3 * T], acc[:, 2, 0:T], SCALE,
                                                 mask1[:, 2 * T:3 * T], ALU.mult, ALU.add)\
                           .then_inc(dl["scores_read"], 1)
                        dve.drain()
                        dve.tensor_reduce(dmx[:, r, 0:1], dp0[r][:], AX, ALU.max)
                        dve.tensor_reduce(dmx[:, r, 1:2], dp1[r][:], AX, ALU.max)
                        dve.drain()
                        dve.tensor_scalar(dmx[:, r, :], dmx[:, r, :], -1.0, None, ALU.mult).then_inc(dl["max"], 1)
                    if h >= 0:
                        dve.wait_ge(dl["out_ps"], n + 1)
                        dve.tensor_copy(u[:, OD + 4 * hf + h, :], acc[:, 7, T:2 * T]).then_inc(dl["out"], 1)
                dve.wait_ge(dl["silu"], hf + 1)
                dve.drain()
                o = u[:, OD + 4 * hf:OD + 4 * hf + 4, :]
                dve.tensor_tensor(o, o, u[:, AG:AG + 4, :], ALU.mult).then_inc(dl["gated"], 1)
            return run

        def dil_pool(hf):
            def run(pool):
                pool.wait_ge(dl["con"], 80)
                def cos(j):
                    pool.wait_ge(acc_free, j + (TASK0["half%d" % hf] + 3))
                    if hf or not isinstance(j, int):
                        pool.wait_ge(dl["turned"], j + 6 * hf)
                    pool.tensor_tensor(t_cos[:], heads(QD, j), wide(cos2[:], 4), ALU.mult).then_inc(dl["cos"], 1)
                cos(0)
                with pool.Fori(1, 6) as j:
                    cos(j)
            return run

        def turn_dve(hf):
            def between(i, t, c):
                dve, j = nc.vector, since(i, t, 0, 6)
                if j is None:
                    return
                if c == 2:
                    dve.drain()
                    dve.wait_ge(dl["rot_ps"], j + 6 * hf + 1)
                    dve.tensor_tensor(t_rot[:], acc[:, 4 * (1 - t):4 * (1 - t) + 2, :].rearrange(
                        "p b (a n) -> p (b a) n", a=2), wide(sin2[:], 4), ALU.mult).then_inc(dl["rot"], 1)
                elif c == 3:
                    dve.drain()
                    dve.wait_ge(dl["cos"], j + 6 * hf + 1)
                    dve.tensor_tensor(heads(QD, j), t_rot[:], t_cos[:], ALU.add).then_inc(dl["turned"], 1)
            return between

        def turn_pe(hf):
            def extra(i, t, c):
                pe, j = nc.tensor, since(i, t, 0, 6)
                if j is None or c != 2:
                    return
                pe.wait_ge(acc_free, j + (TASK0["half%d" % hf] + 3))
                for h in range(2):
                    o = pe.matmul(acc[:, 4 * (1 - t) + h, :], perm2[:],
                                  flat(u[:, bass.ds(j * 4 + (QD + 2 * h), 2), :]), start=True, stop=True)
                o.then_inc(dl["rot_ps"], 1)
            return extra

        def turn_read(hf):
            def banks_read(i, t):
                j = since(i, t, 1, 7)
                if j is not None:
                    nc.tensor.wait_ge(dl["rot"], j + 6 * hf)
            return banks_read

        def dil_pe(hf):
            def run(pe):
                pe.wait_ge(acc_free, TASK0["half%d" % hf] + NTASK["half%d" % hf] + 2)
                pe.wait_ge(dl["turned"], 6 * hf + 6)
                for h in range(-1, 4):
                    n, s = h + 4 * hf, h % 2
                    if h + 1 < 4:
                        m = h + 1
                        if h >= 0:
                            pe.wait_ge(dl["vtok"], n + 1)
                        for i in range(6):
                            o = nc.tensor.transpose(acc[:, 3 + i // 4, (i % 4) * P:(i % 4 + 1) * P],
                                                    u[:, VD + 4 * (i // 2) + m, (i % 2) * P:(i % 2 + 1) * P], ident[:])
                        o.then_inc(dl["vtok_ps"], 1)
                        if h >= 0:
                            pe.wait_ge(dl["scores_read"], n + 1)
                        for g in range(3):
                            q, k = u[:, QD + 4 * g + m, :], u[:, KD + 4 * g + m, :]
                            nc.tensor.matmul(acc[:, 0, g * P:(g + 1) * P], q[:, 0:P], k[:, 0:P], start=True, stop=True)
                            o = nc.tensor.matmul(acc[:, 1 + g // 2, (g % 2) * T:(g % 2 + 1) * T], q[:, P:2 * P], k,
                                                 start=True, stop=True)
                        o.then_inc(dl["score_ps"], 1)
                    if h < 0:
                        continue
                    pe.wait_ge(dl["prob"], n + 1)
                    if n:
                        pe.wait_ge(dl["out"], n + 1)
                    for g in range(3):
                        nc.tensor.transpose(acc[:, 5, g * P:(g + 1) * P], dp0[s][:, g * P:(g + 1) * P], ident[:])
                    for i in range(6):
                        o = nc.tensor.transpose(acc[:, 6 + i // 4, (i % 4) * P:(i % 4 + 1) * P],
                                                dp1[s][:, i * P:(i + 1) * P], ident[:])
                    o.then_inc(dl["ptok_ps"], 1)
                    pe.wait_ge(dl["ptok"], n + 1)
                    pe.wait_ge(dl["vtok"], n + 1)
                    for g in range(3):
                        nc.tensor.matmul(acc[:, 7, T:T + P], dvt[s][:, 2 * g, :], dt0[:, g, :],
                                         start=(g == 0), stop=(g == 2))
                    for i in range(6):
                        o = nc.tensor.matmul(acc[:, 7, T + P:2 * T], dvt[s][:, i, :], dt1[:, i, :],
                                             start=(i == 0), stop=(i == 5))
                    o.then_inc(dl["out_ps"], 1)
                pe.wait_ge(dl["out"], 4 * hf + 5)
            return run

        pre_norm = sem("pre_norm")
        pre_scaled = sem("pre_scaled")
        gates_sig = sem("gates_sig")
        merged = sem("merged")
        fin = sem("fin")

        def pre_act(act):
            act.wait_ge(sums_ready, 6)
            act_rstd(5, 1, acc[:, 0, T:2 * T], 1.0 / DM)
            for q in range(4):
                act.wait_ge(pre_norm, q + 1)
                for m in range(4 * q, 4 * q + 4):
                    act.activation(u[:, m, :], u[:, m, :], ACT.Copy, scale=pcol("ln_pre_g_2", m))
                act.drain()
                hi_part(act, q, u[:, 4 * q:4 * q + 4, :])
            act.dma_start(w_gates[:], d["w_gates"]).then_inc(ru["con"], 16)

        def pre_dve(dve):
            dve.wait_ge(rstd_ready, 6)
            for q in range(4):
                dve.tensor_tensor(u[:, 4 * q:4 * q + 4, :], z[:, 4 * q:4 * q + 4, :], wide(rstd[:], 4), ALU.mult)\
                   .then_inc(pre_norm, 1)
                if q:
                    lo_part(dve, q - 1, u[:, 4 * q - 4:4 * q, :], READY0["rnn_in"] + q)
            lo_part(dve, 3, u[:, 12:16, :], READY0["rnn_in"] + 4)

        def gates_act(act):
            act.wait_ge(acc_free, TASK0["rnn_out"] + 2)
            for q in range(4):
                hi_part(act, q, u[:, UX0 + 4 * q:UX0 + 4 * q + 4, :])
            for q in range(2):
                hi_part(act, q, u[:, OD + 4 * q:OD + 4 * q + 4, :], hid[:, FT - HT + 4 * q:FT - HT + 4 * q + 4, :])
            for q in range(8):
                act.activation(u[:, 32 + 4 * q:36 + 4 * q, :], u[:, 32 + 4 * q:36 + 4 * q, :], ACT.Sigmoid)\
                   .then_inc(gates_sig, 1)

        def gates_dve(dve):
            for q in range(4):
                lo_part(dve, q, u[:, UX0 + 4 * q:UX0 + 4 * q + 4, :], READY0["rnn_out"] + q + 1)
            for q in range(2):
                lo_part(dve, q, u[:, OD + 4 * q:OD + 4 * q + 4, :], READY0["dil_out"] + q + 1,
                        hid[:, FT - HT + 4 * q:FT - HT + 4 * q + 4, :])

        def dve_gated(which):
            def after(i, t, task, n):
                dve = nc.vector
                dve.drain()
                dve.wait_ge(chunk_used, n + 1)
                if which == 0:
                    dve.wait_ge(gates_sig, i * 2 + t + 1)
                else:
                    dve.wait_ge(gates_sig, i * 2 + t + 5)
                for f in range(CF):
                    o = read_out(etmp[:, f, :], 4 * t + f)
                o.then_inc(acc_free, 1)
                dve.drain()
                first = utile(32, 8, i)[:, 4 * t:4 * t + 4, :]
                own = utile(48, 8, i)[:, 4 * t:4 * t + 4, :] if which else first
                o = dve.tensor_tensor(own, own, etmp[:], ALU.mult)
                if which:
                    dve.drain()
                    o = dve.tensor_tensor(first, first, own, ALU.add)
                    o.then_inc(merged, 1)
            return after

        def merge_act(act):
            for q in range(4):
                act.wait_ge(merged, q + 1)
                hi_part(act, q, u[:, 32 + 4 * q:36 + 4 * q, :])

        def merge_dve(dve):
            for q in range(4):
                lo_part(dve, q, u[:, 32 + 4 * q:36 + 4 * q, :], READY0["last_out"] + q + 1)

        def dve_last(i, t, task, n):
            nc.vector.wait_ge(chunk_used, n + 1)
            for f in range(CF):
                o = read_out(u[:, bass.ds(i * 8 + t * 4 + f, 1), :].squeeze(1), 4 * t + f)
                if f == CF - 1:
                    o.then_inc(acc_free, 1)

        def final_act(act):
            act.wait_ge(sums_ready, 7)
            act_rstd(6, 1, acc[:, 0, T:2 * T], 1.0 / DM)

        def final_dve(dve):
            dve.wait_ge(rstd_ready, 7)
            for q in range(4):
                uq = u[:, 4 * q:4 * q + 4, :]
                dve.tensor_tensor(uq, uq, wide(rstd[:], 4), ALU.mult)
                dve.drain()
                for m in range(4 * q, 4 * q + 4):
                    o = dve.scalar_tensor_tensor(z[:, m, :], u[:, m, :], pcol("ln_post_g_2", m), z[:, m, :],
                                                 ALU.mult, ALU.add)
                o.then_inc(out_ready, 1)

        FIRST_TILE = {"mix0_in": 0, "attn_in": 0, "rnn_in": 0, "half0": QD, "half1": QD, "gates": 2 * MT}
        LNS = {"mix0_out": (0, "ln1", 0, "up0"), "down0": (1, "ln2", 0, "attn_in"),
               "attn_out": (2, "ln1", 1, "up1"), "down1": (3, "ln2", 1, None)}

        @block.sync
        def _(sp):
            wd = d["weights"]
            for n in range(2):
                sp.dma_start(raw[:, n, :], wd[n]).then_inc(raw_landed[n], 16)
            with sp.Fori(1, NCHUNKS // 2) as i:
                for s in range(2):
                    sp.wait_ge(weights_split, i * 2 + s - 1)
                    sp.dma_start(raw[:, s, :], wd[bass.ds(i * 2 + s, 1)].squeeze(0)).then_inc(raw_landed[s], 16)
            for q in range(4):
                sp.wait_ge(out_ready, q + 1)
                sp.dma_start(d["out"][:, 4 * q:4 * q + 4, :], z[:, 4 * q:4 * q + 4, :]).then_inc(out_stored, 16)
            sp.wait_ge(out_stored, 64)

        @block.gpsimd
        def _(pool):
            for name in on:
                if name in LNS:
                    pool_sums(LNS[name][0], z)
                elif name.startswith("up"):
                    pool_hidden(int(name[2]))
                elif name == "mix0_in":
                    hgrn_pool(pool)
                elif name == "attn_in":
                    attn_pool(pool)
                elif name.startswith("half"):
                    dil_pool(int(name[4]))(pool)
                elif name == "last_out":
                    pool_sums(5, None)
                if name == "down1":
                    pool_sums(4, None)

        @block.scalar
        def _(act):
            act.dma_start(z[:], d["x"]).then_inc(x_landed, 16)
            act.dma_start(par[:], d["par"]).then_inc(par_landed, 16)

            def con(dst, name, n, s):
                dst = dst if len(dst.shape) == 2 else flat(dst)
                act.dma_start(dst, d["con"][:, CON0[name]:CON0[name] + n]).then_inc(s, 16)
            for dst, name, n in ((ident[:], "ident", P), (seg1[:], "seg_start", T), (fwm[:], "fw_mask", 4 * P)):
                con(dst, name, n, con_landed)
            act.wait_ge(x_landed, 16)
            for q in range(4):
                hi_part(act, q, z[:, 4 * q:4 * q + 4, :])
            cast_chunk(act, 0, 0)
            cast_chunk(act, 1, 1)
            act.wait_ge(par_landed, 16)
            for name in on:
                end = name == STAGES[-1][0]
                if name in LNS:
                    occ, ln, layer, nxt = LNS[name]
                    drive(act, name, cast_chunk, None, unroll=True, between=act_between(occ, z))
                    act_square(occ, 3, z)
                    act_rstd(1 + occ, 0)
                    act_affine(4 * occ, ln + "_g", ln + "_b", nxt, layer * MT)
                    if name == "down0":
                        for dst, cn, n in ((perm1[:], "rope1_perm", P), (cos1[:], "rope1_cos", T),
                                           (sin1[:], "rope1_sin", T)):
                            con(dst, cn, n, at_["con"])
                    if name == "down1":
                        pre_act(act)
                elif name.startswith("up"):
                    drive(act, name, cast_chunk, act_silu(int(name[2])), unroll=end)
                elif name == "last_out":
                    drive(act, name, cast_chunk, None, unroll=True, between=act_between(5, u))
                    act_square(5, 3, u)
                    final_act(act)
                elif name == "mix0_in":
                    drive(act, name, cast_chunk, None, between=hgrn_in_act, unroll=True)
                elif name == "attn_in":
                    drive(act, name, cast_chunk, None, between=norm_turn_act, peel=(1,))
                elif name == "rnn_in":
                    drive(act, name, cast_chunk, None, between=rnn_act, unroll=True)
                else:
                    drive(act, name, cast_chunk, None, unroll=end)
                if name == "mix0_in":
                    hgrn_act(act)
                elif name == "attn_in":
                    attn_act(act)
                elif name == "rnn_in":
                    rnn_act(4, 0, 2)
                    for dst, cn, n in ((perm2[:], "rope2_perm", P), (cos2[:], "rope2_cos", T),
                                       (sin2[:], "rope2_sin", T), (mask0[:], "dil_mask0", 3 * P),
                                       (mask1[:], "dil_mask1", 3 * T)):
                        con(dst, cn, n, dl["con"])
                elif name.startswith("half"):
                    dil_act(int(name[4]))(act)
                elif name == "gates":
                    gates_act(act)
                elif name == "dil_out":
                    merge_act(act)

        @block.vector
        def _(dve):
            dve.memset(ones[:], 1.0)
            dve.memset(eps[:, 0:1], LN_EPS)
            dve.memset(eps[:, 1:2], RMS_EPS).then_inc(acc_free, 2)
            for c, s in enumerate((hid_ready, sq_used, dl["out"])):
                dve.memset(eps[:, 2 + c:3 + c], 0.0).then_inc(s, 1)
            for q in range(4):
                lo_part(dve, q, z[:, 4 * q:4 * q + 4, :], q + 1)
            split_chunk(dve, 0, 0)
            split_chunk(dve, 1, 1)
            dve.wait_ge(par_landed, 16)
            tab = lambda r: par[:, PAR0["hgrn_lb_table"] + r * HT:PAR0["hgrn_lb_table"] + (r + 1) * HT]
            row = lambda r: lbs[:, r * HT:(r + 1) * HT]
            dve.tensor_tensor(row(0), tab(0), tab(1), ALU.max)
            dve.drain()
            dve.tensor_tensor(row(0), row(0), tab(2), ALU.max)
            dve.drain()
            for r in range(3):
                o = dve.tensor_tensor(row(r + 1), tab(r), row(0), ALU.subtract)
            o.then_inc(lb_max, 1)
            for name in on:
                end = name == STAGES[-1][0]
                if name in LNS:
                    occ, ln, layer, nxt = LNS[name]
                    drive(dve, name, split_chunk, dve_residual(), unroll=True, between=dve_between)
                    dve_add(3)
                    dve_mean_var(1 + occ, DM)
                    dve_norm(1 + occ, nxt)
                    if name == "down1":
                        pre_dve(dve)
                elif name.startswith("up"):
                    for pad in (gpad, vpad):
                        dve.memset(pad[:, :, 0:1], 0.0)
                        dve.memset(pad[:, :, T + 1:T + 2], 0.0)
                    dve.drain()
                    between, value = dve_conv(int(name[2]))
                    drive(dve, name, split_chunk, dve_pad, between=between, peel=(1,))
                    value(FG - 1, 1, range(2))
                    value(FG - 1, 2, range(2, 4))
                elif name == "rnn_out":
                    drive(dve, name, split_chunk, dve_gated(0), unroll=end)
                elif name == "dil_out":
                    drive(dve, name, split_chunk, dve_gated(1), unroll=end)
                    merge_dve(dve)
                elif name == "last_out":
                    drive(dve, name, split_chunk, dve_last, unroll=end)
                    final_dve(dve)
                elif name == "mix0_in":
                    dve.wait_ge(con_landed, 48)
                    drive(dve, name, split_chunk, dve_store(FIRST_TILE[name]), between=hgrn_in_dve, unroll=True)
                elif name == "attn_in":
                    dve.wait_ge(at_["con"], 48)
                    drive(dve, name, split_chunk, dve_store(FIRST_TILE[name]), between=norm_turn_dve, peel=(1,))
                elif name == "rnn_in":
                    drive(dve, name, split_chunk, dve_store(FIRST_TILE[name]), between=rnn_dve, unroll=True)
                elif name.startswith("half"):
                    drive(dve, name, split_chunk, dve_store(FIRST_TILE[name]), between=turn_dve(int(name[4])),
                          peel=(1, 3, 4))
                else:
                    drive(dve, name, split_chunk, dve_store(FIRST_TILE[name]), unroll=end)
                if name == "mix0_in":
                    hgrn_dve(dve)
                elif name == "attn_in":
                    attn_dve(dve)
                elif name == "rnn_in":
                    rnn_dve(4, 0, 3)
                    dve.wait_ge(dl["con"], 80)
                elif name.startswith("half"):
                    dil_dve(int(name[4]))(dve)
                elif name == "gates":
                    gates_dve(dve)

        @block.tensor
        def _(pe):
            for name in on:
                if name in ("down0", "down1"):
                    multiply(pe, name, hid_moving, hid_from(int(name[4])))
                elif name == "dil_out":
                    multiply(pe, name, lambda k, a, b: hid[:, FT - HT + k, a:b], ready_from(name))
                elif name.startswith("half"):
                    hf = int(name[4])
                    if hf == 0:
                        pe.wait_ge(dl["con"], 80)
                    multiply(pe, name, x_moving, None, (1, 3, 4), turn_pe(hf), turn_read(hf))
                elif name == "gates":
                    multiply(pe, name, x_moving)
                elif name == "attn_in":
                    pe.wait_ge(at_["con"], 48)
                    multiply(pe, name, x_moving, ready_from(name), (1,), norm_turn_pe, norm_turn_read)
                elif name == "rnn_in":
                    multiply(pe, name, x_moving, ready_from(name), (1, 2, 3), rnn_pe, rnn_read)
                elif name == "mix0_in":
                    multiply(pe, name, x_moving, ready_from(name), range(1, 7), hgrn_in_pe, hgrn_in_read)
                else:
                    multiply(pe, name, x_moving, ready_from(name))
                if name in LNS:
                    pe_sums(pe, 1 + LNS[name][0])
                    if name == "down1":
                        pe_sums(pe, 5)
                elif name == "mix0_in":
                    hgrn_pe(pe)
                elif name == "attn_in":
                    attn_pe(pe)
                elif name.startswith("half"):
                    dil_pe(int(name[4]))(pe)
                elif name == "last_out":
                    pe_sums(pe, 6)


def constants():
    out = np.zeros((P, NCON), np.float32)
    p, t = np.arange(P), np.arange(T)

    def put(name, a):
        a = np.asarray(a, np.float32).reshape(P, -1)
        out[:, CON0[name]:CON0[name] + a.shape[1]] = a

    put("ident", np.eye(P))
    put("seg_start", np.tile((t % SEG != 0), (P, 1)))
    same = p[:, None] // SEG == p[None, :] // SEG
    put("fw_mask", np.tile(same & (p[:, None] <= p[None, :]), (1, 4)))
    put("bw_mask", np.tile(same & (p[:, None] >= p[None, :]), (1, 4)))

    def rope(tag, partner, sign, ang, turned):
        perm = np.zeros((P, P))
        perm[partner[turned], p[turned]] = sign[turned]
        put(tag + "_perm", perm)
        put(tag + "_cos", np.where(turned[:, None], np.cos(ang), 1.0))
        put(tag + "_sin", np.where(turned[:, None], np.sin(ang), 0.0))

    half, n2 = P // 2, P // 4
    inv = np.exp(np.float32(-math.log(10000.0)) * np.arange(0, half, 2, dtype=np.float32) / half).astype(np.float32)
    pos = np.where((p < half)[:, None], (t // 64)[None, :], (t % 64)[None, :]).astype(np.float32)
    first = p % half < n2
    rope("rope1", np.where(first, p + n2, p - n2), np.where(first, -1.0, 1.0),
         pos * inv[p % n2][:, None], np.ones(P, bool))
    rot = P // 4
    inv = np.exp(np.float32(-math.log(500000.0)) * np.arange(rot // 2, dtype=np.float32) * np.float32(2.0 / rot))
    inv = inv.astype(np.float32)
    first = p < rot // 2
    rope("rope2", np.where(first, p + rot // 2, p - rot // 2), np.where(first, -1.0, 1.0),
         t[None, :].astype(np.float32) * inv[p % (rot // 2)][:, None], p < rot)

    def mask(queries, keys):
        gap = queries[:, None] - keys[None, :]
        return [np.where((gap >= 0) & (gap <= w) & (gap % dil == 0), 0.0, -1e30) for w, dil in WINDOWS]
    put("dil_mask0", np.concatenate(mask(p, p), 1))
    put("dil_mask1", np.concatenate(mask(p + P, t), 1))
    return out


def tasks(w, cols=None):
    k, n = w.shape
    a = w.reshape(k // (CK * P), CK, P, n // (CF * P), CF, P).transpose(3, 0, 2, 4, 1, 5)
    return a if cols is None else a[cols]


def kernel(**inputs):
    import concourse.bacc as bacc
    from concourse.bass_utils import run_bass_kernel_spmd

    a = {k: np.asarray(v) for k, v in inputs.items()}
    pairs = [i for g in range(FG) for i in (g, FG + g)]
    win2 = tasks(a["w_in_2"][0])

    def half(h):
        return [first + 2 * g + h for first in (8, 14, 20) for g in range(3)] + [26 + h]
    first = [2, 3, 4, 5, 12, 13, 6, 7, 10, 11, 0, 1, 8, 9]
    parts = [tasks(a["w_in_ab"][0], first), tasks(a["w_out_ab"][0]), tasks(a["ffn_up"][0], pairs), tasks(a["ffn_down"][0]),
             tasks(a["w_in_attn"][0]), tasks(a["w_out_attn"][0]), tasks(a["ffn_up"][1], pairs),
             tasks(a["ffn_down"][1]), win2[0:8], win2[half(0)], win2[half(1)], win2[28:36],
             tasks(a["w_rnn_out_2"][0]), tasks(a["w_attn_out_2"][0]), tasks(a["w_o_2"][0])]
    weights = np.concatenate([x.reshape(-1, P, CHUNK) for x in parts])
    assert weights.shape[0] == NCHUNKS

    def by_feature(x):
        return np.ascontiguousarray(x.reshape(T, MT, P).transpose(2, 1, 0))
    a["qk_norm_g"] = np.concatenate([a["q_norm_g"]] * 8 + [a["k_norm_g"]] * 2)
    par = np.concatenate([a[name].reshape(-1, P) for name, _ in PARS])
    assert par.shape[0] == NPAR
    arrays = {
        "x": by_feature(a["x"][0]),
        "weights": weights,
        "par": np.ascontiguousarray(par.T),
        "con": constants(),
        "gmlp_ws": np.ascontiguousarray(a["gmlp_ws"][0].transpose(2, 0, 1)),
        "gmlp_bias": np.ascontiguousarray(a["gmlp_bias"].reshape(1, HT * P)),
        "w_gates": np.ascontiguousarray(np.stack([a["w_rg_2"][0], a["w_ig_2"][0]]).transpose(2, 0, 1, 3)),
    }
    nc = bacc.Bacc("TRN2", target_bir_lowering=False, num_devices=1)
    d = {k: nc.dram_tensor(k + "_dram", v.shape, F32, kind="ExternalInput").ap() for k, v in arrays.items()}
    d["out"] = nc.dram_tensor("out_dram", (P, MT, T), F32, kind="ExternalOutput").ap()
    program(nc, d)
    r = run_bass_kernel_spmd(nc, [{k + "_dram": v for k, v in arrays.items()}], core_ids=[0])
    out = r.results[0]["out_dram"]
    return np.ascontiguousarray(out.transpose(2, 1, 0)).reshape(1, T, DM)
```

```python
import math
from contextlib import ExitStack

import numpy as np

import concourse.bass as bass
from concourse import mybir
from concourse.alu_op_type import AluOpType as ALU

F32 = mybir.dt.float32
F32R = mybir.dt.float32r
I32 = mybir.dt.int32
ACT = mybir.ActivationFunctionType
AX = mybir.AxisListType.X

P = 128
T = 256
DM = 2048
MT = DM // P
FF = 5632
FT = FF // P
FG = FT // 4
HT = 1024 // P
CK, CF = 4, 4
CHUNK = CK * CF * P
ALPHA = (2.0 * 2) ** 0.25
LN_EPS, RMS_EPS = 1e-5, 1e-6
SEG = 64
NSEG = T // SEG
LRU_C = 8.0
WINDOWS = ((128, 1), (512, 4), (2048, 16))

STAGES = [("mix0_in", 14, 4), ("mix0_out", 4, 4),
          ("up0", 2 * FG, 4), ("down0", 4, FT // CK),
          ("attn_in", 6, 4), ("attn_out", 4, 4),
          ("up1", 2 * FG, 4), ("down1", 4, FT // CK),
          ("rnn_in", 8, 4), ("half0", 10, 4), ("half1", 10, 4), ("gates", 8, 4),
          ("dil_out", 4, 2), ("rnn_out", 4, 4), ("last_out", 4, 4)]
TASK0, CHUNK0, NTASK, NCHUNK_OF = {}, {}, {}, {}
_t = _c = 0
for _name, _n, _k in STAGES:
    TASK0[_name], CHUNK0[_name], NTASK[_name], NCHUNK_OF[_name] = _t, _c, _n, _k
    _t += _n
    _c += _n * _k
NCHUNKS = _c

_READY = ["mix0_in", "mix0_out", "up0", "attn_in", "attn_out", "up1", "rnn_in"]
READY0 = {n: 4 * i for i, n in enumerate(_READY)}
READY0["dil_out"] = 4 * len(_READY)
READY0["rnn_out"] = READY0["dil_out"] + 2
READY0["last_out"] = READY0["rnn_out"] + 4

PARS = [("hgrn_lb_table", 3 * HT), ("hgrn_norm_g", HT), ("gmlp_ln_g", HT), ("gmlp_ln_b", HT),
        ("qk_norm_g", (16 + 4) // 2),
        ("ln1_g", 2 * MT), ("ln1_b", 2 * MT), ("ln2_g", 2 * MT), ("ln2_b", 2 * MT),
        ("ffn_conv_w", 2 * 3 * 2 * FT), ("ffn_conv_b", 2 * 2 * FT),
        ("ln_pre_g_2", MT), ("conv_w_2", 4 * MT), ("conv_b_2", MT), ("b_rg_2", MT), ("b_ig_2", MT),
        ("lru_lambda_2", MT), ("ln_post_g_2", MT)]
PAR0, _c = {}, 0
for _name, _n in PARS:
    PAR0[_name] = _c
    _c += _n
NPAR = _c

CONS = [("ident", P), ("seg_start", T), ("fw_mask", 4 * P), ("bw_mask", 4 * P),
        ("rope1_perm", P), ("rope1_cos", T), ("rope1_sin", T),
        ("rope2_perm", P), ("rope2_cos", T), ("rope2_sin", T),
        ("dil_mask0", 3 * P), ("dil_mask1", 3 * T)]
CON0, _c = {}, 0
for _name, _n in CONS:
    CON0[_name] = _c
    _c += _n
NCON = _c


def program(nc, d):
    ctx = ExitStack()
    with ctx:
        base = (nc.sbuf_base + 63) // 64 * 64
        at = [base]

        def place(name, shape, dt=F32, offset=None):
            size = 4 * int(np.prod(shape[1:]))
            if offset is None:
                offset = at[0]
                at[0] += (size + 31) // 32 * 32
            return nc.alloc_sbuf_tensor_at(name, shape, dt, offset=offset)

        raw = place("w_raw", [P, 2, CHUNK])
        whi = place("w_hi", [P, 2, CHUNK], F32R)
        wlo = place("w_lo", [P, 2, CHUNK], F32R)
        X0 = at[0]
        xhl = place("x_hi_lo", [P, MT, 2 * T], F32R)
        z = place("resid", [P, MT, T])
        U0 = at[0]
        hid = place("hidden_hi_lo", [P, FT, 2 * T], F32R)
        u = place("u_tiles", [P, 2 * FT, T], F32, U0)
        W0 = at[0]
        WSIZE = 4 * 4 * (T + 2) * 2 + 2 * 4 * 4 * T
        at[0] += WSIZE
        par = place("par", [P, NPAR])
        ident = place("ident", [P, P])
        ones = place("ones", [P, P])
        eps = place("eps", [P, 8])
        lbs = place("lower_bound", [P, 4 * HT])
        nrg = place("rnn_cols", [P, 4 * MT])
        sbuf_end = at[0]
        assert sbuf_end <= nc.sbuf_usable_end, (sbuf_end, nc.sbuf_usable_end)
        fence = ctx.enter_context(nc.sbuf_tensor("fence", [P, (sbuf_end - nc.sbuf_base + 3) // 4], F32))

        names = [0]

        def over(start, pieces):
            out, o = [], start
            for shape in pieces:
                names[0] += 1
                out.append(place(f"over{names[0]}", shape, F32, o))
                o += (4 * int(np.prod(shape[1:])) + 31) // 32 * 32
            return out, o

        acc = ctx.enter_context(nc.psum_tensor("acc", [P, 8, 2 * T], F32))

        (gpad, vpad, gconv, vconv), end = over(W0, [[P, 4, T + 2], [P, 4, T + 2], [P, 4, T], [P, 4, T]])
        assert end <= W0 + WSIZE
        (zsum, mu, var, rstd, etmp, esq), end = over(
            W0, [[P, 2 * T], [P, T], [P, T], [P, T], [P, 4, T], [P, 4, T]])
        assert end <= W0 + WSIZE

        def sem(name):
            return ctx.enter_context(nc.semaphore(name))

        raw_landed = [sem("raw_landed0"), sem("raw_landed1")]
        weights_hi = sem("weights_hi")
        weights_split = sem("weights_split")
        chunk_used = sem("chunk_used")
        acc_free = sem("acc_free")
        moving_ready = sem("moving_ready")
        x_landed = [sem("x_landed%d" % q) for q in range(4)]
        par_landed = sem("par_landed")
        con_landed = sem("con_landed")
        consts_ready = sem("consts_ready")
        lb_exp = sem("lb_exp")
        lb_max = sem("lb_max")
        x_hi = sem("x_hi")
        z_ready = sem("z_ready")
        sq_ready = sem("sq_ready")
        sq_used = sem("sq_used")
        partials = sem("partials")
        mean_sums = sem("mean_sums")
        sums_ready = sem("sums_ready")
        var_ready = sem("var_ready")
        rstd_ready = sem("rstd_ready")
        norm_ready = sem("norm_ready")
        out_ready = [sem("out_ready%d" % q) for q in range(4)]
        out_stored = sem("out_stored")

        block = ctx.enter_context(nc.Block())

        on = [name for name, _, _ in STAGES]

        def col(name, i=0, n=1):
            return par[:, bass.ds(PAR0[name] + i, n)]

        def loop(eng, trips, unroll=False):
            if trips == 1 or unroll:
                yield from range(trips)
            else:
                with eng.Fori(0, trips) as i:
                    yield i

        def cast_chunk(act, n, slot):
            act.wait_ge(raw_landed[slot], 16 * (n // 2 + 1) if isinstance(n, int) else n * 8 + (16 - 8 * slot))
            if not isinstance(n, int) or n >= 2:
                act.wait_ge(chunk_used, n - 1)
            nc.scalar.activation(whi[:, slot, :], raw[:, slot, :], ACT.Copy).then_inc(weights_hi, 1)

        def split_chunk(dve, n, slot):
            dve.wait_ge(weights_hi, n + 1)
            nc.vector.tensor_tensor(wlo[:, slot, :], raw[:, slot, :], whi[:, slot, :].bitcast(F32),
                                    ALU.subtract).then_inc(weights_split, 1)

        def drive(eng, name, piece, after_task, unroll=False, between=None, peel=()):
            per, nch = 2, NCHUNK_OF[name]

            for i in spans(eng, name, peel, unroll):
                for t in range(per):
                    for c in range(1, nch):
                        at_c = t * nch + c
                        n = CHUNK0[name] + i * (per * nch) + at_c
                        if not isinstance(n, int) or n + 1 < NCHUNKS:
                            piece(eng, n + 1, (at_c + 1) % 2)
                        if between:
                            between(i, t, c)
                        if c == nch - 1:
                            last = t == 1 and isinstance(i, int) and i == NTASK[name] // 2 - 1
                            if last and after_task:
                                after_task(i, t, TASK0[name] + i * per + t, n)
                            if not isinstance(n, int) or n + 2 < NCHUNKS:
                                piece(eng, n + 2, at_c % 2)
                            if not last and after_task:
                                after_task(i, t, TASK0[name] + i * per + t, n)

        def spans(eng, name, cuts, unroll=False):
            cuts = [0, *cuts, NTASK[name] // 2]
            for lo, hi in zip(cuts, cuts[1:]):
                if unroll or hi - lo == 1:
                    yield from range(lo, hi)
                else:
                    with eng.Fori(lo, hi) as i:
                        yield i

        def multiply(pe, name, moving, ready=None, cuts=(), extra=None, banks_read=None):
            per, nch = 2, NCHUNK_OF[name]
            for i in spans(pe, name, cuts):
                for t in range(per):
                    pe.wait_ge(acc_free, TASK0[name] + i * per + t + 1)
                    if banks_read:
                        banks_read(i, t)
                    for c in range(nch):
                        at_c = t * nch + c
                        s = at_c % 2
                        if extra:
                            extra(i, t, c)
                        if t == 0 and ready:
                            ready(pe, c)
                        pe.wait_ge(weights_split, CHUNK0[name] + i * (per * nch) + at_c + 1)
                        for f in range(CF):
                            bank = 4 * t + f
                            for kk in range(CK):
                                k = CK * c + kk
                                w0 = (f * CK + kk) * P
                                both = (acc[:, bank, :], whi[:, s, w0:w0 + P], moving(k, 0, 2 * T))
                                rest = (acc[:, bank, 0:T], wlo[:, s, w0:w0 + P], moving(k, 0, T))
                                if k == 0:
                                    nc.tensor.matmul(*both, start=True, stop=False)
                                    last = nc.tensor.matmul(*rest, start=False, stop=False)
                                else:
                                    nc.tensor.matmul(*rest, start=False, stop=False)
                                    last = nc.tensor.matmul(*both, start=False,
                                                            stop=(k == CK * nch - 1))
                        last.then_inc(chunk_used, 1)

        def x_moving(k, a, b):
            return xhl[:, k, a:b]

        def hid_moving(k, a, b):
            return hid[:, k, a:b]

        def ready_from(name):
            def ready(pe, c):
                pe.wait_ge(moving_ready, READY0[name] + c + 1)
            return ready

        def halves(bank):
            return acc[:, bank, :].rearrange("p (h n) -> p n h", h=2)

        def read_out(dst, bank):
            return nc.vector.tensor_reduce(dst, halves(bank), AX, ALU.add)

        def dve_store(first_tile):
            def after(i, t, task, n):
                nc.vector.wait_ge(chunk_used, n + 1)
                for f in range(CF):
                    o = read_out(u[:, bass.ds(first_tile + i * 8 + t * 4 + f, 1), :].squeeze(1), 4 * t + f)
                o.then_inc(acc_free, 1)
            return after

        def dve_residual():
            def after(i, t, task, n):
                nc.vector.wait_ge(chunk_used, n + 1)
                for f in range(CF):
                    o = read_out(etmp[:, f, :], 4 * t + f)
                o.then_inc(acc_free, 1)
                if (i, t) == (1, 1):
                    dve_add(3)
            return after

        def dve_add(m):
            zt = z[:, 4 * m:4 * m + 4, :]
            nc.vector.drain()
            nc.vector.scalar_tensor_tensor(zt, zt, ALPHA, etmp[:], ALU.mult, ALU.add).then_inc(z_ready, 1)

        def dve_between(i, t, c):
            if c == 1 and i + t:
                dve_add(2 * i + t - 1)

        def act_square(occ, m, src):
            n = 4 * occ + m
            if occ < 4:
                nc.scalar.wait_ge(z_ready, n + 1)
            else:
                nc.scalar.wait_ge(acc_free, TASK0["last_out"] + m + 3)
            nc.scalar.wait_ge(sq_used, n + 1)
            nc.scalar.activation(esq[:], src[:, 4 * m:4 * m + 4, :], ACT.Square).then_inc(sq_ready, 1)

        def act_between(occ, src):
            def between(i, t, c):
                if c == 2 and i + t:
                    act_square(occ, 2 * i + t - 1, src)
            return between

        def pool_sums(occ, src):
            pool = nc.gpsimd
            if occ == 5:
                pool.wait_ge(acc_free, TASK0["last_out"] + 3)
            else:
                pool.wait_ge(z_ready, 4 * occ + 1)
            pool.memset(zsum[:], 0.0)
            pool.drain()
            for t in range(3):
                pool.wait_ge(sq_ready, 4 * occ + t + 1)
                for f in range(4):
                    if src is not None:
                        pool.tensor_tensor(zsum[:, 0:T], zsum[:, 0:T], src[:, 4 * t + f, :], ALU.add)
                    pool.tensor_tensor(zsum[:, T:2 * T], zsum[:, T:2 * T], esq[:, f, :], ALU.add)
                    pool.drain()
                pool.engine_nop().then_inc(sq_used, 1)
            pool.engine_nop().then_inc(partials, 1)
            pool.wait_ge(sums_ready, occ + 2)
            pool.engine_nop().then_inc(sq_used, 1)

        def pe_sums(pe, s):
            pe.wait_ge(partials, s + 1)
            nc.tensor.matmul(acc[:, 0, :], ones[:], zsum[:], start=True, stop=True).then_inc(sums_ready, 1)

        def keep_clock(pe, n):
            for _ in range(n):
                pe.matmul(acc[:, 2, 0:P], ones[:], ones[:], start=True, stop=True)

        def pe_norm_sums(pe, occ, src):
            pe.wait_ge(partials, occ + 2 if occ < 4 else occ + 1)
            pe.matmul(acc[:, 1, 0:T], ones[:], zsum[:, T:2 * T], start=True, stop=False)
            if src is not None:
                pe.matmul(acc[:, 0, 0:T], ones[:], zsum[:, 0:T], start=True, stop=False)
            keep_clock(pe, 10)
            if src is not None:
                pe.wait_ge(z_ready, 4 * occ + 4)
                for m in range(12, 16):
                    o = pe.matmul(acc[:, 0, 0:T], ones[:], src[:, m, :], start=False, stop=(m == 15))
                o.then_inc(mean_sums, 1)
            pe.wait_ge(sq_ready, 4 * occ + 4)
            for f in range(4):
                o = pe.matmul(acc[:, 1, 0:T], ones[:], esq[:, f, :], start=False, stop=(f == 3))
            o.then_inc(sums_ready, 1)
            if occ < 3:
                keep_clock(pe, 32)

        def pe_square_sums(pe):
            for q in range(4):
                pe.wait_ge(sq_ready, 16 + q + 1)
                for f in range(4):
                    o = pe.matmul(acc[:, 0, 0:T], ones[:], esq[:, f, :], start=(q + f == 0), stop=(q + f == 6))
                o.then_inc(sq_used if q < 3 else sums_ready, 1)
            keep_clock(pe, 32)

        def dve_mean_var(s, width):
            dve = nc.vector
            if s:
                dve.wait_ge(mean_sums, s)
            else:
                dve.wait_ge(sums_ready, s + 1)
            dve.tensor_scalar(mu[:], acc[:, 0, 0:T], 1.0 / width, None, ALU.mult)
            dve.drain()
            dve.tensor_tensor(rstd[:], mu[:], mu[:], ALU.mult)
            dve.drain()
            if s:
                dve.tensor_tensor(z[:, 0:4, :], z[:, 0:4, :], wide(mu[:], 4), ALU.subtract)
                dve.wait_ge(sums_ready, s + 1)
            dve.scalar_tensor_tensor(var[:], acc[:, 1, 0:T] if s else acc[:, 0, T:2 * T], 1.0 / width, rstd[:], ALU.mult, ALU.subtract)
            dve.drain()
            dve.tensor_scalar(var[:], var[:], 0.0, LN_EPS, ALU.max, ALU.add)
            dve.drain()
            dve.reciprocal(var[:], var[:]).then_inc(var_ready, 1)

        def dve_rms(s, width, src):
            dve = nc.vector
            dve.wait_ge(sums_ready, s + 1)
            dve.tensor_scalar(var[:], src, 1.0 / width, RMS_EPS, ALU.mult, ALU.add)
            dve.drain()
            dve.reciprocal(var[:], var[:]).then_inc(var_ready, 1)

        def act_rstd(s):
            act = nc.scalar
            act.wait_ge(var_ready, s + 1)
            act.activation(rstd[:], var[:], ACT.Sqrt).then_inc(rstd_ready, 1)

        def wide(t2, n):
            return t2.unsqueeze(1).to_broadcast([P, n, T])

        def lo_part(dve, q, src, count, dst=None):
            dst = xhl[:, 4 * q:4 * q + 4, :] if dst is None else dst
            dve.wait_ge(x_hi, count)
            nc.vector.tensor_tensor(dst[:, :, T:2 * T], src, dst[:, :, 0:T].bitcast(F32), ALU.subtract)\
                .then_inc(moving_ready, 1)

        def hi_part(act, q, src, dst=None):
            dst = xhl[:, 4 * q:4 * q + 4, :] if dst is None else dst
            nc.scalar.activation(dst[:, :, 0:T], src, ACT.Copy).then_inc(x_hi, 1)

        def dve_norm(occ, nxt):
            dve = nc.vector
            for q in range(4):
                zq = z[:, 4 * q:4 * q + 4, :]
                if q == 0:
                    dve.wait_ge(rstd_ready, occ + 2)
                else:
                    dve.tensor_tensor(zq, zq, wide(mu[:], 4), ALU.subtract)
                    dve.drain()
                dve.tensor_tensor(zq, zq, wide(rstd[:], 4), ALU.mult).then_inc(norm_ready, 1)
                if nxt and q:
                    lo_part(dve, q - 1, z[:, 4 * q - 4:4 * q, :], READY0[nxt] + q)

        def act_affine(occ, g, b, nxt, off, quarters):
            act = nc.scalar
            for q in quarters:
                zq = z[:, 4 * q:4 * q + 4, :]
                act.wait_ge(norm_ready, 4 * occ + q + 1)
                for m in range(4 * q, 4 * q + 4):
                    act.activation(z[:, m, :], z[:, m, :], ACT.Identity,
                                   bias=col(b, off + m), scale=col(g, off + m))
                act.drain()
                if nxt:
                    hi_part(act, q, zq)
                else:
                    m = 16 + q
                    act.wait_ge(sq_used, m + 1)
                    act.activation(esq[:], zq, ACT.Square).then_inc(sq_ready, 1)

        NORM_BEFORE = {"up0": (0, "ln1", 0), "attn_in": (1, "ln2", 0), "up1": (2, "ln1", 1)}

        def late_act(name, between):
            def run(i, t, c):
                if isinstance(i, int) and (i, t, c) == (0, 0, 1):
                    occ, ln, layer = NORM_BEFORE[name]
                    act_affine(occ, ln + "_g", ln + "_b", name, layer * MT, (3,))
                if between:
                    between(i, t, c)
            return run

        def late_dve(name, between):
            def run(i, t, c):
                if isinstance(i, int) and (i, t, c) == (0, 0, 1):
                    lo_part(nc.vector, 3, z[:, 12:16, :], READY0[name] + 4)
                between(i, t, c)
            return run

        gate_conv = sem("gate_conv")
        val_conv = sem("val_conv")
        gate_silu = sem("gate_silu")
        hid_ready = sem("hid_ready")

        def conv(layer, pad, out, i, val, tiles):
            dve = nc.vector
            w0 = PAR0["ffn_conv_w"] + layer * 3 * 2 * FT + val * FT
            b0 = PAR0["ffn_conv_b"] + layer * 2 * FT + val * FT

            def c(first, f):
                return par[:, bass.ds(first + i * 4 + f, 1)]
            for f in tiles:
                dve.tensor_scalar(out[:, f, :], pad[:, f, 1:T + 1], c(w0 + 2 * FT, f), c(b0, f),
                                  ALU.mult, ALU.add)
            for j in (0, 2):
                dve.drain()
                for f in tiles:
                    o = dve.scalar_tensor_tensor(out[:, f, :], pad[:, f, j:j + T], c(w0 + j * 2 * FT, f),
                                                 out[:, f, :], ALU.mult, ALU.add)
            return o

        def dve_pad(i, t, task, n):
            nc.vector.wait_ge(chunk_used, n + 1)
            for f in range(CF):
                o = read_out((vpad if t else gpad)[:, f, 1:T + 1], 4 * t + f)
            o.then_inc(acc_free, 1)

        def dve_conv(layer):
            def between(i, t, c):
                if c > 2:
                    return
                tiles = range(2 * c - 2, 2 * c)
                if t == 1:
                    if c == 1:
                        nc.vector.drain()
                        nc.vector.wait_ge(hid_ready, layer * FG + i + 1)
                    o = conv(layer, gpad, gconv, i, 0, tiles)
                    if c == 2:
                        o.then_inc(gate_conv, 1)
                elif not isinstance(i, int) or i > 0:
                    value(i - 1, c, tiles)

            def value(i, c, tiles):
                if c == 1:
                    nc.vector.drain()
                o = conv(layer, vpad, vconv, i, 1, tiles)
                if c == 2:
                    o.then_inc(val_conv, 1)
            return between, value

        def act_silu(layer):
            def after(i, t, task, n):
                if t == 1:
                    nc.scalar.wait_ge(gate_conv, layer * FG + i + 1)
                    nc.scalar.activation(gconv[:], gconv[:], ACT.Silu).then_inc(gate_silu, 1)
            return after

        def pool_hidden(layer):
            pool = nc.gpsimd
            for i in loop(pool, FG):
                pool.wait_ge(gate_silu, layer * FG + i + 1)
                pool.wait_ge(val_conv, layer * FG + i + 1)
                pool.tensor_tensor(vconv[:], vconv[:], gconv[:], ALU.mult)
                pool.drain()
                pool.tensor_copy(hid[:, bass.ds(i * 4, 4), 0:T], vconv[:])
                pool.drain()
                pool.tensor_tensor(hid[:, bass.ds(i * 4, 4), T:2 * T], vconv[:],
                                   hid[:, bass.ds(i * 4, 4), 0:T].bitcast(F32), ALU.subtract)\
                    .then_inc(hid_ready, 1)

        def hid_from(layer):
            def ready(pe, c):
                pe.wait_ge(hid_ready, layer * FG + c + 2)
            return ready

        F0, V0, I0, UU0, Q0, G0, K0, L0 = 0, 2 * HT, 3 * HT, 4 * HT, 5 * HT, 6 * HT, 7 * HT, 9 * HT
        VT0, IT0, QT0, GT0 = V0 // 4, I0 // 4, Q0 // 4, G0 // 4
        (qmid, prob, state, decay, bwm), end = over(
            X0, [[P, 2, 4, T], [P, 2, 8, P], [P, 2, 4 * 3, P], [P, 2 * HT, NSEG], [P, 4, P]])
        assert end <= X0 + 4 * MT * 2 * T
        osq = u[:, V0:V0 + HT, :]
        (_, seg1, fwm), end = over(W0, [[P, 2 * T + 3 * T + 8 * T], [P, T], [P, 4, P]])
        assert end <= W0 + WSIZE
        (_, gm_bias, gm_ws), _ = over(W0, [[P, 2 * T + 3 * T], [P, HT * P], [P, HT, P]])

        hg = {n: sem("hg_" + n) for n in (
            "sig", "gate", "key", "log", "diff", "exp", "klast", "kmid", "ktok_ps", "ktok", "vtok_ps", "vtok",
            "silu", "masks", "zeroed", "qdiff", "qexp", "qmid", "cumexp", "qcum", "kv_ps", "state", "score_ps", "prob",
            "out_ps", "out", "sq", "ms_ps", "rn", "done")}
        gm = {n: sem("gm_" + n) for n in ("sq", "summed", "norm", "affine", "tok_ps", "tok", "con", "out_ps", "done")}

        def pcol(name, off=0):
            return par[:, PAR0[name] + off:PAR0[name] + off + 1]

        def flat(x):
            return x.rearrange("p a n -> p (a n)")

        def utile(first, n, i):
            return u[:, bass.ds(i * n + first, n), :]

        def tiles(first, n=4):
            return u[:, first:first + n, :]

        def segs(t3):
            return t3.rearrange("p a (s c) -> p (a s) c", c=SEG)

        def seg_point(t3, point):
            n = t3.shape[1] * NSEG
            return segs(t3)[:, :, point:point + 1].to_broadcast([P, n, SEG])

        POINTS = ((SEG // 2 - 1, SEG - 1), (SEG // 2, 0))

        def hgrn_in_act(i, t, c):
            act, task, b0 = nc.scalar, 2 * i + t, 4 * (1 - t)
            j = task - 1
            if c == 1 and task == 0:
                act.wait_ge(lb_max, 1)
                act.activation(lbs[:, HT:4 * HT], lbs[:, HT:4 * HT], ACT.Exp).then_inc(lb_exp, 1)
            if c == 1 and 0 <= j < 4:
                act.wait_ge(acc_free, j + 3)
                act.activation(tiles(F0 + 4 * j), tiles(F0 + 4 * j), ACT.Sigmoid).then_inc(hg["sig"], 1)
            if c == 1 and VT0 <= j < VT0 + 2:
                act.wait_ge(acc_free, j + 3)
                if j > VT0:
                    act.wait_ge(gm["summed"], 1)
                act.activation(esq[:], tiles(4 * j), ACT.Square).then_inc(gm["sq"], 1)
            if c == 2 and 0 <= task - 3 < 4:
                k = task - 3
                act.wait_ge(hg["ktok_ps"], k + 1)
                for b in range(2):
                    o = act.activation(flat(tiles(L0 + 4 * k + 2 * b, 2)), acc[:, b0 + b, :], ACT.Copy)
                o.then_inc(hg["ktok"], 1)
            if c == 3 and 0 <= j < 4:
                act.wait_ge(hg["key"], j + 1)
                act.activation(tiles(F0 + 4 * j), tiles(F0 + 4 * j), ACT.Ln).then_inc(hg["log"], 1)
            if c == 3 and 0 <= task - 2 < 4:
                k = task - 2
                act.wait_ge(hg["diff"], k + 1)
                act.activation(tiles(L0 + 4 * k), tiles(L0 + 4 * k), ACT.Exp)
                act.activation(etmp[:], etmp[:], ACT.Exp).then_inc(hg["exp"], 1)
            if c == 3 and IT0 <= j < IT0 + 2:
                act.wait_ge(hg["vtok_ps"], j - IT0 + 1)
                for b in range(2):
                    o = act.activation(flat(tiles(4 * j + 2 * b, 2)), acc[:, b0 + 2 + b, :], ACT.Copy)
                o.then_inc(hg["vtok"], 1)
            if c == 3 and task == 7:
                act_rstd(0)
            if c == 1 and task == 8:
                act.wait_ge(partials, 1)
                act.wait_ge(hg["kmid"], 4)
                act.dma_start(gm_ws[:], d["gmlp_ws"]).then_inc(gm["con"], 16)
                act.dma_start(gm_bias[0:1, :], d["gmlp_bias"]).then_inc(gm["con"], 16)
            if c == 3 and task == 8:
                act.wait_ge(gm["norm"], 1)
                for m in range(HT):
                    o = act.activation(u[:, V0 + m, :], u[:, V0 + m, :], ACT.Identity,
                                       bias=pcol("gmlp_ln_b", m), scale=pcol("gmlp_ln_g", m))
                o.then_inc(gm["affine"], 1)
            if c == 3 and task == 9:
                act.wait_ge(gm["tok_ps"], 1)
                for b in range(4):
                    o = act.activation(flat(tiles(V0 + 2 * b, 2)), acc[:, b0 + b, :], ACT.Copy)
                o.then_inc(gm["tok"], 1)
            if c == 1 and GT0 <= j < GT0 + 2:
                act.wait_ge(acc_free, j + 3)
                act.activation(tiles(4 * j), tiles(4 * j), ACT.Silu).then_inc(hg["silu"], 1)

        def hgrn_in_dve(i, t, c):
            dve, task, b0 = nc.vector, 2 * i + t, 4 * (1 - t)
            j, k = task - 1, task - 2
            if c == 1 and task == 1:
                row = lambda r: lbs[:, r * HT:(r + 1) * HT]
                dve.wait_ge(lb_exp, 1)
                dve.tensor_tensor(row(0), row(1), row(2), ALU.add)
                dve.drain()
                dve.tensor_tensor(row(0), row(0), row(3), ALU.add)
                dve.drain()
                dve.reciprocal(row(0), row(0))
                dve.drain()
                dve.tensor_tensor(row(0), row(0), row(1), ALU.mult)
                dve.drain()
                dve.tensor_scalar(row(1), row(0), -1.0, 1.0, ALU.mult, ALU.add)
                dve.drain()
            if c == 1 and 0 <= k < 4:
                way = slice(None) if k < 2 else slice(None, None, -1)
                dve.wait_ge(hg["log"], k + 1)
                for m in range(4 * k, 4 * k + 4):
                    dve.tensor_tensor_scan(u[:, F0 + m, way], seg1[:], u[:, F0 + m, way], 0.0, ALU.mult, ALU.add)
                dve.drain()
                f = tiles(F0 + 4 * k)
                dve.tensor_tensor(segs(tiles(L0 + 4 * k)), seg_point(f, POINTS[k // 2][1]), segs(f), ALU.subtract)
            if c == 2 and 0 <= j < 4:
                dve.wait_ge(hg["sig"], j + 1)
                for m in range(4 * j, 4 * j + 4):
                    h = m % HT
                    o = dve.tensor_scalar(u[:, F0 + m, :], u[:, F0 + m, :], lbs[:, HT + h:HT + h + 1],
                                          lbs[:, h:h + 1], ALU.mult, ALU.add)
                o.then_inc(hg["gate"], 1)
            if c == 2 and 0 <= k < 4:
                if k:
                    dve.wait_ge(hg["kmid"], k)
                f = tiles(F0 + 4 * k)
                dve.tensor_tensor(segs(etmp[:]), seg_point(f, POINTS[k // 2][0]), segs(f), ALU.subtract)\
                   .then_inc(hg["diff"], 1)
            if c == 3 and task == 7:
                dve_mean_var(0, HT * P)
            if c == 1 and task == 8:
                dve.drain()
                dve.tensor_tensor(tiles(V0, HT), tiles(V0, HT), wide(mu[:], HT), ALU.subtract)
            if c == 2 and task == 8:
                dve.drain()
                dve.wait_ge(rstd_ready, 1)
                dve.tensor_tensor(tiles(V0, HT), tiles(V0, HT), wide(rstd[:], HT), ALU.mult).then_inc(gm["norm"], 1)
            if c == 3 and task == 11:
                dve.wait_ge(gm["out_ps"], 1)
                for b in range(4):
                    o = dve.tensor_tensor(flat(tiles(UU0 + 2 * b, 2)), flat(tiles(UU0 + 2 * b, 2)),
                                          acc[:, b0 + b, :], ALU.mult)
                o.then_inc(gm["done"], 1)

        def hgrn_in_pool(pool):
            pool.memset(zsum[:], 0.0)
            for task in range(1, VT0 + 3):
                j, k = task - 1, task - 2
                if j < 4:
                    pool.wait_ge(hg["gate"], j + 1)
                    pool.tensor_scalar(tiles(K0 + 4 * j), tiles(F0 + 4 * j), -1.0, 1.0, ALU.mult, ALU.add)\
                        .then_inc(hg["key"], 1)
                if 0 <= k < 4:
                    pool.drain()
                    pool.wait_ge(hg["exp"], k + 1)
                    pool.tensor_tensor(tiles(L0 + 4 * k), tiles(L0 + 4 * k), tiles(K0 + 4 * k), ALU.mult)\
                        .then_inc(hg["klast"], 1)
                    pool.drain()
                    pool.tensor_tensor(tiles(K0 + 4 * k), tiles(K0 + 4 * k), etmp[:], ALU.mult)\
                        .then_inc(hg["kmid"], 1)
                if VT0 <= j < VT0 + 2:
                    pool.drain()
                    pool.wait_ge(gm["sq"], j - VT0 + 1)
                    for f in range(4):
                        pool.tensor_tensor(zsum[:, 0:T], zsum[:, 0:T], u[:, 4 * j + f, :], ALU.add)
                        pool.tensor_tensor(zsum[:, T:2 * T], zsum[:, T:2 * T], esq[:, f, :], ALU.add)
                        pool.drain()
                    pool.engine_nop().then_inc(gm["summed"], 1)
            pool.engine_nop().then_inc(partials, 1)

        def hgrn_in_pe(i, t, c):
            pe, task, b0 = nc.tensor, 2 * i + t, 4 * (1 - t)
            if c != 2:
                return
            j, k = task - 1, task - 3
            if 0 <= k < 4 or task == 7 or task == 9 or task == 11 or IT0 <= j < IT0 + 2:
                pe.wait_ge(acc_free, task + 2)
            if 0 <= k < 4:
                if k == 0:
                    pe.wait_ge(con_landed, 48)
                pe.wait_ge(hg["klast"], k + 1)
                for f in range(4):
                    for b in range(2):
                        x = 2 * f + b
                        o = pe.transpose(acc[:, b0 + x // 4, (x % 4) * P:(x % 4 + 1) * P],
                                         u[:, L0 + 4 * k + f, b * P:(b + 1) * P], ident[:])
                o.then_inc(hg["ktok_ps"], 1)
            if task == 7:
                pe_sums(pe, 0)
            if IT0 <= j < IT0 + 2:
                for f in range(4):
                    for b in range(2):
                        x = 2 * f + b
                        o = pe.transpose(acc[:, b0 + 2 + x // 4, (x % 4) * P:(x % 4 + 1) * P],
                                         u[:, 4 * j + f, b * P:(b + 1) * P], ident[:])
                o.then_inc(hg["vtok_ps"], 1)
            if task == 9:
                pe.wait_ge(gm["affine"], 1)
                for x in range(2 * HT):
                    o = pe.transpose(acc[:, b0 + x // 4, (x % 4) * P:(x % 4 + 1) * P],
                                     u[:, V0 + x // 2, (x % 2) * P:(x % 2 + 1) * P], ident[:])
                o.then_inc(gm["tok_ps"], 1)
            if task == 11:
                pe.wait_ge(gm["con"], 32)
                for m in range(HT):
                    for n in range(2):
                        dst = acc[:, b0 + m // 2, (m % 2) * T + n * P:(m % 2) * T + (n + 1) * P]
                        pe.matmul(dst, ones[0:1, :], gm_bias[0:1, m * P:(m + 1) * P], start=True, stop=False)
                        o = pe.matmul(dst, u[:, V0 + m, n * P:(n + 1) * P], gm_ws[:, m, :], start=False, stop=True)
                o.then_inc(gm["out_ps"], 1)

        def hgrn_in_read(i, t):
            pe, task = nc.tensor, 2 * i + t
            if 0 <= task - 4 < 4:
                pe.wait_ge(hg["ktok"], task - 3)
            if IT0 <= task - 2 < IT0 + 2:
                pe.wait_ge(hg["vtok"], task - 1 - IT0)
            if task == 8:
                pe.wait_ge(var_ready, 1)
            if task == 10:
                pe.wait_ge(gm["tok"], 1)
            if task == 12:
                pe.wait_ge(gm["done"], 1)

        NG = HT // 2
        kv_order = [[(a, sg) for a in range(4) for sg in ((0, 1, 2) if a < 2 else (3, 2, 1)) if sg % 2 == odd]
                    for odd in range(2)]

        def kv_place(a, sg):
            i = kv_order[sg % 2].index((a, sg))
            return acc[:, 3 + 2 * (sg % 2) + i // 4, (i % 4) * P:(i % 4 + 1) * P]

        def ftile(g, a):
            return HT * (a // 2) + 2 * g + a % 2

        def hgrn_act(act):
            act.wait_ge(acc_free, TASK0["mix0_out"] + 2)
            act.dma_start(flat(bwm[:]), d["con"][:, CON0["bw_mask"]:CON0["bw_mask"] + 4 * P]).then_inc(hg["masks"], 16)
            hgrn_in_act(7, 0, 1)
            for g in range(NG):
                act.wait_ge(hg["qdiff"], g + 1)
                act.activation(qmid[:, g % 2], qmid[:, g % 2], ACT.Exp).then_inc(hg["qexp"], 1)
                for dr, last in enumerate((SEG - 1, 0)):
                    f = tiles(ftile(g, 2 * dr), 2)
                    act.activation(decay[:, ftile(g, 2 * dr):ftile(g, 2 * dr) + 2, :], f[:, :, last:T:SEG], ACT.Exp)
                act.drain()
                for dr in range(2):
                    f = tiles(ftile(g, 2 * dr), 2)
                    o = act.activation(f, f, ACT.Exp)
                o.then_inc(hg["cumexp"], 1)
            for b in range(4):
                act.wait_ge(hg["out"], b + 1)
                act.activation(osq[:, 2 * b:2 * b + 2, :], tiles(Q0 + 2 * b, 2), ACT.Square).then_inc(hg["sq"], 1)
            for q in (2, 3):
                hi_part(act, q, tiles(UU0 - 8 + 4 * q))
            act.wait_ge(hg["ms_ps"], 1)
            rn = osq.rearrange("p (b a) n -> p b (a n)", b=4)
            act.activation(rn, acc[:, 4:8, :], ACT.Ln, bias=eps[:, 1:2], scale=1.0 / P)
            act.drain()
            for b in range(2):
                act.activation(osq[:, 4 * b:4 * b + 4, :], osq[:, 4 * b:4 * b + 4, :], ACT.Exp, scale=-0.5)\
                   .then_inc(hg["rn"], 1)
            act.wait_ge(hg["done"], 1)
            hi_part(act, 0, tiles(Q0))

        def hgrn_dve(dve):
            def qdiff(g):
                for dr in range(2):
                    f = tiles(ftile(g, 2 * dr), 2)
                    o = dve.tensor_tensor(segs(qmid[:, g % 2, 2 * dr:2 * dr + 2, :]), segs(f),
                                          seg_point(f, POINTS[dr][0]), ALU.subtract)
                o.then_inc(hg["qdiff"], 1)
            qdiff(0)
            for g in range(NG):
                s, q = g % 2, tiles(Q0 + 2 * g, 2)
                if g + 1 < NG:
                    qdiff(g + 1)
                dve.wait_ge(hg["qexp"], g + 1)
                for dr in range(2):
                    o = dve.tensor_tensor(qmid[:, s, 2 * dr:2 * dr + 2, :], qmid[:, s, 2 * dr:2 * dr + 2, :], q, ALU.mult)
                o.then_inc(hg["qmid"], 1)
                dve.wait_ge(hg["cumexp"], g + 1)
                dve.wait_ge(hg["kv_ps"], g + 1)
                for j in range(3):
                    for a in range(4):
                        sg = j if a < 2 else NSEG - 1 - j
                        kv, st = kv_place(a, sg), lambda j: state[:, s, 3 * a + j, :]
                        if j == 0:
                            o = dve.tensor_copy(st(j), kv)
                        else:
                            o = dve.scalar_tensor_tensor(st(j), st(j - 1), decay[:, ftile(g, a), sg:sg + 1], kv,
                                                         ALU.mult, ALU.add)
                    if j < 2:
                        dve.drain()
                o.then_inc(hg["state"], 1)
                if g == 0:
                    dve.wait_ge(hg["masks"], 16)
                    dve.wait_ge(hg["zeroed"], 1)
                dve.wait_ge(hg["score_ps"], g + 1)
                for dr, mask in enumerate((fwm, bwm)):
                    o = dve.copy_predicated(prob[:, s, 4 * dr:4 * dr + 4, :], mask[:].bitcast(I32),
                                            acc[:, 1 + dr, :].rearrange("p (a n) -> p a n", a=4))
                o.then_inc(hg["prob"], 1)
                if g:
                    hgrn_take(dve, g - 1)
            hgrn_take(dve, NG - 1)
            for q in (2, 3):
                lo_part(dve, q, tiles(UU0 - 8 + 4 * q), READY0["mix0_out"] + q - 1)
            for b in range(2):
                dve.wait_ge(hg["rn"], b + 1)
                for h in range(4 * b, 4 * b + 4):
                    dve.scalar_tensor_tensor(u[:, Q0 + h, :], u[:, Q0 + h, :], pcol("hgrn_norm_g", h), osq[:, h, :],
                                             ALU.mult, ALU.mult)
                dve.drain()
                dve.wait_ge(hg["silu"], 2)
                dve.tensor_tensor(tiles(Q0 + 4 * b), tiles(Q0 + 4 * b), tiles(G0 + 4 * b), ALU.mult)\
                   .then_inc(hg["done"], 1)
            lo_part(dve, 0, tiles(Q0), READY0["mix0_out"] + 3)

        def hgrn_take(dve, g):
            dve.wait_ge(hg["qcum"], g + 1)
            dve.wait_ge(hg["out_ps"], g + 1)
            dve.tensor_copy(flat(tiles(Q0 + 2 * g, 2)), acc[:, 7 * (g % 2), :]).then_inc(hg["out"], 1)

        def hgrn_pool(pool):
            hgrn_in_pool(pool)
            pool.wait_ge(chunk_used, CHUNK0["mix0_out"])
            pool.memset(prob[:], 0.0).then_inc(hg["zeroed"], 1)
            for g in range(NG):
                pool.wait_ge(hg["cumexp"], g + 1)
                for dr in range(2):
                    f = tiles(ftile(g, 2 * dr), 2)
                    o = pool.tensor_tensor(f, f, tiles(Q0 + 2 * g, 2), ALU.mult)
                o.then_inc(hg["qcum"], 1)

        def hgrn_pe(pe):
            def kv(g):
                for a in range(4):
                    for j in range(3):
                        sg = j if a < 2 else NSEG - 1 - j
                        rows, b = slice(SEG * (sg % 2), SEG * (sg % 2) + SEG), sg // 2
                        o = nc.tensor.matmul(kv_place(a, sg), u[rows, L0 + ftile(g, a), b * P:(b + 1) * P],
                                             u[rows, I0 + 2 * g + a % 2, b * P:(b + 1) * P], start=True, stop=True)
                o.then_inc(hg["kv_ps"], 1)

            def scores(g):
                pe.wait_ge(hg["qmid"], g + 1)
                for a in range(4):
                    for b in range(2):
                        i = 2 * a + b
                        o = nc.tensor.matmul(acc[:, 1 + i // 4, (i % 4) * P:(i % 4 + 1) * P],
                                             u[:, K0 + ftile(g, a), b * P:(b + 1) * P],
                                             qmid[:, g % 2, a, b * P:(b + 1) * P], start=True, stop=True)
                o.then_inc(hg["score_ps"], 1)
            pe.wait_ge(acc_free, TASK0["mix0_out"] + 2)
            kv(0)
            scores(0)
            for g in range(NG):
                pe.wait_ge(hg["state"], g + 1)
                if g + 1 < NG:
                    kv(g + 1)
                pe.wait_ge(hg["prob"], g + 1)
                if g + 1 < NG:
                    scores(g + 1)
                pe.wait_ge(hg["qcum"], g + 1)
                if g >= 2:
                    pe.wait_ge(hg["out"], g - 1)
                for hh in range(2):
                    o0, bank = hh * T, 7 * (g % 2)
                    for a in (hh, 2 + hh):
                        for b in range(2):
                            nc.tensor.matmul(acc[:, bank, o0 + b * P:o0 + (b + 1) * P],
                                             u[:, I0 + 2 * g + hh, b * P:(b + 1) * P],
                                             prob[:, g % 2, 2 * a + b, :], start=(a < 2 and b == 0), stop=False)
                        for j in range(3):
                            sg = j + 1 if a < 2 else NSEG - 2 - j
                            o = nc.tensor.matmul(acc[:, bank, o0 + sg * SEG:o0 + (sg + 1) * SEG],
                                                 state[:, g % 2, 3 * a + j, :],
                                                 u[:, ftile(g, a), sg * SEG:(sg + 1) * SEG], start=False,
                                                 stop=(a >= 2 and j == 2))
                o.then_inc(hg["out_ps"], 1)
            for b in range(4):
                pe.wait_ge(hg["sq"], b + 1)
                o = nc.tensor.matmul(acc[:, 4 + b, :], ones[:], flat(osq[:, 2 * b:2 * b + 2, :]), start=True, stop=True)
            o.then_inc(hg["ms_ps"], 1)

        def hgrn_read(i, t):
            if (i, t) == (0, 1):
                nc.tensor.wait_ge(hg["rn"], 1)

        (r_sq, r_rn, r_g, r_cos, perm1, cos1, sin1), end = over(
            U0 + 4 * 24 * T, [[P, 4, T]] * 4 + [[P, P], [P, T], [P, T]])
        (v_tok, p_row, p_tok, mx, rs), end = over(
            end, [[P, 8, P], [P, 2, 4, T], [P, 2, 2 * T], [P, 2, 4], [P, 2, 4]])
        assert end <= W0
        at_ = {n: sem("at_" + n) for n in (
            "con", "sq", "ms_ps", "rn", "g", "rot_ps", "cos", "rot", "turned", "vtok_ps", "vtok", "score_ps", "max",
            "exp", "prob", "ptok_ps", "ptok", "out_ps", "hi", "lo")}
        NUNIT = 8
        SCALE = float(P) ** -0.5
        NTURN = 5

        def heads(first, j):
            return u[:, bass.ds(j * 4 + first, 4), :]

        def since(i, t, lo, hi):
            j = 2 * i + t - 1 if isinstance(i, int) else i * 2 + (t - 1)
            return j if not isinstance(i, int) or lo <= j < hi else None

        def heads(first, j):
            return u[:, bass.ds(j * 4 + first, 4), :]

        def since(i, t, lo, hi):
            j = 2 * i + t - 1 if isinstance(i, int) else i * 2 + (t - 1)
            return j if not isinstance(i, int) or lo <= j < hi else None

        def flat(x):
            return x.rearrange("p a n -> p (a n)")

        def norm_turn_act(i, t, c):
            act, j = nc.scalar, since(i, t, 0, NTURN)
            if j is None:
                return
            if c == 1:
                act.wait_ge(acc_free, TASK0["attn_in"] + j + 3)
                act.activation(r_sq[:], heads(0, j), ACT.Square).then_inc(at_["sq"], 1)
            elif c == 2:
                act.wait_ge(at_["ms_ps"], j + 1)
                act.wait_ge(at_["g"], j + 1)
                act.activation(r_rn[:].rearrange("p (b a) n -> p b (a n)", b=2),
                               acc[:, 4 * (1 - t):4 * (1 - t) + 2, :], ACT.Ln, bias=eps[:, 1:2], scale=1.0 / P)
                act.drain()
                act.activation(r_rn[:], r_rn[:], ACT.Exp, scale=-0.5).then_inc(at_["rn"], 1)

        def norm_turn_dve(i, t, c):
            dve, j = nc.vector, since(i, t, 0, NTURN)
            if j is None:
                return
            four = heads(0, j)
            if c == 1:
                dve.drain()
                dve.tensor_scalar(r_g[:], four, col("qk_norm_g", j * 2), None, ALU.mult).then_inc(at_["g"], 1)
            elif c == 2:
                dve.drain()
                dve.wait_ge(at_["con"], 48)
                dve.wait_ge(at_["rot_ps"], j + 1)
                dve.tensor_tensor(four, acc[:, 4 * (1 - t) + 2:4 * (1 - t) + 4, :].rearrange("p b (a n) -> p (b a) n", a=2),
                                  wide(sin1[:], 4), ALU.mult).then_inc(at_["rot"], 1)
            elif c == 3:
                dve.drain()
                dve.wait_ge(at_["cos"], j + 1)
                dve.tensor_tensor(four, four, r_cos[:], ALU.add)
                dve.drain()
                dve.wait_ge(at_["rn"], j + 1)
                dve.tensor_tensor(four, four, r_rn[:], ALU.mult).then_inc(at_["turned"], 1)

        def norm_turn_pe(i, t, c):
            pe, j = nc.tensor, since(i, t, 0, NTURN)
            if j is None or c != 2:
                return
            b0 = 4 * (1 - t)
            pe.wait_ge(acc_free, TASK0["attn_in"] + j + 3)
            pe.wait_ge(at_["sq"], j + 1)
            for h in range(2):
                o = pe.matmul(acc[:, b0 + h, :], ones[:], flat(r_sq[:, 2 * h:2 * h + 2, :]), start=True, stop=True)
            o.then_inc(at_["ms_ps"], 1)
            pe.wait_ge(at_["con"], 48)
            pe.wait_ge(at_["g"], j + 1)
            for h in range(2):
                o = pe.matmul(acc[:, b0 + 2 + h, :], perm1[:], flat(r_g[:, 2 * h:2 * h + 2, :]), start=True, stop=True)
            o.then_inc(at_["rot_ps"], 1)

        def norm_turn_read(i, t):
            j = since(i, t, 1, NTURN + 1)
            if j is not None:
                nc.tensor.wait_ge(at_["rn"], j)
                nc.tensor.wait_ge(at_["rot"], j)

        def attn_act(act):
            act.wait_ge(acc_free, TASK0["attn_out"] + 2)
            act.wait_ge(at_["vtok_ps"], 1)
            for b in range(2):
                o = act.activation(flat(v_tok[:, 4 * b:4 * b + 4, :]), acc[:, 6 + b, :], ACT.Copy)
            o.then_inc(at_["vtok"], 1)
            for n in range(NUNIT + 1):
                if n < NUNIT:
                    s = n % 2
                    act.wait_ge(at_["max"], n + 1)
                    if n >= 2:
                        act.wait_ge(at_["ptok_ps"], n - 1)
                    for i in range(4):
                        o = act.activation(p_row[:, s, i, :], acc[:, 2 * s + i // 2, (i % 2) * T:(i % 2 + 1) * T],
                                           ACT.Exp, bias=mx[:, s, i:i + 1], scale=SCALE, accum_out=rs[:, s, i:i + 1])
                    o.then_inc(at_["exp"], 1)
                if n:
                    m = n - 1
                    act.wait_ge(at_["ptok_ps"], m + 1)
                    for h in range(2):
                        o = act.activation(p_tok[:, h, :], acc[:, 4 + h, :], ACT.Copy)
                    o.then_inc(at_["ptok"], 1)
                    act.wait_ge(at_["out_ps"], m + 1)
                    act.activation(xhl[:, 2 * m:2 * m + 2, 0:T],
                                   acc[:, 6 + m % 2, :].rearrange("p (h n) -> p h n", h=2), ACT.Copy)\
                       .then_inc(x_hi if m % 2 else at_["hi"], 1)

        def attn_dve(dve):
            for n in range(NUNIT + 2):
                if 1 <= n <= NUNIT:
                    m = n - 1
                    s = m % 2
                    dve.wait_ge(at_["exp"], m + 1)
                    dve.reciprocal(rs[:, s, :], rs[:, s, :])
                    dve.drain()
                    dve.tensor_tensor(p_row[:, s], p_row[:, s], rs[:, s, :].unsqueeze(2).to_broadcast([P, 4, T]),
                                      ALU.mult).then_inc(at_["prob"], 1)
                if n < NUNIT:
                    s = n % 2
                    if n >= 2:
                        dve.drain()
                        dve.wait_ge(at_["exp"], n - 1)
                    dve.wait_ge(at_["score_ps"], n + 1)
                    dve.tensor_reduce(mx[:, s, :], acc[:, 2 * s:2 * s + 2, :].rearrange("p h (b n) -> p (h b) n", b=2),
                                      AX, ALU.max)
                    dve.drain()
                    dve.tensor_scalar(mx[:, s, :], mx[:, s, :], -SCALE, None, ALU.mult).then_inc(at_["max"], 1)
                if n >= 2:
                    m = n - 2
                    if m % 2:
                        dve.wait_ge(x_hi, READY0["attn_out"] + m // 2 + 1)
                    else:
                        dve.wait_ge(at_["hi"], m // 2 + 1)
                    dst = xhl[:, 2 * m:2 * m + 2, :]
                    o = dve.tensor_tensor(dst[:, :, T:2 * T], acc[:, 6 + m % 2, :].rearrange("p (h n) -> p h n", h=2),
                                          dst[:, :, 0:T].bitcast(F32), ALU.subtract)
                    o.then_inc(moving_ready if m % 2 else at_["lo"], 1)

        def attn_pool(pool):
            pool.wait_ge(at_["con"], 48)
            for j in loop(pool, NTURN):
                pool.wait_ge(at_["g"], j + 1)
                pool.tensor_tensor(r_cos[:], r_g[:], wide(cos1[:], 4), ALU.mult).then_inc(at_["cos"], 1)

        def attn_pe(pe):
            def scores(n):
                for i in range(4):
                    q = 2 * n + i // 2
                    o = nc.tensor.matmul(acc[:, 2 * (n % 2) + i // 2, (i % 2) * T:(i % 2 + 1) * T],
                                         u[:, q, (i % 2) * P:(i % 2 + 1) * P], u[:, 16 + q // 4, :],
                                         start=True, stop=True)
                o.then_inc(at_["score_ps"], 1)
            pe.wait_ge(acc_free, TASK0["attn_out"] + 1)
            pe.wait_ge(at_["turned"], NTURN)
            scores(0)
            scores(1)
            pe.wait_ge(acc_free, TASK0["attn_out"] + 2)
            for g in range(4):
                for b in range(2):
                    o = nc.tensor.transpose(acc[:, 6 + g // 2, (2 * (g % 2) + b) * P:(2 * (g % 2) + b + 1) * P],
                                            u[:, 20 + g, b * P:(b + 1) * P], ident[:])
            o.then_inc(at_["vtok_ps"], 1)
            for n in range(NUNIT):
                pe.wait_ge(at_["prob"], n + 1)
                for i in range(8):
                    h, sb, b = i // 4, i // 2 % 2, i % 2
                    o = nc.tensor.transpose(acc[:, 4 + h, sb * T + b * P:sb * T + (b + 1) * P],
                                            p_row[:, n % 2, 2 * h + b, sb * P:(sb + 1) * P], ident[:])
                o.then_inc(at_["ptok_ps"], 1)
                if n + 2 < NUNIT:
                    scores(n + 2)
                pe.wait_ge(at_["ptok"], n + 1)
                if n == 0:
                    pe.wait_ge(at_["vtok"], 1)
                if n >= 2:
                    if n % 2:
                        pe.wait_ge(moving_ready, READY0["attn_out"] + n // 2)
                    else:
                        pe.wait_ge(at_["lo"], n // 2)
                for i in range(4):
                    h, sb = i // 2, i % 2
                    o = nc.tensor.matmul(acc[:, 6 + n % 2, h * T:(h + 1) * T], v_tok[:, 2 * (n // 2) + sb, :],
                                         p_tok[:, h, sb * T:(sb + 1) * T], start=(sb == 0), stop=(sb == 1))
                o.then_inc(at_["out_ps"], 1)
            pe.wait_ge(moving_ready, READY0["attn_out"] + 4)

        UX0, UG0, XC0, R0, IG0 = 0, MT, 2 * MT, 3 * MT, 4 * MT
        (w_gates,), end = over(W0, [[P, 2, MT, P]])
        assert end <= W0 + WSIZE
        ru = {n: sem("ru_" + n) for n in ("con", "abs", "e", "cols", "conv", "ps", "sig", "tanh", "bsq",
                                          "sqrt", "silu", "done")}
        NSP, TMP = 0, MT

        def rnn_act(i, t, c):
            act, task = nc.scalar, 2 * i + t
            if c == 1 and task == 0:
                act.wait_ge(ru["abs"], 1)
                act.activation(nrg[:, TMP:TMP + MT], nrg[:, TMP:TMP + MT], ACT.Exp, scale=-1.0).then_inc(ru["e"], 1)
            q = task - 1
            if c == 3 and 0 <= q < 4:
                act.wait_ge(ru["ps"], q + 1)
                for f in range(4):
                    m, bank = 4 * q + f, 4 * (1 - t) + f
                    act.activation(u[:, R0 + m, :], acc[:, bank, 0:T], ACT.Sigmoid, bias=pcol("b_rg_2", m))
                    o = act.activation(u[:, IG0 + m, :], acc[:, bank, T:2 * T], ACT.Sigmoid, bias=pcol("b_ig_2", m))
                o.then_inc(ru["sig"], 1)
            q = task - 2
            if c == 1 and 0 <= q < 4:
                act.wait_ge(ru["cols"], 1)
                act.drain()
                for f in range(4):
                    m = 4 * q + f
                    act.activation(u[:, UX0 + m, :], u[:, R0 + m, :], ACT.Exp, scale=nrg[:, NSP + m:NSP + m + 1])
                for f in range(4):
                    m = 4 * q + f
                    o = act.activation(u[:, R0 + m, :], u[:, R0 + m, :], ACT.Tanh, scale=nrg[:, NSP + m:NSP + m + 1])
                o.then_inc(ru["tanh"], 1)
            q = task - 3
            if c == 1 and 0 <= q < 4:
                act.wait_ge(ru["bsq"], q + 1)
                xq = u[:, XC0 + 4 * q:XC0 + 4 * q + 4, :]
                act.activation(xq, xq, ACT.Sqrt, scale=-1.0).then_inc(ru["sqrt"], 1)
            if c == 1 and task == 5:
                for dst, cn, n in ((perm2[:], "rope2_perm", P), (cos2[:], "rope2_cos", T),
                                   (sin2[:], "rope2_sin", T), (mask0[:], "dil_mask0", 3 * P),
                                   (mask1[:], "dil_mask1", 3 * T)):
                    act.dma_start(dst, d["con"][:, CON0[cn]:CON0[cn] + n]).then_inc(dl["con"], 16)
            q = task - 5
            if c == 2 and 0 <= q < 4:
                act.wait_ge(acc_free, TASK0["rnn_in"] + 4 + q + 3)
                gq = u[:, UG0 + 4 * q:UG0 + 4 * q + 4, :]
                act.activation(gq, gq, ACT.Silu).then_inc(ru["silu"], 1)

        def rnn_cols(dve):
            c = lambda at0: nrg[:, at0:at0 + MT]
            lam = par[:, PAR0["lru_lambda_2"]:PAR0["lru_lambda_2"] + MT]
            dve.wait_ge(ru["e"], 1)
            dve.tensor_scalar(c(NSP), c(TMP), 2.0, None, ALU.add)
            dve.drain()
            dve.reciprocal(c(NSP), c(NSP))
            dve.drain()
            dve.tensor_tensor(c(TMP), c(TMP), c(NSP), ALU.mult)
            dve.drain()
            sq, ser = c(2 * MT), c(3 * MT)
            dve.tensor_tensor(sq, c(TMP), c(TMP), ALU.mult)
            dve.memset(ser, 1.0 / 19)
            dve.drain()
            for k in range(8, -1, -1):
                dve.tensor_tensor(ser, ser, sq, ALU.mult)
                dve.drain()
                dve.tensor_scalar(ser, ser, 1.0 / (2 * k + 1), None, ALU.add)
                dve.drain()
            dve.scalar_tensor_tensor(c(TMP), ser, 2.0, c(TMP), ALU.mult, ALU.mult)
            dve.tensor_scalar(sq, lam, -1.0, 0.0, ALU.mult, ALU.max)
            dve.drain()
            dve.tensor_tensor(c(TMP), c(TMP), sq, ALU.add)
            dve.drain()
            dve.tensor_scalar(c(NSP), c(TMP), -LRU_C, None, ALU.mult).then_inc(ru["cols"], 1)

        def rnn_dve(i, t, c):
            dve, task = nc.vector, 2 * i + t
            four = lambda at0, q: u[:, at0 + 4 * q:at0 + 4 * q + 4, :]
            if c == 1 and task == 0:
                lam = par[:, PAR0["lru_lambda_2"]:PAR0["lru_lambda_2"] + MT]
                dve.scalar_tensor_tensor(nrg[:, TMP:TMP + MT], lam, -1.0, lam, ALU.mult, ALU.max)\
                   .then_inc(ru["abs"], 1)
            if c == 3 and task == 0:
                rnn_cols(dve)
            q = task - 1
            if c == 1 and 0 <= q < 4:
                cw = PAR0["conv_w_2"]
                dve.drain()
                for m in range(4 * q, 4 * q + 4):
                    o = dve.tensor_scalar(u[:, XC0 + m, :], u[:, UX0 + m, :], par[:, cw + 3 * MT + m:cw + 3 * MT + m + 1],
                                          pcol("conv_b_2", m), ALU.mult, ALU.add)
                for s in (1, 2, 3):
                    dve.drain()
                    for m in range(4 * q, 4 * q + 4):
                        w = cw + (3 - s) * MT + m
                        o = dve.scalar_tensor_tensor(u[:, XC0 + m, s:T], u[:, UX0 + m, 0:T - s], par[:, w:w + 1],
                                                     u[:, XC0 + m, s:T], ALU.mult, ALU.add)
                o.then_inc(ru["conv"], 1)
            q = task - 2
            if c == 2 and 0 <= q < 4:
                dve.wait_ge(ru["tanh"], q + 1)
                a, xq, g = four(UX0, q), four(XC0, q), four(IG0, q)
                dve.tensor_tensor(g, g, xq, ALU.mult)
                dve.drain()
                dve.tensor_tensor(xq, a, a, ALU.mult)
                dve.drain()
                dve.scalar_tensor_tensor(xq, xq, 1.0, four(R0, q), ALU.add, ALU.mult).then_inc(ru["bsq"], 1)
            q = task - 3
            if c == 2 and 0 <= q < 4:
                dve.wait_ge(ru["sqrt"], q + 1)
                dve.tensor_tensor(four(IG0, q), four(IG0, q), four(XC0, q), ALU.mult)
                dve.drain()
                for m in range(4 * q, 4 * q + 4):
                    dve.tensor_tensor_scan(u[:, R0 + m, :], u[:, UX0 + m, :], u[:, IG0 + m, :], 0.0, ALU.mult, ALU.add)
            q = task - 5
            if c == 3 and 0 <= q < 4:
                dve.drain()
                dve.wait_ge(ru["silu"], q + 1)
                dve.tensor_tensor(four(UX0, q), four(R0, q), four(UG0, q), ALU.mult).then_inc(ru["done"], 1)

        def rnn_pe(i, t, c):
            pe, q = nc.tensor, 2 * i + t - 1
            if c == 3 and 0 <= q < 4:
                if q == 0:
                    pe.wait_ge(ru["con"], 16)
                pe.wait_ge(acc_free, TASK0["rnn_in"] + q + 3)
                pe.wait_ge(ru["conv"], q + 1)
                for f in range(4):
                    m = 4 * q + f
                    for j in range(2):
                        o = pe.matmul(acc[:, 4 * (1 - t) + f, j * T:(j + 1) * T], w_gates[:, j, m, :],
                                      u[:, XC0 + m, :], start=True, stop=True)
                o.then_inc(ru["ps"], 1)

        def rnn_read(i, t):
            if 0 <= 2 * i + t - 2 < 4:
                nc.tensor.wait_ge(ru["sig"], 2 * i + t - 1)

        QD, KD, VD, AG = 2 * MT, 2 * MT + 12, 2 * MT + 24, 2 * MT + 36
        OD = MT
        (perm2, cos2, sin2, mask0, mask1, t_cos, t_rot), end = over(
            W0, [[P, P], [P, T], [P, T], [P, 3 * P], [P, 3 * T], [P, 4, T], [P, 4, T]])
        assert end <= W0 + WSIZE
        (dvt1, dp01, dp11), end = over(U0 + 4 * 24 * T, [[P, 6, P], [P, 3 * P], [P, 3 * T]])
        assert end <= U0 + 4 * 32 * T
        (dvt0, dp00, dp10, dt0, dt1, dmx, drs), end = over(
            U0 + 4 * 72 * T, [[P, 6, P], [P, 3 * P], [P, 3 * T], [P, 3, P], [P, 6, P], [P, 2, 2], [P, 2, 2]])
        assert end <= W0
        dvt, dp0, dp1 = (dvt0, dvt1), (dp00, dp01), (dp10, dp11)
        dl = {n: sem("dl_" + n) for n in ("con", "rot_ps", "cos", "rot", "turned", "vtok_ps", "vtok", "score_ps",
                                          "scores_read", "max", "exp", "prob", "ptok_ps", "ptok", "out_ps", "out", "silu", "gated",
                                          "o_done")}

        def dil_act(hf):
            def run(act):
                act.wait_ge(acc_free, TASK0["half%d" % hf] + NTASK["half%d" % hf] + 2)
                for h in range(-1, 4):
                    n, s = h + 4 * hf, h % 2
                    if h >= 0:
                        act.wait_ge(dl["max"], n + 1)
                        act.activation(dp0[s][:], dp0[s][:], ACT.Exp, bias=dmx[:, s, 0:1], accum_out=drs[:, s, 0:1])
                        act.activation(dp1[s][:], dp1[s][:], ACT.Exp, bias=dmx[:, s, 1:2], accum_out=drs[:, s, 1:2])\
                           .then_inc(dl["exp"], 1)
                    if h + 1 < 4:
                        m, r = n + 1, 1 - s
                        act.wait_ge(dl["vtok_ps"], m + 1)
                        act.activation(flat(dvt[r][:])[:, 0:4 * P], acc[:, 3, :], ACT.Copy)
                        act.activation(flat(dvt[r][:])[:, 4 * P:6 * P], acc[:, 4, 0:2 * P], ACT.Copy)\
                           .then_inc(dl["vtok"], 1)
                    if h >= 0:
                        act.wait_ge(dl["ptok_ps"], n + 1)
                        act.activation(flat(dt0[:]), acc[:, 5, 0:3 * P], ACT.Copy)
                        act.activation(flat(dt1[:])[:, 0:4 * P], acc[:, 6, :], ACT.Copy)
                        act.activation(flat(dt1[:])[:, 4 * P:6 * P], acc[:, 7, 0:2 * P], ACT.Copy)\
                           .then_inc(dl["ptok"], 1)
                act.activation(u[:, AG:AG + 4, :], u[:, AG:AG + 4, :], ACT.Silu).then_inc(dl["silu"], 1)
            return run

        def dil_dve(hf):
            def run(dve):
                for h in range(-1, 4):
                    n, s = h + 4 * hf, h % 2
                    if h >= 0:
                        dve.wait_ge(dl["exp"], n + 1)
                        dve.reciprocal(drs[:, s, :], drs[:, s, :])
                        dve.drain()
                        dve.tensor_scalar(dp0[s][:], dp0[s][:], drs[:, s, 0:1], None, ALU.mult)
                        dve.tensor_scalar(dp1[s][:], dp1[s][:], drs[:, s, 1:2], None, ALU.mult)\
                           .then_inc(dl["prob"], 1)
                    if h + 1 < 4:
                        m, r = n + 1, 1 - s
                        dve.wait_ge(dl["score_ps"], m + 1)
                        if h >= 1:
                            dve.wait_ge(dl["ptok_ps"], m - 1)
                        dve.scalar_tensor_tensor(dp0[r][:], acc[:, 0, 0:3 * P], SCALE, mask0[:], ALU.mult, ALU.add)
                        dve.scalar_tensor_tensor(dp1[r][:, 0:2 * T], acc[:, 1, :], SCALE, mask1[:, 0:2 * T],
                                                 ALU.mult, ALU.add)
                        dve.scalar_tensor_tensor(dp1[r][:, 2 * T:3 * T], acc[:, 2, 0:T], SCALE,
                                                 mask1[:, 2 * T:3 * T], ALU.mult, ALU.add)\
                           .then_inc(dl["scores_read"], 1)
                        dve.drain()
                        dve.tensor_reduce(dmx[:, r, 0:1], dp0[r][:], AX, ALU.max)
                        dve.tensor_reduce(dmx[:, r, 1:2], dp1[r][:], AX, ALU.max)
                        dve.drain()
                        dve.tensor_scalar(dmx[:, r, :], dmx[:, r, :], -1.0, None, ALU.mult).then_inc(dl["max"], 1)
                    if h >= 0:
                        dve.wait_ge(dl["out_ps"], n + 1)
                        dve.tensor_copy(u[:, OD + 4 * hf + h, :], acc[:, 7, T:2 * T]).then_inc(dl["out"], 1)
                dve.wait_ge(dl["silu"], hf + 1)
                dve.drain()
                o = u[:, OD + 4 * hf:OD + 4 * hf + 4, :]
                dve.tensor_tensor(o, o, u[:, AG:AG + 4, :], ALU.mult).then_inc(dl["gated"], 1)
            return run

        def dil_pool(hf):
            def run(pool):
                pool.wait_ge(dl["con"], 80)
                def cos(j):
                    pool.wait_ge(acc_free, j + (TASK0["half%d" % hf] + 3))
                    if hf or not isinstance(j, int):
                        pool.wait_ge(dl["turned"], j + 6 * hf)
                    pool.tensor_tensor(t_cos[:], heads(QD, j), wide(cos2[:], 4), ALU.mult).then_inc(dl["cos"], 1)
                cos(0)
                with pool.Fori(1, 6) as j:
                    cos(j)
            return run

        def turn_dve(hf):
            def between(i, t, c):
                dve, j = nc.vector, since(i, t, 0, 6)
                if j is None:
                    return
                if c == 2:
                    dve.drain()
                    dve.wait_ge(dl["rot_ps"], j + 6 * hf + 1)
                    dve.tensor_tensor(t_rot[:], acc[:, 4 * (1 - t):4 * (1 - t) + 2, :].rearrange(
                        "p b (a n) -> p (b a) n", a=2), wide(sin2[:], 4), ALU.mult).then_inc(dl["rot"], 1)
                elif c == 3:
                    dve.drain()
                    dve.wait_ge(dl["cos"], j + 6 * hf + 1)
                    dve.tensor_tensor(heads(QD, j), t_rot[:], t_cos[:], ALU.add).then_inc(dl["turned"], 1)
            return between

        def turn_pe(hf):
            def extra(i, t, c):
                pe, j = nc.tensor, since(i, t, 0, 6)
                if j is None or c != 2:
                    return
                pe.wait_ge(acc_free, j + (TASK0["half%d" % hf] + 3))
                for h in range(2):
                    o = pe.matmul(acc[:, 4 * (1 - t) + h, :], perm2[:],
                                  flat(u[:, bass.ds(j * 4 + (QD + 2 * h), 2), :]), start=True, stop=True)
                o.then_inc(dl["rot_ps"], 1)
            return extra

        def turn_read(hf):
            def banks_read(i, t):
                j = since(i, t, 1, 7)
                if j is not None:
                    nc.tensor.wait_ge(dl["rot"], j + 6 * hf)
            return banks_read

        def dil_pe(hf):
            def run(pe):
                pe.wait_ge(acc_free, TASK0["half%d" % hf] + NTASK["half%d" % hf] + 2)
                pe.wait_ge(dl["turned"], 6 * hf + 6)
                for h in range(-1, 4):
                    n, s = h + 4 * hf, h % 2
                    if h + 1 < 4:
                        m = h + 1
                        if h >= 0:
                            pe.wait_ge(dl["vtok"], n + 1)
                        for i in range(6):
                            o = nc.tensor.transpose(acc[:, 3 + i // 4, (i % 4) * P:(i % 4 + 1) * P],
                                                    u[:, VD + 4 * (i // 2) + m, (i % 2) * P:(i % 2 + 1) * P], ident[:])
                        o.then_inc(dl["vtok_ps"], 1)
                        if h >= 0:
                            pe.wait_ge(dl["scores_read"], n + 1)
                        for g in range(3):
                            q, k = u[:, QD + 4 * g + m, :], u[:, KD + 4 * g + m, :]
                            nc.tensor.matmul(acc[:, 0, g * P:(g + 1) * P], q[:, 0:P], k[:, 0:P], start=True, stop=True)
                            o = nc.tensor.matmul(acc[:, 1 + g // 2, (g % 2) * T:(g % 2 + 1) * T], q[:, P:2 * P], k,
                                                 start=True, stop=True)
                        o.then_inc(dl["score_ps"], 1)
                    if h < 0:
                        continue
                    pe.wait_ge(dl["prob"], n + 1)
                    if n:
                        pe.wait_ge(dl["out"], n + 1)
                    for g in range(3):
                        nc.tensor.transpose(acc[:, 5, g * P:(g + 1) * P], dp0[s][:, g * P:(g + 1) * P], ident[:])
                    for i in range(6):
                        o = nc.tensor.transpose(acc[:, 6 + i // 4, (i % 4) * P:(i % 4 + 1) * P],
                                                dp1[s][:, i * P:(i + 1) * P], ident[:])
                    o.then_inc(dl["ptok_ps"], 1)
                    pe.wait_ge(dl["ptok"], n + 1)
                    pe.wait_ge(dl["vtok"], n + 1)
                    for g in range(3):
                        nc.tensor.matmul(acc[:, 7, T:T + P], dvt[s][:, 2 * g, :], dt0[:, g, :],
                                         start=(g == 0), stop=(g == 2))
                    for i in range(6):
                        o = nc.tensor.matmul(acc[:, 7, T + P:2 * T], dvt[s][:, i, :], dt1[:, i, :],
                                             start=(i == 0), stop=(i == 5))
                    o.then_inc(dl["out_ps"], 1)
                pe.wait_ge(dl["out"], 4 * hf + 5)
            return run

        pre_norm = sem("pre_norm")
        pre_scaled = sem("pre_scaled")
        gates_sig = sem("gates_sig")
        merged = sem("merged")
        fin = sem("fin")

        def pre_act(act):
            act_rstd(5)
            for q in range(4):
                act.wait_ge(pre_norm, q + 1)
                for m in range(4 * q, 4 * q + 4):
                    act.activation(u[:, m, :], u[:, m, :], ACT.Copy, scale=pcol("ln_pre_g_2", m))
                act.drain()
                hi_part(act, q, u[:, 4 * q:4 * q + 4, :])
            act.dma_start(w_gates[:], d["w_gates"]).then_inc(ru["con"], 16)

        def pre_dve(dve):
            dve_rms(5, DM, acc[:, 0, 0:T])
            dve.wait_ge(rstd_ready, 6)
            for q in range(4):
                dve.tensor_tensor(u[:, 4 * q:4 * q + 4, :], z[:, 4 * q:4 * q + 4, :], wide(rstd[:], 4), ALU.mult)\
                   .then_inc(pre_norm, 1)
                if q:
                    lo_part(dve, q - 1, u[:, 4 * q - 4:4 * q, :], READY0["rnn_in"] + q)
            lo_part(dve, 3, u[:, 12:16, :], READY0["rnn_in"] + 4)

        DX, GR, GA, Y0 = FT - HT, 2 * MT, 3 * MT, 3 * MT

        def four_hidden(first):
            return hid[:, first:first + 4, :]

        def gates_act(i, t, c):
            act = nc.scalar
            if isinstance(i, int) and (i, t) == (0, 0) and c < 3:
                act.wait_ge(dl["gated"], 2)
                hi_part(act, 0, tiles(OD + 4 * (c - 1)), four_hidden(DX + 4 * (c - 1)))
            j = since(i, t, 0, 8)
            if c == 1 and j is not None:
                act.wait_ge(acc_free, TASK0["gates"] + j + 3)
                act.activation(heads(GR, j), heads(GR, j), ACT.Sigmoid).then_inc(gates_sig, 1)

        def gates_dve(i, t, c):
            if isinstance(i, int) and (i, t) == (0, 0) and c > 1:
                lo_part(nc.vector, 0, tiles(OD + 4 * (c - 2)), READY0["dil_out"] + c - 1, four_hidden(DX + 4 * (c - 2)))

        def rnn_split_act(i, t, c):
            if i == 0:
                if t == 0:
                    nc.scalar.wait_ge(chunk_used, CHUNK0["dil_out"])
                for q in (2 * t, 2 * t + 1):
                    hi_part(nc.scalar, q, tiles(UX0 + 4 * q))

        def rnn_split_dve(i, t, c):
            if i == 0:
                for q in (2 * t, 2 * t + 1):
                    lo_part(nc.vector, q, tiles(UX0 + 4 * q), READY0["rnn_out"] + q + 1)

        def dve_gated(which):
            def after(i, t, task, n):
                dve, q = nc.vector, 2 * i + t
                dve.drain()
                dve.wait_ge(chunk_used, n + 1)
                dve.wait_ge(gates_sig, q + (1 if which else 5))
                for f in range(CF):
                    o = read_out(etmp[:, f, :], 4 * t + f)
                o.then_inc(acc_free, 1)
                dve.drain()
                first, own = tiles(GA + 4 * q), tiles((GR if which else GA) + 4 * q)
                o = dve.tensor_tensor(own, own, etmp[:], ALU.mult)
                if which:
                    dve.drain()
                    dve.tensor_tensor(own, first, own, ALU.add).then_inc(merged, 1)
            return after

        def merge_act(i, t, c):
            q = 2 * i + t - 1
            if c == 1 and q >= 0:
                nc.scalar.wait_ge(merged, q + 1)
                hi_part(nc.scalar, q, tiles(GR + 4 * q), four_hidden(4 * q))

        def merge_dve(i, t, c):
            q = 2 * i + t - 1
            if c == 2 and q >= 0:
                lo_part(nc.vector, q, tiles(GR + 4 * q), READY0["last_out"] + q + 1, four_hidden(4 * q))

        def dve_last(i, t, task, n):
            nc.vector.wait_ge(chunk_used, n + 1)
            for f in range(CF):
                o = read_out(u[:, Y0 + 8 * i + 4 * t + f, :], 4 * t + f)
                if f == CF - 1:
                    o.then_inc(acc_free, 1)

        def scale_dve(i, t, c):
            dve, q = nc.vector, 2 * i + t - 1
            if c == 2 and q >= 0:
                dve.wait_ge(sq_ready, 4 * 5 + q + 1)
                for m in range(4 * q, 4 * q + 4):
                    o = dve.tensor_scalar(u[:, Y0 + m, :], u[:, Y0 + m, :], pcol("ln_post_g_2", m), None, ALU.mult)
                if q == 3:
                    o.then_inc(fin, 1)

        def final_quarter(eng, q):
            y, out = tiles(Y0 + 4 * q), z[:, 4 * q:4 * q + 4, :]
            eng.tensor_tensor(y, y, wide(rstd[:], 4), ALU.mult)
            eng.drain()
            eng.tensor_tensor(out, out, y, ALU.add).then_inc(out_ready[q], 1)

        def final_dve(dve):
            dve_rms(6, DM, acc[:, 1, 0:T])
            dve.wait_ge(rstd_ready, 7)
            for q in range(3):
                final_quarter(dve, q)

        def final_pool(pool):
            pool.wait_ge(fin, 1)
            pool.wait_ge(rstd_ready, 7)
            final_quarter(pool, 3)

        FIRST_TILE = {"mix0_in": 0, "attn_in": 0, "rnn_in": 0, "half0": QD, "half1": QD, "gates": 2 * MT}
        LNS = {"mix0_out": (0, "ln1", 0, "up0"), "down0": (1, "ln2", 0, "attn_in"),
               "attn_out": (2, "ln1", 1, "up1"), "down1": (3, "ln2", 1, None)}

        @block.sync
        def _(sp):
            wd = d["weights"]
            for n in range(2):
                sp.dma_start(raw[:, n, :], wd[n]).then_inc(raw_landed[n], 16)
            with sp.Fori(1, NCHUNKS // 2) as i:
                for s in range(2):
                    sp.wait_ge(weights_split, i * 2 + s - 1)
                    sp.dma_start(raw[:, s, :], wd[bass.ds(i * 2 + s, 1)].squeeze(0)).then_inc(raw_landed[s], 16)
            for q in range(4):
                sp.wait_ge(out_ready[q], 1)
                sp.dma_start(d["out"][:, 4 * q:4 * q + 4, :], z[:, 4 * q:4 * q + 4, :]).then_inc(out_stored, 16)
            sp.wait_ge(out_stored, 64)

        @block.gpsimd
        def _(pool):
            for name in on:
                if name in LNS:
                    pool_sums(LNS[name][0], z)
                elif name.startswith("up"):
                    pool_hidden(int(name[2]))
                elif name == "mix0_in":
                    hgrn_pool(pool)
                elif name == "attn_in":
                    attn_pool(pool)
                elif name.startswith("half"):
                    dil_pool(int(name[4]))(pool)
                elif name == "last_out":
                    pool_sums(5, None)
                    final_pool(pool)
                if name == "down1":
                    pool.wait_ge(sums_ready, 6)
                    pool.engine_nop().then_inc(sq_used, 1)

        @block.scalar
        def _(act):
            for q in range(4):
                act.dma_start(z[:, 4 * q:4 * q + 4, :], d["x"][:, 4 * q:4 * q + 4, :]).then_inc(x_landed[q], 16)
            act.dma_start(par[:], d["par"]).then_inc(par_landed, 16)

            def con(dst, name, n, s):
                dst = dst if len(dst.shape) == 2 else flat(dst)
                act.dma_start(dst, d["con"][:, CON0[name]:CON0[name] + n]).then_inc(s, 16)
            for dst, name, n in ((ident[:], "ident", P), (seg1[:], "seg_start", T), (fwm[:], "fw_mask", 4 * P)):
                con(dst, name, n, con_landed)
            for q in range(4):
                act.wait_ge(x_landed[q], 16)
                hi_part(act, q, z[:, 4 * q:4 * q + 4, :])
                if q == 0:
                    cast_chunk(act, 0, 0)
            cast_chunk(act, 1, 1)
            act.wait_ge(par_landed, 16)
            for name in on:
                end = name == STAGES[-1][0]
                if name in LNS:
                    occ, ln, layer, nxt = LNS[name]

                    def square_between(i, t, c):
                        if name == "mix0_out" and (i, t, c) == (0, 0, 1):
                            act.wait_ge(hg["done"], 2)
                            hi_part(act, 1, tiles(Q0 + 4))
                        act_between(occ, z)(i, t, c)
                    drive(act, name, cast_chunk, None, unroll=True, between=square_between)
                    act_square(occ, 3, z)
                    if name == "down0":
                        act.wait_ge(chunk_used, CHUNK0["attn_in"])
                        for dst, cn, n in ((perm1[:], "rope1_perm", P), (cos1[:], "rope1_cos", T),
                                           (sin1[:], "rope1_sin", T)):
                            con(dst, cn, n, at_["con"])
                    act_rstd(1 + occ)
                    act_affine(occ, ln + "_g", ln + "_b", nxt, layer * MT, range(3 if nxt else 4))
                    if name == "down1":
                        pre_act(act)
                elif name.startswith("up"):
                    drive(act, name, cast_chunk, act_silu(int(name[2])), between=late_act(name, None), peel=(1,))
                elif name == "gates":
                    drive(act, name, cast_chunk, None, between=gates_act, peel=(1,))
                    gates_act(4, 0, 1)
                elif name == "dil_out":
                    drive(act, name, cast_chunk, None, between=rnn_split_act, unroll=True)
                elif name == "rnn_out":
                    drive(act, name, cast_chunk, None, between=merge_act, unroll=True)
                    merge_act(2, 0, 1)
                elif name == "last_out":
                    y = u[:, Y0:Y0 + MT, :]
                    drive(act, name, cast_chunk, None, unroll=True, between=act_between(5, y))
                    act_square(5, 3, y)
                    act_rstd(6)
                elif name == "mix0_in":
                    drive(act, name, cast_chunk, None, between=hgrn_in_act, unroll=True)
                elif name == "attn_in":
                    drive(act, name, cast_chunk, None, between=late_act(name, norm_turn_act), peel=(1,))
                elif name == "rnn_in":
                    drive(act, name, cast_chunk, None, between=rnn_act, unroll=True)
                else:
                    drive(act, name, cast_chunk, None, unroll=end)
                if name == "mix0_in":
                    hgrn_act(act)
                elif name == "attn_in":
                    attn_act(act)
                elif name == "rnn_in":
                    rnn_act(4, 0, 2)
                elif name.startswith("half"):
                    dil_act(int(name[4]))(act)

        @block.vector
        def _(dve):
            dve.memset(ones[:], 1.0)
            dve.memset(eps[:, 0:1], LN_EPS)
            dve.memset(eps[:, 1:2], RMS_EPS).then_inc(acc_free, 2)
            for c, s in enumerate((hid_ready, sq_used, dl["out"])):
                dve.memset(eps[:, 2 + c:3 + c], 0.0).then_inc(s, 1)
            for q in range(4):
                lo_part(dve, q, z[:, 4 * q:4 * q + 4, :], q + 1)
                if q == 0:
                    split_chunk(dve, 0, 0)
            split_chunk(dve, 1, 1)
            dve.wait_ge(par_landed, 16)
            tab = lambda r: par[:, PAR0["hgrn_lb_table"] + r * HT:PAR0["hgrn_lb_table"] + (r + 1) * HT]
            row = lambda r: lbs[:, r * HT:(r + 1) * HT]
            dve.tensor_tensor(row(0), tab(0), tab(1), ALU.max)
            dve.drain()
            dve.tensor_tensor(row(0), row(0), tab(2), ALU.max)
            dve.drain()
            for r in range(3):
                o = dve.tensor_tensor(row(r + 1), tab(r), row(0), ALU.subtract)
            o.then_inc(lb_max, 1)
            for name in on:
                end = name == STAGES[-1][0]
                if name in LNS:
                    occ, ln, layer, nxt = LNS[name]

                    def residual_between(i, t, c):
                        if name.startswith("down") and (i, t, c) == (0, 0, 1):
                            last_value(FG - 1, 1, range(2))
                            last_value(FG - 1, 2, range(2, 4))
                        if name == "mix0_out" and (i, t, c) == (0, 0, 1):
                            lo_part(dve, 1, tiles(Q0 + 4), READY0[name] + 4)
                        dve_between(i, t, c)
                    drive(dve, name, split_chunk, dve_residual(), unroll=True, between=residual_between)
                    dve_mean_var(1 + occ, DM)
                    dve_norm(occ, nxt)
                    if name == "down1":
                        pre_dve(dve)
                elif name.startswith("up"):
                    dve.drain()
                    for pad in (gpad, vpad):
                        dve.memset(pad[:, :, 0:1], 0.0)
                        dve.memset(pad[:, :, T + 1:T + 2], 0.0)
                    dve.drain()
                    between, value = dve_conv(int(name[2]))
                    drive(dve, name, split_chunk, dve_pad, between=late_dve(name, between), peel=(1,))
                    last_value = value
                elif name == "gates":
                    drive(dve, name, split_chunk, dve_store(FIRST_TILE[name]), between=gates_dve, peel=(1,))
                elif name == "dil_out":
                    drive(dve, name, split_chunk, dve_gated(0), between=rnn_split_dve, unroll=True)
                elif name == "rnn_out":
                    drive(dve, name, split_chunk, dve_gated(1), between=merge_dve, unroll=True)
                    merge_dve(2, 0, 2)
                elif name == "last_out":
                    drive(dve, name, split_chunk, dve_last, between=scale_dve, unroll=True)
                    scale_dve(2, 0, 2)
                    final_dve(dve)
                elif name == "mix0_in":
                    dve.wait_ge(con_landed, 48)
                    drive(dve, name, split_chunk, dve_store(FIRST_TILE[name]), between=hgrn_in_dve, unroll=True)
                elif name == "attn_in":
                    drive(dve, name, split_chunk, dve_store(FIRST_TILE[name]), between=late_dve(name, norm_turn_dve), peel=(1,))
                elif name == "rnn_in":
                    drive(dve, name, split_chunk, dve_store(FIRST_TILE[name]), between=rnn_dve, unroll=True)
                elif name.startswith("half"):
                    drive(dve, name, split_chunk, dve_store(FIRST_TILE[name]), between=turn_dve(int(name[4])),
                          peel=(1, 3, 4))
                else:
                    drive(dve, name, split_chunk, dve_store(FIRST_TILE[name]), unroll=end)
                if name == "mix0_in":
                    hgrn_dve(dve)
                elif name == "attn_in":
                    attn_dve(dve)
                elif name == "rnn_in":
                    rnn_dve(4, 0, 3)
                    dve.wait_ge(dl["con"], 80)
                elif name.startswith("half"):
                    dil_dve(int(name[4]))(dve)

        @block.tensor
        def _(pe):
            for name in on:
                if name in ("down0", "down1"):
                    multiply(pe, name, hid_moving, hid_from(int(name[4])))
                elif name == "dil_out":
                    multiply(pe, name, lambda k, a, b: hid[:, DX + k, a:b], ready_from(name))
                elif name == "last_out":
                    multiply(pe, name, hid_moving, ready_from(name))
                elif name == "mix0_out":
                    multiply(pe, name, lambda k, a, b: xhl[:, (k + HT) % MT, a:b], ready_from(name), (1,),
                             banks_read=hgrn_read)
                elif name.startswith("half"):
                    hf = int(name[4])
                    if hf == 0:
                        pe.wait_ge(dl["con"], 80)
                    multiply(pe, name, x_moving, None, (1, 3, 4), turn_pe(hf), turn_read(hf))
                elif name == "gates":
                    multiply(pe, name, x_moving)
                elif name == "attn_in":
                    multiply(pe, name, x_moving, ready_from(name), (1,), norm_turn_pe, norm_turn_read)
                elif name == "rnn_in":
                    multiply(pe, name, x_moving, ready_from(name), (1, 2, 3), rnn_pe, rnn_read)
                elif name == "mix0_in":
                    multiply(pe, name, x_moving, ready_from(name), range(1, 7), hgrn_in_pe, hgrn_in_read)
                else:
                    multiply(pe, name, x_moving, ready_from(name))
                if name in LNS:
                    pe_norm_sums(pe, LNS[name][0], z)
                    if name == "down1":
                        pe.wait_ge(var_ready, 5)
                        pe_square_sums(pe)
                elif name == "mix0_in":
                    hgrn_pe(pe)
                elif name == "attn_in":
                    attn_pe(pe)
                elif name.startswith("half"):
                    dil_pe(int(name[4]))(pe)
                elif name == "last_out":
                    pe_norm_sums(pe, 5, None)


def constants():
    out = np.zeros((P, NCON), np.float32)
    p, t = np.arange(P), np.arange(T)

    def put(name, a):
        a = np.asarray(a, np.float32).reshape(P, -1)
        out[:, CON0[name]:CON0[name] + a.shape[1]] = a

    put("ident", np.eye(P))
    put("seg_start", np.tile((t % SEG != 0), (P, 1)))
    same = p[:, None] // SEG == p[None, :] // SEG
    put("fw_mask", np.tile(same & (p[:, None] <= p[None, :]), (1, 4)))
    put("bw_mask", np.tile(same & (p[:, None] >= p[None, :]), (1, 4)))

    def rope(tag, partner, sign, ang, turned):
        perm = np.zeros((P, P))
        perm[partner[turned], p[turned]] = sign[turned]
        put(tag + "_perm", perm)
        put(tag + "_cos", np.where(turned[:, None], np.cos(ang), 1.0))
        put(tag + "_sin", np.where(turned[:, None], np.sin(ang), 0.0))

    half, n2 = P // 2, P // 4
    inv = np.exp(np.float32(-math.log(10000.0)) * np.arange(0, half, 2, dtype=np.float32) / half).astype(np.float32)
    pos = np.where((p < half)[:, None], (t // 64)[None, :], (t % 64)[None, :]).astype(np.float32)
    first = p % half < n2
    rope("rope1", np.where(first, p + n2, p - n2), np.where(first, -1.0, 1.0),
         pos * inv[p % n2][:, None], np.ones(P, bool))
    rot = P // 4
    inv = np.exp(np.float32(-math.log(500000.0)) * np.arange(rot // 2, dtype=np.float32) * np.float32(2.0 / rot))
    inv = inv.astype(np.float32)
    first = p < rot // 2
    rope("rope2", np.where(first, p + rot // 2, p - rot // 2), np.where(first, -1.0, 1.0),
         t[None, :].astype(np.float32) * inv[p % (rot // 2)][:, None], p < rot)

    def mask(queries, keys):
        gap = queries[:, None] - keys[None, :]
        return [np.where((gap >= 0) & (gap <= w) & (gap % dil == 0), 0.0, -1e30) for w, dil in WINDOWS]
    put("dil_mask0", np.concatenate(mask(p, p), 1))
    put("dil_mask1", np.concatenate(mask(p + P, t), 1))
    return out


def tasks(w, cols=None):
    k, n = w.shape
    a = w.reshape(k // (CK * P), CK, P, n // (CF * P), CF, P).transpose(3, 0, 2, 4, 1, 5)
    return a if cols is None else a[cols]


def kernel(**inputs):
    import concourse.bacc as bacc
    from concourse.bass_utils import run_bass_kernel_spmd

    a = {k: np.asarray(v) for k, v in inputs.items()}
    pairs = [i for g in range(FG) for i in (g, FG + g)]
    win2 = tasks(a["w_in_2"][0])

    def half(h):
        return [first + 2 * g + h for first in (8, 14, 20) for g in range(3)] + [26 + h]
    first = [2, 3, 4, 5, 12, 13, 6, 7, 10, 11, 0, 1, 8, 9]
    parts = [tasks(a["w_in_ab"][0], first), tasks(np.roll(a["w_out_ab"][0], -HT * P, 0)), tasks(a["ffn_up"][0], pairs), tasks(a["ffn_down"][0]),
             tasks(a["w_in_attn"][0]), tasks(a["w_out_attn"][0]), tasks(a["ffn_up"][1], pairs),
             tasks(a["ffn_down"][1]), win2[0:8], win2[half(0)], win2[half(1)], win2[28:36],
             tasks(a["w_attn_out_2"][0]), tasks(a["w_rnn_out_2"][0]), tasks(a["w_o_2"][0])]
    weights = np.concatenate([x.reshape(-1, P, CHUNK) for x in parts])
    assert weights.shape[0] == NCHUNKS

    def by_feature(x):
        return np.ascontiguousarray(x.reshape(T, MT, P).transpose(2, 1, 0))
    a["qk_norm_g"] = np.concatenate([a["q_norm_g"]] * 8 + [a["k_norm_g"]] * 2)
    par = np.concatenate([a[name].reshape(-1, P) for name, _ in PARS])
    assert par.shape[0] == NPAR
    arrays = {
        "x": by_feature(a["x"][0]),
        "weights": weights,
        "par": np.ascontiguousarray(par.T),
        "con": constants(),
        "gmlp_ws": np.ascontiguousarray(a["gmlp_ws"][0].transpose(2, 0, 1)),
        "gmlp_bias": np.ascontiguousarray(a["gmlp_bias"].reshape(1, HT * P)),
        "w_gates": np.ascontiguousarray(np.stack([a["w_rg_2"][0], a["w_ig_2"][0]]).transpose(2, 0, 1, 3)),
    }
    nc = bacc.Bacc("TRN2", target_bir_lowering=False, num_devices=1)
    d = {k: nc.dram_tensor(k + "_dram", v.shape, F32, kind="ExternalInput").ap() for k, v in arrays.items()}
    d["out"] = nc.dram_tensor("out_dram", (P, MT, T), F32, kind="ExternalOutput").ap()
    program(nc, d)
    r = run_bass_kernel_spmd(nc, [{k + "_dram": v for k, v in arrays.items()}], core_ids=[0])
    out = r.results[0]["out_dram"]
    return np.ascontiguousarray(out.transpose(2, 1, 0)).reshape(1, T, DM)
```
